# Optimizing a Trainium2 kernel written in Bass

```python
import math
import jax, jax.numpy as jnp
from jax import lax
import numpy as np

D_MODEL = 1024
BATCH = 1
SEQ = 256
DEPTH = 2
DEC_BATCH = 8
DEC_SEQ = 8
PAST_LEN = 2048
PAGE_SIZE = 128

N_EVEN = (DEPTH + 1) // 2
N_ODD = DEPTH // 2
NORM_EPS = 1e-6

MLA_HEADS = 8
MLA_NOPE = 64
MLA_ROPE = 32
MLA_V = 64
MLA_Q_RANK = 384
MLA_KV_RANK = 256
MLA_LAT = MLA_KV_RANK + MLA_ROPE
MLA_SCALE = (MLA_NOPE + MLA_ROPE) ** -0.5
ROPE_THETA = 10000.0
Q_BLOCK = 128

RWKV_HEADS = 8
RWKV_HEAD = 64
RWKV_DIM = RWKV_HEADS * RWKV_HEAD
RWKV_W_LORA = 64
RWKV_A_LORA = 64
RWKV_G_LORA = 128
RWKV_PROJ = 3 * RWKV_DIM + RWKV_W_LORA + RWKV_A_LORA + RWKV_G_LORA
RWKV_SPLITS = [RWKV_DIM, 2 * RWKV_DIM, 3 * RWKV_DIM, 3 * RWKV_DIM + RWKV_W_LORA, 3 * RWKV_DIM + RWKV_W_LORA + RWKV_A_LORA]
RWKV_LN_EPS = 64e-5

EVEN_IN = MLA_Q_RANK + MLA_LAT + RWKV_PROJ
EVEN_MIX = MLA_HEADS * MLA_V + RWKV_DIM

GLA_HEADS = 4
GLA_DK = 128
GLA_DV = 256
GLA_KDIM = GLA_HEADS * GLA_DK
GLA_VDIM = GLA_HEADS * GLA_DV
GLA_GATE_RANK = 16
GLA_GATE_NORM = 16.0
GLA_CHUNK = 64
GLA_SPLITS = [GLA_KDIM, 2 * GLA_KDIM, 2 * GLA_KDIM + GLA_VDIM, 2 * GLA_KDIM + 2 * GLA_VDIM]
ODD_IN = 2 * GLA_KDIM + 2 * GLA_VDIM + GLA_GATE_RANK

D_FF = 2816
N_EXPERTS = 8
TOP_K = 2
D_FF_EXPERT = 3584

kernel_name = 'mla_rwkv7_gla_moe_decode_step'

def rmsnorm(x, g, eps=NORM_EPS):
    xf = x.astype(jnp.float32)
    y = xf * lax.rsqrt(jnp.mean(xf * xf, axis=-1, keepdims=True) + eps)
    return (y * g.astype(jnp.float32)).astype(x.dtype)

def rope_angles(pos):
    inv = ROPE_THETA ** (-jnp.arange(0, MLA_ROPE, 2, dtype=jnp.float32) / MLA_ROPE)
    ang = pos.astype(jnp.float32)[:, None] * inv[None, :]
    return jnp.cos(ang), jnp.sin(ang)

def apply_rope(x, cos, sin):
    x1, x2 = jnp.split(x.astype(jnp.float32), 2, axis=-1)
    return jnp.concatenate([x1 * cos - x2 * sin, x1 * sin + x2 * cos], axis=-1).astype(x.dtype)

def swiglu(x, w_gu, w_down):
    gate, up = jnp.split(x @ w_gu, 2, axis=-1)
    return (jax.nn.silu(gate) * up) @ w_down

def mla_attend(q_lat, q_pe, q_pos, c_kv, k_pe, k_pos, w_uv):
    s = (jnp.einsum('bthc,bsc->bhts', q_lat, c_kv) + jnp.einsum('bthr,bsr->bhts', q_pe, k_pe)).astype(jnp.float32) * MLA_SCALE
    s = jnp.where(k_pos[None, :] <= q_pos[:, None], s, -jnp.inf)
    p = jax.nn.softmax(s, axis=-1).astype(c_kv.dtype)
    o_lat = jnp.einsum('bhts,bsc->bthc', p, c_kv)
    return jnp.einsum('bthc,chv->bthv', o_lat, w_uv)

def mla_prompt(q_lat, q_pe, c_kv, k_pe, w_uv):
    B, T, H, C = q_lat.shape
    nb = T // Q_BLOCK
    k_pos = jnp.arange(T)

    def blk(args):
        ql, qp, qpos = args
        return mla_attend(ql, qp, qpos, c_kv, k_pe, k_pos, w_uv)

    ql = q_lat.reshape(B, nb, Q_BLOCK, H, C).swapaxes(0, 1)
    qp = q_pe.reshape(B, nb, Q_BLOCK, H, MLA_ROPE).swapaxes(0, 1)
    qpos = jnp.arange(T).reshape(nb, Q_BLOCK)
    o = lax.map(blk, (ql, qp, qpos))
    return o.swapaxes(0, 1).reshape(B, T, H, MLA_V)

def rwkv7_scan(r, w, k, v, a, b, S0):
    xs = tuple(jnp.moveaxis(t.astype(jnp.float32), 1, 0) for t in (r, w, k, v, a, b))

    def step(S, inp):
        rt, wt, kt, vt, at, bt = inp
        sa = jnp.einsum('bhvk,bhk->bhv', S, at)
        S = S * wt[:, :, None, :] + sa[..., None] * bt[:, :, None, :] + vt[..., None] * kt[:, :, None, :]
        return S, jnp.einsum('bhvk,bhk->bhv', S, rt)

    S, y = lax.scan(step, S0.astype(jnp.float32), xs)
    return jnp.moveaxis(y, 0, 1).astype(r.dtype), S.astype(S0.dtype)

def gla_chunked(q, k, v, log_a, S0):
    B, T, H, DK = q.shape
    DV = v.shape[-1]
    C = min(GLA_CHUNK, T)
    n = -(-T // C)
    pad = n * C - T

    def blocks(t):
        t = jnp.pad(t.astype(jnp.float32), ((0, 0), (0, pad), (0, 0), (0, 0)))
        return jnp.transpose(t.reshape(B, n, C, H, t.shape[-1]), (1, 0, 3, 2, 4))

    causal = jnp.tril(jnp.ones((C, C), dtype=bool))

    def step(S, inp):
        qc, kc, vc, gc = inp
        b = jnp.cumsum(gc, axis=-2)
        inter = jnp.einsum('bhtd,bhdv->bhtv', qc * jnp.exp(b), S)
        diff = b[:, :, :, None, :] - b[:, :, None, :, :]
        decay = jnp.exp(jnp.where(causal[:, :, None], diff, -jnp.inf))
        A = jnp.einsum('bhtd,bhsd,bhtsd->bhts', qc, kc, decay)
        intra = jnp.einsum('bhts,bhsv->bhtv', A, vc)
        b_end = b[:, :, -1:, :]
        S = S * jnp.exp(b_end)[:, :, 0, :, None] + jnp.einsum('bhsd,bhsv->bhdv', kc * jnp.exp(b_end - b), vc)
        return S, inter + intra

    S, o = lax.scan(step, S0.astype(jnp.float32), (blocks(q), blocks(k), blocks(v), blocks(log_a)))
    o = jnp.transpose(o, (1, 0, 3, 2, 4)).reshape(B, n * C, H, DV)[:, :T]
    return o.astype(v.dtype), S.astype(S0.dtype)

def even_mixer(h, pos, S0, shift0, past_lat, p):
    B, T, _ = h.shape
    proj = h @ p['w_in']
    q_c, kv_c, rw = jnp.split(proj, [MLA_Q_RANK, MLA_Q_RANK + MLA_LAT], axis=-1)
    c_q = rmsnorm(q_c, p['q_norm'])
    q = (c_q @ p['w_uq']).reshape(B, T, MLA_HEADS, MLA_NOPE + MLA_ROPE)
    q_nope, q_pe = jnp.split(q, [MLA_NOPE], axis=-1)
    cos, sin = rope_angles(pos)
    q_pe = apply_rope(q_pe, cos[None, :, None, :], sin[None, :, None, :])
    c_kv = rmsnorm(kv_c[..., :MLA_KV_RANK], p['kv_norm'])
    k_pe = apply_rope(kv_c[..., MLA_KV_RANK:], cos[None], sin[None])
    new_lat = jnp.concatenate([c_kv, k_pe], axis=-1)
    q_lat = jnp.einsum('bthn,chn->bthc', q_nope, p['w_uk'])
    if past_lat is None:
        o_a = mla_prompt(q_lat, q_pe, c_kv, k_pe, p['w_uv'])
    else:
        lat = jnp.concatenate([past_lat.astype(new_lat.dtype), new_lat], axis=1)
        o_a = mla_attend(q_lat, q_pe, pos, lat[..., :MLA_KV_RANK], lat[..., MLA_KV_RANK:], jnp.arange(lat.shape[1]), p['w_uv'])
    prev = jnp.concatenate([shift0[:, None, :].astype(rw.dtype), rw[:, :-1]], axis=1)
    xs = rw + (prev - rw) * p['mu']
    r, k, v, xw, xa, xg = jnp.split(xs, RWKV_SPLITS, axis=-1)
    w_log = -jax.nn.softplus(-(p['w0'] + jnp.tanh(xw) @ p['w2']).astype(jnp.float32)) - 0.5
    decay = jnp.exp(-jnp.exp(w_log))
    a = jax.nn.sigmoid(p['a0'] + xa @ p['a2'])
    g = jax.nn.sigmoid(xg) @ p['g2']
    shp = (B, T, RWKV_HEADS, RWKV_HEAD)
    r, k, v, a, decay = r.reshape(shp), k.reshape(shp), v.reshape(shp), a.reshape(shp), decay.reshape(shp)
    kk = (k * p['k_k']).astype(jnp.float32)
    kk = (kk / jnp.maximum(jnp.sqrt(jnp.sum(kk * kk, axis=-1, keepdims=True)), 1e-12)).astype(k.dtype)
    k = k * (1 + (a - 1) * p['k_a'])
    y, S = rwkv7_scan(r, decay, k, v, -kk, kk * a, S0)
    yf = y.astype(jnp.float32)
    mean = jnp.mean(yf, axis=-1, keepdims=True)
    var = jnp.mean(jnp.square(yf - mean), axis=-1, keepdims=True)
    yn = ((yf - mean) * lax.rsqrt(var + RWKV_LN_EPS) * p['ln_g'] + p['ln_b']).astype(v.dtype)
    yn = yn + jnp.sum(r * k * p['r_k'], axis=-1, keepdims=True) * v
    o_b = yn.reshape(B, T, RWKV_DIM) * g
    mix = jnp.concatenate([o_a.reshape(B, T, MLA_HEADS * MLA_V), o_b], axis=-1) @ p['w_out']
    return mix, new_lat, S, rw[:, -1]

def odd_mixer(h, S0, p):
    B, T, _ = h.shape
    proj = h @ p['w_in']
    q, k, v, g, xa = jnp.split(proj, GLA_SPLITS, axis=-1)
    log_a = jax.nn.log_sigmoid((xa @ p['a2'] + p['ab']).astype(jnp.float32)) / GLA_GATE_NORM
    q = q.reshape(B, T, GLA_HEADS, GLA_DK) * (GLA_DK ** -0.5)
    k = k.reshape(B, T, GLA_HEADS, GLA_DK)
    v = v.reshape(B, T, GLA_HEADS, GLA_DV)
    log_a = log_a.reshape(B, T, GLA_HEADS, GLA_DK)
    o, S = gla_chunked(q, k, v, log_a, S0)
    o = rmsnorm(o, p['norm']).reshape(B, T, GLA_VDIM) * jax.nn.silu(g)
    return o @ p['w_out'], S

def moe_ffn(h, router, w_gu, w_down):
    B, T, D = h.shape
    xf = h.reshape(-1, D)
    logits = (xf @ router).astype(jnp.float32)
    top_v, top_i = lax.top_k(logits, TOP_K)
    gates = jax.nn.softmax(top_v, axis=-1)
    comb = jnp.einsum('nk,nke->ne', gates, jax.nn.one_hot(top_i, N_EXPERTS, dtype=jnp.float32)).astype(h.dtype)
    out = jnp.zeros_like(xf)
    for e in range(N_EXPERTS):
        out = out + comb[:, e:e + 1] * swiglu(xf, w_gu[e], w_down[e])
    return out.reshape(B, T, D)

def even_layer(x, pos, S0, shift0, past_lat, p):
    mix, lat, S, sh = even_mixer(rmsnorm(x, p['norm_mix']), pos, S0, shift0, past_lat, p)
    x = x + mix
    x = x + swiglu(rmsnorm(x, p['norm_ffn']), p['ffn_gu'], p['ffn_down'])
    return x, lat, S, sh

def odd_layer(x, S0, p):
    mix, S = odd_mixer(rmsnorm(x, p['norm_mix']), S0, p)
    x = x + mix
    x = x + moe_ffn(rmsnorm(x, p['norm_ffn']), p['router'], p['moe_gu'], p['moe_down'])
    return x, S

def setup_inputs(seed: int = 0) -> dict:
    key = jax.random.key(seed)
    ks = iter(jax.random.split(key, 48))
    f32 = jnp.float32

    def nrm(shape, scale):
        return scale * jax.random.normal(next(ks), shape, f32)

    def gain(shape):
        return 1.0 + 0.05 * jax.random.normal(next(ks), shape, f32)

    def unif(shape, lo, hi):
        return jax.random.uniform(next(ks), shape, f32, lo, hi)

    n_pages = PAST_LEN // PAGE_SIZE
    n_used = DEC_BATCH * n_pages
    n_pool = n_used + n_used // 4
    perm = jax.random.permutation(next(ks), n_pool)
    page_table = perm[:n_used].reshape(DEC_BATCH, n_pages).astype(jnp.int32)
    D = D_MODEL
    return {
        'x_prompt': nrm((BATCH, SEQ, D), 1.0),
        'x_sample': nrm((DEC_BATCH, DEC_SEQ, D), 1.0),
        'cache_mla': nrm((N_EVEN, n_pool, PAGE_SIZE, MLA_LAT), 1.0),
        'state_rwkv': nrm((N_EVEN, DEC_BATCH, RWKV_HEADS, RWKV_HEAD, RWKV_HEAD), 0.1),
        'state_rwkv_shift': nrm((N_EVEN, DEC_BATCH, RWKV_PROJ), 1.0),
        'state_gla': nrm((N_ODD, DEC_BATCH, GLA_HEADS, GLA_DK, GLA_DV), 0.1),
        'page_table': page_table,
        'norm_mix_even': gain((N_EVEN, D)),
        'norm_ffn_even': gain((N_EVEN, D)),
        'w_in_even': nrm((N_EVEN, D, EVEN_IN), D ** -0.5),
        'mla_q_norm': gain((N_EVEN, MLA_Q_RANK)),
        'mla_kv_norm': gain((N_EVEN, MLA_KV_RANK)),
        'mla_w_uq': nrm((N_EVEN, MLA_Q_RANK, MLA_HEADS * (MLA_NOPE + MLA_ROPE)), MLA_Q_RANK ** -0.5),
        'mla_w_uk': nrm((N_EVEN, MLA_KV_RANK, MLA_HEADS, MLA_NOPE), MLA_KV_RANK ** -0.5),
        'mla_w_uv': nrm((N_EVEN, MLA_KV_RANK, MLA_HEADS, MLA_V), MLA_KV_RANK ** -0.5),
        'rwkv_mu': unif((N_EVEN, RWKV_PROJ), 0.0, 1.0),
        'rwkv_w0': unif((N_EVEN, RWKV_DIM), -2.5, 0.5),
        'rwkv_w2': nrm((N_EVEN, RWKV_W_LORA, RWKV_DIM), 0.1),
        'rwkv_a0': nrm((N_EVEN, RWKV_DIM), 0.5),
        'rwkv_a2': nrm((N_EVEN, RWKV_A_LORA, RWKV_DIM), 0.5 * RWKV_A_LORA ** -0.5),
        'rwkv_g2': nrm((N_EVEN, RWKV_G_LORA, RWKV_DIM), RWKV_G_LORA ** -0.5),
        'rwkv_k_k': gain((N_EVEN, RWKV_HEADS, RWKV_HEAD)),
        'rwkv_k_a': gain((N_EVEN, RWKV_HEADS, RWKV_HEAD)),
        'rwkv_r_k': nrm((N_EVEN, RWKV_HEADS, RWKV_HEAD), 0.1),
        'rwkv_ln_g': gain((N_EVEN, RWKV_HEADS, RWKV_HEAD)),
        'rwkv_ln_b': nrm((N_EVEN, RWKV_HEADS, RWKV_HEAD), 0.02),
        'w_out_even': nrm((N_EVEN, EVEN_MIX, D), EVEN_MIX ** -0.5),
        'ffn_w_gu_even': nrm((N_EVEN, D, 2 * D_FF), D ** -0.5),
        'ffn_w_down_even': nrm((N_EVEN, D_FF, D), D_FF ** -0.5),
        'norm_mix_odd': gain((N_ODD, D)),
        'norm_ffn_odd': gain((N_ODD, D)),
        'w_in_odd': nrm((N_ODD, D, ODD_IN), D ** -0.5),
        'gla_a2': nrm((N_ODD, GLA_GATE_RANK, GLA_KDIM), GLA_GATE_RANK ** -0.5),
        'gla_ab': nrm((N_ODD, GLA_KDIM), 0.5),
        'gla_norm': gain((N_ODD, GLA_HEADS, GLA_DV)),
        'w_out_odd': nrm((N_ODD, GLA_VDIM, D), GLA_VDIM ** -0.5),
        'moe_router': nrm((N_ODD, D, N_EXPERTS), D ** -0.5),
        'moe_w_gu': nrm((N_ODD, N_EXPERTS, D, 2 * D_FF_EXPERT), D ** -0.5),
        'moe_w_down': nrm((N_ODD, N_EXPERTS, D_FF_EXPERT, D), D_FF_EXPERT ** -0.5),
        'final_norm': gain((D,)),
    }

def reference(x_prompt, x_sample, cache_mla, state_rwkv, state_rwkv_shift, state_gla, page_table,
              norm_mix_even, norm_ffn_even, w_in_even, mla_q_norm, mla_kv_norm, mla_w_uq, mla_w_uk, mla_w_uv,
              rwkv_mu, rwkv_w0, rwkv_w2, rwkv_a0, rwkv_a2, rwkv_g2, rwkv_k_k, rwkv_k_a, rwkv_r_k, rwkv_ln_g, rwkv_ln_b,
              w_out_even, ffn_w_gu_even, ffn_w_down_even,
              norm_mix_odd, norm_ffn_odd, w_in_odd, gla_a2, gla_ab, gla_norm, w_out_odd,
              moe_router, moe_w_gu, moe_w_down, final_norm):
    bp, tp, _ = x_prompt.shape
    pos_p = jnp.arange(tp)
    pos_s = PAST_LEN + jnp.arange(x_sample.shape[1])
    db, n_pages = page_table.shape
    hp, hs = x_prompt, x_sample
    lat_p, lat_s, rs_p, rs_s, sh_p, sh_s, gs_p, gs_s = [], [], [], [], [], [], [], []
    for layer in range(DEPTH):
        i = layer // 2
        if layer % 2 == 0:
            p = dict(norm_mix=norm_mix_even[i], norm_ffn=norm_ffn_even[i], w_in=w_in_even[i],
                     q_norm=mla_q_norm[i], kv_norm=mla_kv_norm[i], w_uq=mla_w_uq[i], w_uk=mla_w_uk[i], w_uv=mla_w_uv[i],
                     mu=rwkv_mu[i], w0=rwkv_w0[i], w2=rwkv_w2[i], a0=rwkv_a0[i], a2=rwkv_a2[i], g2=rwkv_g2[i],
                     k_k=rwkv_k_k[i], k_a=rwkv_k_a[i], r_k=rwkv_r_k[i], ln_g=rwkv_ln_g[i], ln_b=rwkv_ln_b[i],
                     w_out=w_out_even[i], ffn_gu=ffn_w_gu_even[i], ffn_down=ffn_w_down_even[i])
            S0_p = jnp.zeros((bp, RWKV_HEADS, RWKV_HEAD, RWKV_HEAD), x_prompt.dtype)
            shift0_p = jnp.zeros((bp, RWKV_PROJ), x_prompt.dtype)
            hp, lp, sp, shp = even_layer(hp, pos_p, S0_p, shift0_p, None, p)
            past = cache_mla[i][page_table].reshape(db, n_pages * PAGE_SIZE, MLA_LAT)
            hs, ls, ss, shs = even_layer(hs, pos_s, state_rwkv[i], state_rwkv_shift[i], past, p)
            lat_p.append(lp); lat_s.append(ls); rs_p.append(sp); rs_s.append(ss); sh_p.append(shp); sh_s.append(shs)
        else:
            p = dict(norm_mix=norm_mix_odd[i], norm_ffn=norm_ffn_odd[i], w_in=w_in_odd[i], a2=gla_a2[i], ab=gla_ab[i],
                     norm=gla_norm[i], w_out=w_out_odd[i], router=moe_router[i], moe_gu=moe_w_gu[i], moe_down=moe_w_down[i])
            G0_p = jnp.zeros((bp, GLA_HEADS, GLA_DK, GLA_DV), x_prompt.dtype)
            hp, gp = odd_layer(hp, G0_p, p)
            hs, gsa = odd_layer(hs, state_gla[i], p)
            gs_p.append(gp); gs_s.append(gsa)
    y_prompt = rmsnorm(hp, final_norm)
    y_sample = rmsnorm(hs, final_norm)
    new_mla_prompt = jnp.stack(lat_p)
    new_mla_sample = jnp.stack(lat_s)
    new_rwkv_prompt = jnp.stack(rs_p)
    new_rwkv_sample = jnp.stack(rs_s)
    new_shift_prompt = jnp.stack(sh_p)
    new_shift_sample = jnp.stack(sh_s)
    new_gla_prompt = jnp.stack(gs_p)
    new_gla_sample = jnp.stack(gs_s)
    return (y_prompt, y_sample, new_mla_prompt, new_mla_sample, new_rwkv_prompt, new_rwkv_sample,
            new_shift_prompt, new_shift_sample, new_gla_prompt, new_gla_sample)


_drawn_inputs = setup_inputs


def setup_inputs(seed=0):
    import zlib

    import numpy as np

    out = dict(_drawn_inputs(seed))
    spreads = {}
    factors = {}
    for name, (base, spread) in spreads.items():
        noise = np.random.default_rng([zlib.crc32(name.encode()), seed]).standard_normal(out[name].shape)
        drawn = base * np.exp(spread * noise) if base else spread * noise
        out[name] = __import__('jax').numpy.asarray(drawn.astype(out[name].dtype))
    for name, factor in factors.items():
        out[name] = (out[name] * factor).astype(out[name].dtype)
    return out
```

```python
from contextlib import ExitStack

import numpy as np

import concourse.bass as bass
from concourse import mybir

F32 = mybir.dt.float32
I32 = mybir.dt.int32
ALU = mybir.AluOpType
ACT = mybir.ActivationFunctionType
AX_X = mybir.AxisListType.X

P = 128
D = 1024
DC = D // P
SEQ, NB, DS = 256, 8, 8
TOK = SEQ + NB * DS
TILES = [(0, P), (P, P), (2 * P, NB * DS)]
PAST, PAGE = 2048, 128
NPAGE = PAST // PAGE
H = 8
NOPE, ROPE, VD = 64, 32, 64
QR, KVR = 384, 256
LAT = KVR + ROPE
SCALE = float((NOPE + ROPE) ** -0.5)
RH, RD = 8, 64
RDIM = RH * RD
RPROJ = 3 * RDIM + 64 + 64 + 128
RT = RPROJ // P
EVEN_IN = QR + LAT + RPROJ
GH, DK, DV = 4, 128, 256
GRANK = 16
GK, GV = GH * DK, GH * DV
ODD_IN = 2 * GK + 2 * GV + GRANK
DFF, DFE = 2816, 3584
NE = 8
RC, GC = 64, 32
EPS = 1e-6
LN_EPS = 64e-5
HALF_E = float(np.exp(np.float32(-0.5)))
FAR = 1.0e4
MAXJOB = 16

VEC = {}
_at = 0
for _name, _n in [("norm_mix_even", 8), ("norm_ffn_even", 8), ("mla_q_norm", 3), ("mla_kv_norm", 2),
                  ("rwkv_mu", RT), ("rwkv_w0", 4), ("rwkv_a0", 4), ("rwkv_k_k", 4), ("rwkv_k_a", 4),
                  ("rwkv_r_k", 4), ("rwkv_ln_g", 4), ("rwkv_ln_b", 4), ("norm_mix_odd", 8),
                  ("norm_ffn_odd", 8), ("gla_ab", 4), ("gla_norm", 8), ("final_norm", 8)]:
    VEC[_name] = (_at, _n)
    _at += _n
NVEC = _at


def constants():
    p = np.arange(P)
    i, j = p[:, None], p[None, :]
    f = {}
    f["ident"] = (i == j)
    f["ones"] = np.ones((P, P))
    f["head_ones"] = (i // 64 == j // 64)
    f["rw_T"] = np.concatenate([(i // RC == j // RC) & (i < j), (i // RC == j // RC) & (i <= j)], 1)
    s8T = np.zeros((P, 2 * P))
    s8T[:64, 0:64] = ((i // DS == j // DS) & (i < j))[:64, :64]
    s8T[:64, P:P + 64] = ((i // DS == j // DS) & (i <= j))[:64, :64]
    f["sm_T"] = s8T
    for s in (1, 2, 4, 8, 16, 32):
        low = (i // (2 * s) == j // (2 * s)) & (i % (2 * s) >= s) & (j % (2 * s) < s)
        f[f"lev{s}"] = low
        if s == 1:
            f["lev1_T"] = low.T
    f["causal"] = np.where(i <= j, 0.0, -1e30)
    f["own"] = np.where((i % DS >= np.arange(DS)[None, :]), 0.0, -1e30)
    f["gla_T"] = (i // GC == j // GC) & (i <= j)
    pos = np.arange(TOK)
    for name, c in (("reset_rw", RC), ("reset_gla", GC)):
        start = np.where(pos < SEQ, pos % c == 0, (pos - SEQ) % DS == 0)
        f[name] = np.broadcast_to(np.where(start, 0.0, 1.0)[None], (P, TOK))
    place = np.where(pos < SEQ, pos, PAST + (pos - SEQ) % DS).astype(np.float32)
    inv = (np.float32(10000.0) ** (-np.arange(0, ROPE, 2, dtype=np.float32) / np.float32(ROPE))).astype(np.float32)
    ang = (place[None, :] * inv[:, None]).astype(np.float32)
    for name, t in (("cos", np.cos(ang)), ("sin", np.sin(ang))):
        full = np.zeros((P, TOK), np.float32)
        full[:32] = np.concatenate([t, t], 0)
        f[name] = full
    rot = np.zeros((P, ROPE))
    for a in range(16):
        rot[a + 16, a] = -1.0
        rot[a, a + 16] = 1.0
    f["rot"] = rot
    bsel = np.zeros((P, NB))
    bsel[:64] = (i[:64] // DS == np.arange(NB)[None, :])
    f["bsel"] = bsel
    f["before"] = (i < j)
    f["slots"] = np.broadcast_to(j, (P, P))
    e = np.arange(NE)
    f["tie"] = np.broadcast_to((e[None, :] < e[:, None]).reshape(1, 64), (P, 64))
    c = np.arange(16)
    f["part"] = np.broadcast_to((128.0 * (1 + c // 8))[None], (P, 16))
    f["expert"] = np.broadcast_to((c % 8)[None], (P, 16))
    f["jobno"] = np.broadcast_to(np.repeat(np.arange(8), 16)[None], (P, 128))
    cols, at, parts = {}, 0, []
    for k, a in f.items():
        a = np.ascontiguousarray(a, dtype=np.float32)
        cols[k] = (at, a.shape[1])
        at += a.shape[1]
        parts.append(a)
    return cols, np.concatenate(parts, 1)


class Signal:
    def __init__(self, sem):
        self.sem, self.n = sem, 0


def done(eng, ins, sig):
    ins.then_inc(sig.sem, 1)
    sig.n += 1
    eng.wait_ge(sig.sem, sig.n)
    return sig.n


def model(nc, A, O):
    ctx = ExitStack()
    names = [0]

    layer_sems = []

    def sem(name):
        names[0] += 1
        layer_sems.append(nc.alloc_semaphore(f"{name}_{names[0]}"))
        return layer_sems[-1]

    def next_part():
        nc.all_engine_barrier()
        nc.clear_and_free_semaphores(layer_sems)
        layer_sems.clear()
        nc.all_engine_barrier()

    def sbuf(scope, name, shape, dt=F32):
        names[0] += 1
        return scope.enter_context(nc.sbuf_tensor(f"{name}_{names[0]}", shape, dt))

    with ctx:
        CC, _ = constants()
        consts = sbuf(ctx, "consts", [P, sum(n for _, n in CC.values())])

        def C(name, rows=P, lo=0, hi=None):
            at, n = CC[name]
            return consts[0:rows, at + lo:at + (n if hi is None else hi)]

        vecs = sbuf(ctx, "vecs", [P, NVEC])

        def V(name, k=0, n=1):
            return vecs[:, VEC[name][0] + k:VEC[name][0] + k + n]

        xT = sbuf(ctx, "xT", [P, DC, TOK])
        hT = sbuf(ctx, "hT", [P, DC, TOK])
        mixT = sbuf(ctx, "mixT", [P, DC, TOK])
        rstd = sbuf(ctx, "rstd", [P, TOK])
        ps = [ctx.enter_context(nc.psum_tensor(f"bank{b}", [P, 512], F32)) for b in range(8)]
        dve_order, act_order, pool_order, stored = (Signal(ctx.enter_context(nc.semaphore(x))) for x in (
            "dve_order", "act_order", "pool_order", "stored"))

        def dv(v, ins):
            done(v, ins, dve_order)

        def ac(s, ins):
            done(s, ins, act_order)

        def po(g, ins):
            done(g, ins, pool_order)

        def store(eng, dst, src):
            eng.dma_start(dst, src).then_inc(stored.sem, 16)
            stored.n += 16

        def load(eng, dst, src, sig):
            eng.dma_start(dst, src).then_inc(sig.sem, 16)
            sig.n += 16

        class Linear:
            def __init__(self, name, tiles, banks):
                self.full, self.act, self.dve = sem(name + "_full"), sem(name + "_act"), sem(name + "_dve")
                self.tiles, self.banks = tiles, banks
                assert len(banks) % 2 == 0

            def pe(self, pe, weights, chunks, rhs, ready=None, rows=None):
                nb = len(self.banks)
                for t in range(self.tiles):
                    if ready:
                        ready(t)
                    if t >= nb:
                        pe.wait_ge(self.act if t % 2 == 0 else self.dve, (t - nb) // 2 + 1)
                    for k in range(chunks):
                        w = weights(t, k)
                        n = w.shape[1] if len(w.shape) == 2 else w.shape[1] * w.shape[2]
                        mm = pe.matmul(ps[self.banks[t % nb]][0:n, 0:TOK], w, rhs(k), start=(k == 0), stop=(k == chunks - 1))
                    mm.then_inc(self.full, 1)

            def out(self, t, rows=P):
                return ps[self.banks[t % len(self.banks)]][0:rows, 0:TOK]

            def run_act(self, s, body):
                for t in range(0, self.tiles, 2):
                    s.wait_ge(self.full, t + 1)
                    body(t).then_inc(self.act, 1)

            def run_dve(self, v, body):
                for t in range(1, self.tiles, 2):
                    v.wait_ge(self.full, t + 1)
                    body(t).then_inc(self.dve, 1)

        def rms_steps(name, src, chunks, gain, dst, width, eps=EPS, bank=7, scratch=None):
            sq_ready, sum_ready, var_ready, rstd_ready = (sem(f"{name}_{x}") for x in ("sq", "sum", "var", "rstd"))

            def dve(v):
                dv(v, v.tensor_tensor(scratch[:, 0:chunks, :], src, src, ALU.mult))
                v.sem_inc(sq_ready, 1)
                v.wait_ge(sum_ready, 1)
                v.tensor_scalar(rstd[:, :], ps[bank][:, 0:TOK], 1.0 / width, eps, ALU.mult, ALU.add).then_inc(var_ready, 1)
                v.wait_ge(rstd_ready, 1)
                dv(v, v.reciprocal(rstd[:, :], rstd[:, :]))
                for k in range(chunks):
                    last = v.scalar_tensor_tensor(out=dst[:, k, :], in0=src[:, k, :], scalar=gain[:, k:k + 1],
                                                  in1=rstd[:, :], op0=ALU.mult, op1=ALU.mult)
                dv(v, last)

            def pe(t):
                t.wait_ge(sq_ready, 1)
                for k in range(chunks):
                    mm = t.matmul(ps[bank][:, 0:TOK], C("ones"), scratch[:, k, :], start=(k == 0), stop=(k == chunks - 1))
                mm.then_inc(sum_ready, 1)

            def act(s):
                s.wait_ge(var_ready, 1)
                s.activation(rstd[:, :], rstd[:, :], ACT.Sqrt).then_inc(rstd_ready, 1)

            return dve, pe, act

        with ExitStack() as st:
            xtok = sbuf(st, "xtok", [P, 3, D])
            vrow = sbuf(st, "vrow", [P, P])
            consts_in, rows_in, x_in = Signal(sem("consts_in")), Signal(sem("rows_in")), Signal(sem("x_in"))
            turned, x_act, x_dve, vec_full = sem("turned"), sem("x_act"), sem("x_dve"), sem("vec_full")
            with nc.Block() as block:
                @block.sync
                def _(sp):
                    load(sp, consts[:, :], A["consts"], consts_in)
                    load(sp, xtok[:, 0:2, :], A["x_prompt"][0].rearrange("(t p) d -> p t d", p=P), x_in)
                    load(sp, xtok[0:64, 2, :], A["x_sample"].rearrange("b t d -> (b t) d"), x_in)

                @block.scalar
                def _(s):
                    for k, (at, n) in VEC.items():
                        a = A[k]
                        flat = {1: "a -> a", 2: "a b -> (a b)", 3: "a b c -> (a b c)"}[len(a.shape)]
                        a = a.rearrange(flat) if len(a.shape) > 1 else a
                        load(s, vrow[at:at + n, :], a.rearrange("(c p) -> c p", p=P), rows_in)
                    for g in range(0, 6, 2):
                        s.wait_ge(turned, g + 1)
                        t, half = g // 2, g % 2
                        r = TILES[t][1]
                        s.activation(xT[:, 4 * half:4 * half + 4, TILES[t][0]:TILES[t][0] + r],
                                     ps[g % 4][:, :].rearrange("p (c t) -> p c t", c=4)[:, :, 0:r], ACT.Copy).then_inc(x_act, 1)

                @block.tensor
                def _(t):
                    t.wait_ge(consts_in.sem, 16)
                    t.wait_ge(x_in.sem, 32)
                    for g in range(6):
                        if g >= 4:
                            t.wait_ge(x_act if g % 2 == 0 else x_dve, 1)
                        i, half = g // 2, g % 2
                        r = TILES[i][1]
                        for c in range(4):
                            mm = t.transpose(ps[g % 4][:, c * P:c * P + r], xtok[0:r, i, (4 * half + c) * P:(4 * half + c + 1) * P],
                                             C("ident", r, 0, r))
                        mm.then_inc(turned, 1)
                    t.wait_ge(rows_in.sem, 16 * len(VEC))
                    t.transpose(ps[4][:, 0:NVEC], vrow[0:NVEC, :], C("ident", NVEC, 0, NVEC)).then_inc(vec_full, 1)

                @block.vector
                def _(v):
                    for g in range(1, 6, 2):
                        v.wait_ge(turned, g + 1)
                        t, half = g // 2, g % 2
                        r = TILES[t][1]
                        v.tensor_copy(xT[:, 4 * half:4 * half + 4, TILES[t][0]:TILES[t][0] + r],
                                      ps[g % 4][:, :].rearrange("p (c t) -> p c t", c=4)[:, :, 0:r]).then_inc(x_dve, 1)
                    v.wait_ge(vec_full, 1)
                    dv(v, v.tensor_copy(vecs[:, :], ps[4][:, 0:NVEC]))

        with ExitStack() as ev:
            kvT = sbuf(ev, "kvT", [P, 2, TOK])
            kpe = sbuf(ev, "kpe", [ROPE, TOK])
            qcT = sbuf(ev, "qcT", [P, 3, TOK])
            rwT = sbuf(ev, "rwT", [P, RT, TOK])
            with ExitStack() as st:
                win = sbuf(st, "win", [P, DC, EVEN_IN])
                sq = sbuf(st, "sq", [P, DC, TOK])
                cuts = [0, QR + LAT, QR + LAT + 512, QR + LAT + 1024, EVEN_IN]
                win_in = [sem("win_in") for _ in range(4)]
                n_dve, n_pe, n_act = rms_steps("mixn", xT[:, :, :], DC, V("norm_mix_even", 0, 8), hT, D, scratch=sq)
                cols = [(k * P, P) for k in range(5)] + [(5 * P, ROPE)] + [(QR + LAT + k * P, P) for k in range(RT)]
                dest = [qcT[:, k, :] for k in range(3)] + [kvT[:, k, :] for k in range(2)] + [kpe[:, :]] + [rwT[:, k, :] for k in range(RT)]
                lin = Linear("proj", 20, [0, 1, 2, 3, 4, 5])
                h_ready = sem("h_ready")
                with nc.Block() as block:
                    @block.sync
                    def _(sp):
                        w = A["w_in_even"][0].rearrange("(c p) n -> p c n", p=P)
                        for g in range(4):
                            sp.dma_start(win[:, :, cuts[g]:cuts[g + 1]], w[:, :, cuts[g]:cuts[g + 1]]).then_inc(win_in[g], 16)

                    @block.vector
                    def _(v):
                        n_dve(v)
                        v.sem_inc(h_ready, 1)
                        lin.run_dve(v, lambda t: v.tensor_copy(dest[t], lin.out(t, cols[t][1])))

                    @block.scalar
                    def _(s):
                        n_act(s)
                        lin.run_act(s, lambda t: s.activation(dest[t], lin.out(t, cols[t][1]), ACT.Copy))


                    @block.tensor
                    def _(t):
                        n_pe(t)
                        t.wait_ge(h_ready, 1)

                        def landed(i):
                            for g in range(4):
                                if cols[i][0] == (cuts[g] if g else 0):
                                    t.wait_ge(win_in[g], 16)
                        lin.pe(t, lambda i, k: win[:, k, cols[i][0]:cols[i][0] + cols[i][1]], DC, lambda k: hT[:, k, :], landed)

            with ExitStack() as ml:
                latT = sbuf(ml, "latT", [P, 2, TOK])
                kroT = sbuf(ml, "kroT", [ROPE, TOK])
                latK = sbuf(ml, "latK", [P, 3, LAT])
                qlT = sbuf(ml, "qlT", [P, 2, H, TOK])
                qpT = sbuf(ml, "qpT", [ROPE, H, TOK])
                uv = sbuf(ml, "uv", [P, 2, H * VD])
                uv_in = Signal(sem("uv_in"))
                with ExitStack() as st:
                    cqT = sbuf(st, "cqT", [P, 3, TOK])
                    sq = sbuf(st, "sq", [P, 3, TOK])
                    uqn = sbuf(st, "uqn", [P, 3, H * NOPE])
                    uqp = sbuf(st, "uqp", [P, 3, H * ROPE])
                    small_in = Signal(sem("small_in"))
                    uk = sbuf(st, "uk", [P, 2, H * NOPE])
                    ukT = sbuf(st, "ukT", [P, 4, KVR])
                    qnT = sbuf(st, "qnT", [P, 4, TOK])
                    qpe = sbuf(st, "qpe", [ROPE, H, TOK])
                    qsw = sbuf(st, "qsw", [ROPE, H, TOK])
                    ksw = sbuf(st, "ksw", [ROPE, TOK])
                    a_dve, a_pe, a_act = rms_steps("qn", qcT[:, :, :], 3, V("mla_q_norm", 0, 3), cqT, QR, bank=7, scratch=sq)
                    b_dve, b_pe, b_act = rms_steps("kvn", kvT[:, :, :], 2, V("mla_kv_norm", 0, 2), latT, KVR, bank=6, scratch=sq)
                    uk_in, ukt_full, ukt_ready = Signal(sem("uk_in")), sem("ukt_full"), sem("ukt_ready")
                    cq_ready, rot_full, rot_free, kro_full, kro_ready, lk_full, lk_ready = (
                        sem(x) for x in ("cq_ready", "rot_full", "rot_free", "kro_full", "kro_ready", "lk_full", "lk_ready"))
                    qlin, qlin_out = Linear("q", 12, [0, 1, 2, 3]), None
                    klin = Linear("ql", 2 * H, [0, 1, 2, 3])
                    qdest = [qnT[:, k, :] for k in range(4)] + [qpe[:, h, :] for h in range(H)]
                    with nc.Block() as block:
                        @block.sync
                        def _(sp):
                            load(sp, uk[:, :, :], A["mla_w_uk"][0].rearrange("(c p) h n -> p c (h n)", p=P), uk_in)
                            for c in range(3):
                                w = A["mla_w_uq"][0, c * P:(c + 1) * P, :].rearrange("p (h n) -> p h n", h=H)
                                load(sp, uqn[:, c, :].rearrange("p (h n) -> p h n", h=H), w[:, :, 0:NOPE], small_in)
                                load(sp, uqp[:, c, :].rearrange("p (h n) -> p h n", h=H), w[:, :, NOPE:NOPE + ROPE], small_in)
                            load(sp, uv[:, :, :], A["mla_w_uv"][0].rearrange("(c p) h n -> p c (h n)", p=P), uv_in)
                            sp.wait_ge(lk_ready, 3)
                            store(sp, O["new_mla_prompt"][0, 0].rearrange("(t p) c -> p t c", p=P), latK[:, 0:2, :])
                            store(sp, O["new_mla_sample"][0].rearrange("b t c -> (b t) c"), latK[0:64, 2, :])
                            sp.wait_ge(stored.sem, stored.n)

                        @block.gpsimd
                        def _(g):
                            g.wait_ge(qlin.act, 6)
                            g.wait_ge(qlin.dve, 6)
                            for h in range(H):
                                last = g.tensor_tensor(qpT[:, h, :], qpe[:, h, :], C("cos", ROPE), ALU.mult)
                            po(g, last)
                            g.wait_ge(rot_free, H + 1)
                            po(g, g.tensor_tensor(qpT[:, :, :], qpT[:, :, :], qsw[:, :, :], ALU.add))

                        @block.vector
                        def _(v):
                            a_dve(v)
                            v.sem_inc(cq_ready, 1)
                            b_dve(v)
                            v.sem_inc(cq_ready, 1)
                            v.wait_ge(ukt_full, 1)
                            for g in range(2):
                                last = v.tensor_copy(ukT[:, 2 * g:2 * g + 2, :], ps[4 + g][:, :].rearrange("p (a c) -> p a c", a=2))
                            dv(v, last)
                            v.sem_inc(ukt_ready, 1)
                            qlin.run_dve(v, lambda t: v.tensor_copy(qdest[t], qlin.out(t, P if t < 4 else ROPE)))
                            for h in range(H + 1):
                                v.wait_ge(rot_full, h + 1)
                                dst = ksw[:, :] if h == H else qsw[:, h, :]
                                v.tensor_tensor(dst, ps[4 + h % 2][0:ROPE, 0:TOK], C("sin", ROPE), ALU.mult).then_inc(rot_free, 1)
                            dv(v, v.tensor_tensor(kroT[:, :], kpe[:, :], C("cos", ROPE), ALU.mult))
                            v.wait_ge(rot_free, H + 1)
                            dv(v, v.tensor_tensor(kroT[:, :], kroT[:, :], ksw[:, :], ALU.add))
                            v.sem_inc(kro_ready, 1)
                            klin.run_dve(v, lambda t: v.tensor_copy(qlT[:, t % 2, t // 2, :], klin.out(t)))

                        @block.scalar
                        def _(s):
                            a_act(s)
                            b_act(s)
                            qlin.run_act(s, lambda t: s.activation(qdest[t], qlin.out(t, P if t < 4 else ROPE), ACT.Copy))
                            klin.run_act(s, lambda t: s.activation(qlT[:, t % 2, t // 2, :], klin.out(t), ACT.Copy))
                            for i, (lo, r) in enumerate(TILES):
                                s.wait_ge(lk_full, i + 1)
                                s.activation(latK[0:r, i, :], ps[4 + i][0:r, 0:LAT], ACT.Copy).then_inc(lk_ready, 1)

                        @block.tensor
                        def _(t):
                            a_pe(t)
                            t.wait_ge(uk_in.sem, 16)
                            for pr in range(4):
                                for c in range(2):
                                    mm = t.transpose(ps[4 + pr // 2][:, (pr % 2) * KVR + c * P:(pr % 2) * KVR + (c + 1) * P],
                                                     uk[:, c, pr * P:(pr + 1) * P], C("ident"))
                            mm.then_inc(ukt_full, 1)
                            t.wait_ge(cq_ready, 1)
                            b_pe(t)
                            t.wait_ge(small_in.sem, 96)

                            def wq(i, k):
                                return uqn[:, k, i * P:(i + 1) * P] if i < 4 else uqp[:, k, (i - 4) * ROPE:(i - 3) * ROPE]
                            qlin.pe(t, wq, 3, lambda k: cqT[:, k, :])
                            t.wait_ge(qlin.act, 6)
                            t.wait_ge(qlin.dve, 6)
                            t.wait_ge(ukt_ready, 1)
                            for h in range(H + 1):
                                if h >= 2:
                                    t.wait_ge(rot_free, h - 1)
                                t.matmul(ps[4 + h % 2][0:ROPE, 0:TOK], C("rot", ROPE), kpe[:, :] if h == H else qpe[:, h, :],
                                         start=True, stop=True).then_inc(rot_full, 1)
                            def wk(i, k):
                                h, c = i // 2, i % 2
                                return ukT[(h % 2) * 64:(h % 2) * 64 + 64, h // 2, c * P:(c + 1) * P]
                            nb = 4
                            for i in range(2 * H):
                                h = i // 2
                                if i >= nb:
                                    t.wait_ge(klin.act if i % 2 == 0 else klin.dve, (i - nb) // 2 + 1)
                                t.matmul(ps[klin.banks[i % nb]][:, 0:TOK], wk(i, 0), qnT[(h % 2) * 64:(h % 2) * 64 + 64, h // 2, :],
                                         start=True, stop=True).then_inc(klin.full, 1)
                            t.wait_ge(kro_ready, 1)
                            t.wait_ge(cq_ready, 2)
                            for i, (lo, r) in enumerate(TILES):
                                for c in range(2):
                                    t.transpose(ps[4 + i][0:r, c * P:(c + 1) * P], latT[:, c, lo:lo + r], C("ident"))
                                t.transpose(ps[4 + i][0:r, KVR:LAT], kroT[:, lo:lo + r], C("ident", ROPE, 0, ROPE)).then_inc(lk_full, 1)

                with ExitStack() as st:
                    olB = sbuf(st, "olB", [P, H, TOK])
                    olT = [hT, olB]
                    NPB = 3
                    page_in = [sem(f"page_in{b}") for b in range(NPB)]
                    NQ = H * DS
                    pgs = [sbuf(st, f"pages{b}", [P, NPAGE, LAT]) for b in range(NPB)]
                    pgT = sbuf(st, "pgT", [P, 2, NPAGE * P])
                    pgR = mixT[0:ROPE, :, :].rearrange("p c t -> p (c t)")[:, 0:NPAGE * P]
                    sc = sbuf(st, "scores", [P, NPAGE + 1, NQ])
                    pr = sbuf(st, "probs", [P, NPAGE + 1, NQ])
                    tmax = qcT[:, :, :].rearrange("p c t -> p (c t)")[:, 0:512]
                    qmax = sbuf(st, "qmax", [P, 4])
                    mrep = kvT[:, :, :].rearrange("p c t -> p (c t)")[:, 0:512].rearrange("p (n t) -> p n t", n=4)
                    mall = sbuf(st, "mall", [P, 512])
                    rsum = sbuf(st, "rsum", [P, 512])
                    table = sbuf(st, "page_table", [1, NB * NPAGE], I32)
                    table_in = Signal(sem("table_in"))
                    Prow = mixT[64:128, :, :].rearrange("p c t -> p (c t)")[:, 0:NPAGE * P + 64]
                    orow = mixT[64:128, :, :].rearrange("p c t -> p (c t)")[:, NPAGE * P + 64:NPAGE * P + 64 + KVR]
                    qsl = sc[:, 0:16, :].rearrange("p (c b) q -> p c b q", c=2)
                    qsp = mall[0:ROPE, :].rearrange("p (b q) -> p b q", b=NB)
                    srows = sbuf(st, "srows", [P, 8 + 5 + 5 + 4])
                    snew, mx, esum, m1 = srows[64:128, 0:8], srows[64:128, 8:13], srows[64:128, 13:18], srows[64:128, 18:22]
                    (q_packed, s_full, mx_ready, ex_ready, pt_full, pt_dve, pt_act, v_full, o_ready, ot_full, ol_ready, np_zero) = (sem(x) for x in (
                        "q_packed", "sscore_full", "smax_ready", "sexp_ready", "probs_turned", "probsT_dve", "probsT_act", "values_full",
                        "orow_ready", "orow_turned", "olat_ready", "newkeys_zeroed"))
                    (u_score, u_mcol, u_tr, u_rep, u_mrow, u_sub, u_exp, u_pv, u_out, pg_tr, pg_act, pg_dve) = (
                        sem(x) for x in ("u_score", "u_mcol", "u_tr", "u_rep", "u_mrow", "u_sub", "u_exp", "u_pv", "u_out",
                                         "pg_turned", "pg_act", "pg_dve"))
                    NT = 12

                    def turned_group(q):
                        part, quad = q % 3, q // 3
                        dst = pgT[:, part, quad * 512:(quad + 1) * 512] if part < 2 else pgR[:, quad * 512:(quad + 1) * 512]
                        return part, quad, dst, P if part < 2 else ROPE
                    psc = sc[:, :, :].rearrange("p a b -> p (a b)")
                    ppr = pr[:, :, :].rearrange("p a b -> p (a b)")
                    UNITS = [("p", g) for g in range(4)] + [("s", b) for b in range(NB)]
                    with nc.Block() as block:
                        @block.sync
                        def _(sp):
                            load(sp, table[:, :], A["page_table"].rearrange("(o b) n -> o (b n)", o=1), table_in)
                            sp.wait_ge(table_in.sem, 16)
                            for b in range(NB):
                                _, rows = nc.values_load_multi_w_load_instructions(
                                    table[0:1, b * NPAGE:(b + 1) * NPAGE], engines=(mybir.EngineType.SP,), min_val=0,
                                    max_val=A["cache_mla"].shape[1] - 1)
                                for n in range(NPAGE):
                                    row = rows[n]
                                    if b >= NPB and n == 0:
                                        sp.wait_ge(v_full, b - NPB + 1)
                                        sp.nop()
                                    sp.dma_start(pgs[b % NPB][:, n, :], A["cache_mla"][0, bass.ds(row, 1)].rearrange("o p c -> (o p) c"))\
                                      .then_inc(page_in[b % NPB], 16)

                        @block.tensor
                        def _(t):
                            def turn(b, groups):
                                if b == NB:
                                    return
                                if groups[0] == 0:
                                    t.wait_ge(page_in[b % NPB], 16 * NPAGE * (b // NPB + 1))
                                for q in groups:
                                    n = NT * b + q
                                    part, quad, _, rows = turned_group(q)
                                    if n >= 2:
                                        t.wait_ge(pg_act if n % 2 == 0 else pg_dve, (n - 2) // 2 + 1)
                                    for x in range(4):
                                        src = pgs[b % NPB][:, 4 * quad + x, :]
                                        src = src[:, part * P:(part + 1) * P] if part < 2 else src[:, KVR:LAT]
                                        mm = t.transpose(ps[5 + n % 2][0:rows, x * P:(x + 1) * P], src, C("ident"))
                                    mm.then_inc(pg_tr, 1)

                            def scores(b):
                                t.wait_ge(pg_act, NT // 2 * (b + 1))
                                t.wait_ge(pg_dve, NT // 2 * (b + 1))
                                if b:
                                    t.wait_ge(pt_dve, b)
                                    t.wait_ge(pt_act, b)
                                for k in range(5):
                                    for c in range(3):
                                        lhs = qsl[:, c, b, :] if c < 2 else qsp[:, b, :]
                                        if k < 4:
                                            rhs = pgT[:, c, k * 512:(k + 1) * 512] if c < 2 else pgR[:, k * 512:(k + 1) * 512]
                                        else:
                                            new = slice(SEQ + b * DS, SEQ + (b + 1) * DS)
                                            rhs = latT[:, c, new] if c < 2 else kroT[:, new]
                                        mm = t.matmul(ps[k][64:128, 0:rhs.shape[1]], lhs, rhs, start=(c == 0), stop=(c == 2))
                                mm.then_inc(s_full, 1)

                            def turn_probs(b):
                                t.wait_ge(ex_ready, b + 1)
                                for n in range(NPAGE + 1):
                                    out = ps[n // 8][:, (n % 8) * NQ:(n % 8 + 1) * NQ] if n < NPAGE else ps[4][0:64, P:P + NQ]
                                    w = P if n < NPAGE else 64
                                    mm = t.transpose(out, Prow[:, n * P:n * P + w], C("ident")[64:128, 64:128])
                                mm.then_inc(pt_full, 1)

                            def values(b):
                                t.wait_ge(pt_dve, b + 1)
                                t.wait_ge(pt_act, b + 1)
                                if b:
                                    t.wait_ge(ol_ready, b)
                                for n in range(NPAGE + 1):
                                    rows = P if n < NPAGE else 64
                                    rhs = pgs[b % NPB][:, n, 0:KVR] if n < NPAGE else latK[0:64, 2, 0:KVR]
                                    mm = t.matmul(ps[7][64:128, 0:KVR], pr[0:rows, n, :], rhs, start=(n == 0), stop=(n == NPAGE))
                                mm.then_inc(v_full, 1)

                            def turn_out(b):
                                t.wait_ge(o_ready, b + 1)
                                for c in range(2):
                                    mm = t.transpose(ps[7][:, KVR + c * NQ:KVR + (c + 1) * NQ], orow[:, c * P:(c + 1) * P], C("ident")[64:128, 64:128])
                                mm.then_inc(ot_full, 1)
                            for u, (kind, g) in enumerate(UNITS):
                                if kind == "p":
                                    W = 512
                                    if u:
                                        t.wait_ge(u_sub, u)
                                    for bank, cols, kb, q0, nq in ((0, 0, 0, 0, 256), (1, 0, 1, P, P)):
                                        for c in range(3):
                                            lhs = latT[:, c, kb * P:(kb + 1) * P] if c < 2 else kroT[:, kb * P:(kb + 1) * P]
                                            rhs = (qlT[:, c, 2 * g:2 * g + 2, q0:q0 + nq] if c < 2 else qpT[:, 2 * g:2 * g + 2, q0:q0 + nq])
                                            mm = t.matmul(ps[bank][:, 0:2 * nq], lhs, rhs, start=(c == 0), stop=(c == 2))
                                    mm.then_inc(u_score, 1)
                                    t.wait_ge(u_mcol, u + 1)
                                    for n in range(4):
                                        mm = t.transpose(ps[3][:, n * P:(n + 1) * P], tmax[:, n * P:(n + 1) * P], C("ident"))
                                    mm.then_inc(u_tr, 1)
                                    t.wait_ge(u_rep, u + 1)
                                    for n in range(4):
                                        mm = t.matmul(ps[4][:, n * P:(n + 1) * P], mrep[:, n, :], C("ident"), start=True, stop=True)
                                    mm.then_inc(u_mrow, 1)
                                    t.wait_ge(u_exp, u + 1)
                                    t.matmul(ps[5][:, 0:512], C("ones"), ppr[:, 0:512], start=True, stop=False)
                                    for h in range(2):
                                        t.matmul(ps[5][:, h * 256 + P:h * 256 + 256], C("ones"), ppr[:, 512 + h * P:512 + (h + 1) * P],
                                                 start=False, stop=(h == 1))
                                    for c in range(2):
                                        t.matmul(ps[6 + c][:, 0:512], latK[:, 0, c * P:(c + 1) * P], ppr[:, 0:512], start=True, stop=False)
                                        for h in range(2):
                                            mm = t.matmul(ps[6 + c][:, h * 256 + P:h * 256 + 256], latK[:, 1, c * P:(c + 1) * P],
                                                          ppr[:, 512 + h * P:512 + (h + 1) * P], start=False, stop=(h == 1))
                                    mm.then_inc(u_pv, 1)
                                else:
                                    b = g
                                    if b == 0:
                                        t.wait_ge(u_out, 4)
                                        turn(0, range(NT))
                                        t.wait_ge(q_packed, 1)
                                    scores(b)
                                    if b:
                                        turn_out(b - 1)
                                    turn(b + 1, range(0, 10))
                                    turn_probs(b)
                                    turn(b + 1, range(10, NT))
                                    values(b)
                            turn_out(NB - 1)

                        @block.vector
                        def _(v):
                            def turned_out(b, groups):
                                for q in groups if b < NB else []:
                                    _, _, dst, rows = turned_group(q)
                                    v.wait_ge(pg_tr, NT * b + q + 1)
                                    v.tensor_copy(dst, ps[6][0:rows, :]).then_inc(pg_dve, 1)

                            def scale_out(b):
                                v.wait_ge(v_full, b + 1)
                                dv(v, v.tensor_reduce(m1[:, 1:2], esum, AX_X, ALU.add))
                                dv(v, v.reciprocal(m1[:, 2:3], m1[:, 1:2]))
                                v.tensor_scalar(orow, ps[7][64:128, 0:KVR], m1[:, 2:3], None, ALU.mult).then_inc(o_ready, 1)

                            def lat_out(b):
                                v.wait_ge(ot_full, b + 1)
                                for c in range(2):
                                    last = v.tensor_copy(olT[c][:, :, SEQ + b * DS:SEQ + (b + 1) * DS],
                                                         ps[7][:, KVR + c * NQ:KVR + (c + 1) * NQ].rearrange("p (h q) -> p h q", h=H))
                                dv(v, last)
                                v.sem_inc(ol_ready, 1)
                            for u, (kind, g) in enumerate(UNITS):
                                if kind == "p":
                                    v.wait_ge(u_score, u + 1)
                                    s0 = ps[0][:, 0:512].rearrange("p (h q) -> p h q", h=2)
                                    d0 = psc[:, 0:512].rearrange("p (h q) -> p h q", h=2)
                                    d1 = psc[:, 512:768].rearrange("p (h q) -> p h q", h=2)
                                    s1 = ps[1][:, 0:256].rearrange("p (h q) -> p h q", h=2)
                                    v.tensor_copy(d0[:, :, P:256], s0[:, :, P:256])
                                    for h in range(2):
                                        v.tensor_tensor(d0[:, h, 0:P], s0[:, h, 0:P], C("causal"), ALU.add)
                                        last = v.tensor_tensor(d1[:, h, :], s1[:, h, :], C("causal"), ALU.add)
                                    dv(v, last)
                                    tm = tmax[:, :].rearrange("p (h q) -> p h q", h=2)
                                    v.tensor_copy(tm[:, :, 0:P], d0[:, :, 0:P])
                                    dv(v, v.tensor_tensor(tm[:, :, P:256], d0[:, :, P:256], d1, ALU.max))
                                    v.sem_inc(u_mcol, 1)
                                    v.wait_ge(u_tr, u + 1)
                                    dv(v, v.tensor_reduce(qmax[:, 0:4], ps[3][:, :].rearrange("p (n k) -> p n k", n=4), AX_X, ALU.max))
                                    for n in range(4):
                                        last = v.tensor_scalar(mrep[:, n, :], C("ones"), qmax[:, n:n + 1], None, ALU.mult)
                                    last.then_inc(u_rep, 1)
                                    v.wait_ge(u_mrow, u + 1)
                                    dv(v, v.tensor_copy(mall[:, :], ps[4][:, :]))
                                    m3 = mall[:, :].rearrange("p (h q) -> p h q", h=2)
                                    dv(v, v.tensor_tensor(psc[:, 0:512], psc[:, 0:512], mall[:, :], ALU.subtract))
                                    dv(v, v.tensor_tensor(d1, d1, m3[:, :, P:256], ALU.subtract))
                                    v.sem_inc(u_sub, 1)
                                    v.wait_ge(u_pv, u + 1)
                                    dv(v, v.reciprocal(rsum[:, :], ps[5][:, :]))
                                    for c in range(2):
                                        last = v.tensor_tensor(olT[c][:, 2 * g:2 * g + 2, 0:SEQ],
                                                               ps[6 + c][:, :].rearrange("p (h q) -> p h q", h=2),
                                                               rsum[:, :].rearrange("p (h q) -> p h q", h=2), ALU.mult)
                                    dv(v, last)
                                    v.sem_inc(u_out, 1)
                                else:
                                    b = g
                                    if b == 0:
                                        v.wait_ge(u_exp, 4)
                                        for c in range(2):
                                            v.tensor_copy(qsl[:, c, :, :].rearrange("p b (h t) -> p b h t", h=H),
                                                          qlT[:, c, :, SEQ:TOK].rearrange("p h (b t) -> p b h t", b=NB))
                                        dv(v, v.tensor_copy(qsp.rearrange("p b (h t) -> p b h t", h=H), qpT[:, :, SEQ:TOK].rearrange("p h (b t) -> p b h t", b=NB)))
                                        v.sem_inc(q_packed, 1)
                                        turned_out(0, range(1, NT, 2))
                                    else:
                                        scale_out(b - 1)
                                    v.wait_ge(s_full, b + 1)
                                    for k in range(4):
                                        v.tensor_reduce(mx[:, k:k + 1], ps[k][64:128, :], AX_X, ALU.max)
                                    v.memset(Prow[:, NPAGE * P:NPAGE * P + 64], 0.0)
                                    dv(v, v.tensor_tensor(snew, ps[4][64:128, 0:DS], C("own")[64:128, :], ALU.add))
                                    dv(v, v.tensor_reduce(mx[:, 4:5], snew, AX_X, ALU.max))
                                    dv(v, v.tensor_reduce(m1[:, 3:4], mx, AX_X, ALU.max))
                                    dv(v, v.tensor_scalar(m1[:, 0:1], m1[:, 3:4], -SCALE, None, ALU.mult))
                                    v.sem_inc(mx_ready, 1)
                                    if b:
                                        lat_out(b - 1)
                                    turned_out(b + 1, range(1, 10, 2))
                                    v.wait_ge(pt_full, b + 1)
                                    v.tensor_copy(pr[:, 0:8, :], ps[0][:, :].rearrange("p (n q) -> p n q", n=8))
                                    v.tensor_copy(pr[0:64, NPAGE, :], ps[4][0:64, P:P + NQ]).then_inc(pt_dve, 1)
                                    turned_out(b + 1, range(11, NT, 2))
                            scale_out(NB - 1)
                            lat_out(NB - 1)

                        @block.scalar
                        def _(s):
                            def turned_out(b, groups):
                                for q in groups if b < NB else []:
                                    _, _, dst, rows = turned_group(q)
                                    s.wait_ge(pg_tr, NT * b + q + 1)
                                    s.activation(dst, ps[5][0:rows, :], ACT.Copy).then_inc(pg_act, 1)
                            for u, (kind, g) in enumerate(UNITS):
                                if kind == "p":
                                    s.wait_ge(u_sub, u + 1)
                                    s.activation(ppr[:, 0:768], psc[:, 0:768], ACT.Exp, scale=SCALE).then_inc(u_exp, 1)
                                else:
                                    if g == 0:
                                        turned_out(0, range(0, NT, 2))
                                    turned_out(g + 1, range(0, 4, 2))
                                    s.wait_ge(mx_ready, g + 1)
                                    for k in range(4):
                                        s.activation(Prow[:, k * 512:(k + 1) * 512], ps[k][64:128, :], ACT.Exp, bias=m1[:, 0:1], scale=SCALE,
                                                     accum_out=esum[:, k:k + 1])
                                    s.activation(Prow[:, NPAGE * P + g * DS:NPAGE * P + (g + 1) * DS], snew, ACT.Exp, bias=m1[:, 0:1], scale=SCALE,
                                                 accum_out=esum[:, 4:5]).then_inc(ex_ready, 1)
                                    turned_out(g + 1, range(4, 10, 2))
                                    s.wait_ge(pt_full, g + 1)
                                    s.activation(pr[:, 8:16, :], ps[1][:, :].rearrange("p (n q) -> p n q", n=8), ACT.Copy).then_inc(pt_act, 1)
                                    turned_out(g + 1, range(10, NT, 2))

                    full, out_a, out_d = sem("ov_full"), sem("ov_act"), sem("ov_dve")
                    with nc.Block() as block:
                        @block.tensor
                        def _(t):
                            t.wait_ge(uv_in.sem, 16)
                            for h in range(H):
                                for c in range(2):
                                    mm = t.matmul(ps[h // 2][(h % 2) * 64:(h % 2) * 64 + 64, 0:TOK], uv[:, c, h * VD:(h + 1) * VD],
                                                  olT[c][:, h, :], start=(c == 0), stop=(c == 1))
                                mm.then_inc(full, 1)

                        @block.vector
                        def _(v):
                            for g in (0, 1):
                                v.wait_ge(full, 2 * g + 2)
                                dv(v, v.tensor_copy(mixT[:, g, :], ps[g][:, 0:TOK]))

                        @block.scalar
                        def _(s):
                            for g in (2, 3):
                                s.wait_ge(full, 2 * g + 2)
                                ac(s, s.activation(mixT[:, g, :], ps[g][:, 0:TOK], ACT.Copy))

            AR = hT[:, :, :].rearrange("p (c a) t -> p c a t", a=2)
            with ExitStack() as rk:
                bF = sbuf(rk, "bF", [P, 4, TOK])
                kF = sbuf(rk, "kF", [P, 4, TOK])
                gT = sbuf(rk, "gT", [P, 4, TOK])
                bonus = sbuf(rk, "bonus", [P, 4, TOK])
                rowB = sbuf(rk, "rowB", [P, 3, RDIM])
                rowK = sbuf(rk, "rowK", [P, 3, RDIM])
                rowV = sbuf(rk, "rowV", [P, 3, RDIM])
                wend = sbuf(rk, "wend", [P, 4, 4])
                wends = sbuf(rk, "wends", [P, 4, NB])
                S0T = sbuf(rk, "S0T", [P, NB, 4, RD])
                with ExitStack() as st:
                    shrow = sbuf(st, "shrow", [NB, RPROJ])
                    shT = sbuf(st, "shT", [P, RT, NB])
                    srow = sbuf(st, "srow", [RD, NB, RDIM])
                    lora = sbuf(st, "lora", [P, RDIM])
                    g2 = sbuf(st, "g2", [P, RDIM])
                    lastc = sbuf(st, "last_cols", [P, 1 + NB, RT])
                    lastr = sbuf(st, "last_rows", [(1 + NB) * RT, P])
                    dif = sbuf(st, "dif", [P, RT, TOK])
                    tw = sbuf(st, "tw", [64, TOK])
                    sg = sbuf(st, "sg", [P, TOK])
                    t1, t2, t3, t4, t5 = (dif[:, 4 * n:4 * n + 4, :] if n < 3 else sbuf(st, f"t{n}", [P, 4, TOK])[:, :, :] for n in range(5))
                    sh_in, s_in, lo_in = Signal(sem("shift_in")), Signal(sem("state_in")), Signal(sem("lora_in"))
                    (sh_full, lc_ready, lr_full, lr_ready, st_full, st_free, xs_ready, tg_ready, lo_full, lo_act, lo_dve, sq_ready,
                     kk_full, kk_var, kk_rstd, ex_in, ex_out, bo_ready, bo_full, ops_ready, row_full, row_free) = (sem(x) for x in (
                         "shift_turned", "last_ready", "last_turned", "last_rows_ready", "state_turned", "state_taken", "xs_ready",
                         "tanh_ready", "lora_full", "lora_act", "lora_dve", "kk_sq", "kk_sum", "kk_var", "kk_rstd", "exp_in",
                         "exp_out", "bonus_in", "bonus_sum", "operands_ready", "rows_turned", "rows_taken"))
                    with nc.Block() as block:
                        @block.sync
                        def _(sp):
                            load(sp, shrow[:, :], A["state_rwkv_shift"][0], sh_in)
                            load(sp, lora[0:64, :], A["rwkv_w2"][0], lo_in)
                            load(sp, lora[64:128, :], A["rwkv_a2"][0], lo_in)
                            load(sp, g2[:, :], A["rwkv_g2"][0], lo_in)
                            for b in range(NB):
                                load(sp, srow[:, b, :].rearrange("v (h k) -> v h k", h=RH), A["state_rwkv"][0, b].rearrange("h v k -> v h k"), s_in)
                            sp.wait_ge(lr_ready, 1)
                            store(sp, O["new_shift_prompt"][0].rearrange("b (c p) -> (b c) p", p=P), lastr[0:RT, :])
                            store(sp, O["new_shift_sample"][0].rearrange("b (c p) -> (b c) p", p=P), lastr[RT:(1 + NB) * RT, :])
                            sp.wait_ge(stored.sem, stored.n)

                        @block.vector
                        def _(v):
                            v.tensor_copy(lastc[:, 0, :], rwT[:, :, SEQ - 1])
                            dv(v, v.tensor_copy(lastc[:, 1:1 + NB, :], rwT[:, :, SEQ + DS - 1:TOK:DS].rearrange("p c b -> p b c")))
                            v.sem_inc(lc_ready, 1)
                            v.wait_ge(sh_full, 1)
                            dv(v, v.tensor_copy(shT[:, :, :], ps[0][:, 0:RT * NB].rearrange("p (c b) -> p c b", c=RT)))
                            rs = rwT[:, :, SEQ:TOK].rearrange("p c (b t) -> p c b t", b=NB)
                            ds = dif[:, :, SEQ:TOK].rearrange("p c (b t) -> p c b t", b=NB)
                            v.tensor_tensor(dif[:, :, 1:SEQ], rwT[:, :, 0:SEQ - 1], rwT[:, :, 1:SEQ], ALU.subtract)
                            v.tensor_scalar(dif[:, :, 0], rwT[:, :, 0], -1.0, None, ALU.mult)
                            v.tensor_tensor(ds[:, :, :, 1:DS], rs[:, :, :, 0:DS - 1], rs[:, :, :, 1:DS], ALU.subtract)
                            dv(v, v.tensor_tensor(ds[:, :, :, 0], shT[:, :, :], rs[:, :, :, 0], ALU.subtract))
                            for c in range(RT):
                                last = v.scalar_tensor_tensor(out=rwT[:, c, :], in0=dif[:, c, :], scalar=V("rwkv_mu", c), in1=rwT[:, c, :],
                                                              op0=ALU.mult, op1=ALU.add)
                            dv(v, last)
                            v.sem_inc(xs_ready, 1)
                            v.wait_ge(lr_full, 1)
                            v.tensor_copy(lastr[:, :], ps[1][0:(1 + NB) * RT, 0:P]).then_inc(lr_ready, 1)
                            kk, rT, kT, vT = t1, rwT[:, 0:4, :], rwT[:, 4:8, :], rwT[:, 8:12, :]
                            for c in range(4):
                                last = v.tensor_scalar(kk[:, c, :], kT[:, c, :], V("rwkv_k_k", c), None, ALU.mult)
                            dv(v, last)
                            dv(v, v.tensor_tensor(t2, kk, kk, ALU.mult))
                            v.sem_inc(sq_ready, 1)
                            v.wait_ge(kk_full, 1)
                            for c in range(4):
                                last = v.tensor_scalar(t2[:, c, :], ps[4 + c][:, 0:TOK], 1e-24, None, ALU.max)
                            dv(v, last)
                            v.sem_inc(kk_var, 1)
                            v.wait_ge(lo_act, 4)
                            for c in range(4):
                                last = v.tensor_tensor_scan(t4[:, c, :], C("reset_rw"), t3[:, c, :], 0.0, ALU.mult, ALU.add)
                            dv(v, last)
                            dv(v, v.tensor_tensor(t3, t4, t3, ALU.subtract))
                            v.sem_inc(ex_in, 1)
                            v.wait_ge(lo_act, 8)
                            for c in range(4):
                                last = v.tensor_scalar(bF[:, c, :], t5[:, c, :], 1.0, V("rwkv_k_a", c), ALU.subtract, ALU.mult)
                            dv(v, last)
                            dv(v, v.scalar_tensor_tensor(out=kT, in0=bF[:, :, :], scalar=1.0, in1=kT, op0=ALU.add, op1=ALU.mult))
                            v.wait_ge(kk_rstd, 1)
                            dv(v, v.reciprocal(t2, t2))
                            dv(v, v.tensor_tensor(kk, kk, t2, ALU.mult))
                            for c in range(4):
                                last = v.scalar_tensor_tensor(out=t2[:, c, :], in0=rT[:, c, :], scalar=V("rwkv_r_k", c), in1=kT[:, c, :],
                                                              op0=ALU.mult, op1=ALU.mult)
                            dv(v, last)
                            v.sem_inc(bo_ready, 1)
                            for c in range(4):
                                v.wait_ge(lo_full, 9 + c)
                                last = v.tensor_copy(gT[:, c, :], ps[c][:, 0:TOK])
                            dv(v, last)
                            v.wait_ge(ex_out, 3)
                            v.scalar_tensor_tensor(out=AR[:, :, 0, :], in0=kk, scalar=-1.0, in1=t3, op0=ALU.mult, op1=ALU.mult)
                            v.tensor_tensor(AR[:, :, 1, :], rT, bonus[:, :, :], ALU.mult)
                            v.tensor_copy(wend[:, :, :], bonus[:, :, RC - 1:SEQ:RC])
                            v.tensor_copy(wends[:, :, :], bonus[:, :, SEQ + DS - 1:TOK:DS])
                            dv(v, v.tensor_tensor(bF[:, :, :], kk, t5, ALU.mult))
                            dv(v, v.tensor_tensor(bF[:, :, :], bF[:, :, :], kF[:, :, :], ALU.mult))
                            dv(v, v.tensor_tensor(kF[:, :, :], kT, kF[:, :, :], ALU.mult))
                            v.sem_inc(ops_ready, 1)
                            v.wait_ge(bo_full, 1)
                            for c in range(4):
                                last = v.tensor_tensor(bonus[:, c, :], ps[4 + c][:, 0:TOK], vT[:, c, :], ALU.mult)
                            dv(v, last)
                            v.sem_inc(ops_ready, 1)
                            for n in range(9):
                                v.wait_ge(row_full, n + 1)
                                r = TILES[n % 3][1]
                                v.tensor_copy((rowB, rowK, rowV)[n // 3][0:r, n % 3, :], ps[n % 2][0:r, :]).then_inc(row_free, 1)

                        @block.scalar
                        def _(s):
                            s.wait_ge(xs_ready, 1)
                            s.activation(tw[:, :], rwT[0:64, 12, :], ACT.Tanh).then_inc(tg_ready, 1)
                            s.activation(sg[:, :], rwT[:, 13, :], ACT.Sigmoid).then_inc(tg_ready, 1)
                            for n in range(8):
                                s.wait_ge(lo_full, n + 1)
                                c = n % 4
                                dst, bias = (t3, "rwkv_w0") if n < 4 else (t5, "rwkv_a0")
                                ac(s, s.activation(dst[:, c, :], ps[c][:, 0:TOK], ACT.Sigmoid, bias=V(bias, c)))
                                s.sem_inc(lo_act, 1)
                            s.wait_ge(kk_var, 1)
                            ac(s, s.activation(t2, t2, ACT.Sqrt))
                            s.sem_inc(kk_rstd, 1)
                            s.wait_ge(ex_in, 1)
                            s.activation(bonus[:, :, :], t4, ACT.Exp, scale=-HALF_E).then_inc(ex_out, 1)
                            s.activation(kF[:, :, :], t4, ACT.Exp, scale=HALF_E).then_inc(ex_out, 1)
                            s.activation(t3, t3, ACT.Exp, scale=-HALF_E).then_inc(ex_out, 1)
                            for q in range(8):
                                s.wait_ge(st_full, q + 1)
                                s.activation(S0T[:, q, :, :], ps[2 + q % 2][:, 0:256].rearrange("p (c v) -> p c v", c=4), ACT.Copy).then_inc(st_free, 1)

                        @block.tensor
                        def _(t):
                            t.wait_ge(sh_in.sem, 16)
                            for c in range(RT):
                                mm = t.transpose(ps[0][:, c * NB:(c + 1) * NB], shrow[:, c * P:(c + 1) * P], C("ident", NB, 0, NB))
                            mm.then_inc(sh_full, 1)
                            t.wait_ge(lc_ready, 1)
                            t.transpose(ps[1][0:(1 + NB) * RT, 0:P], lastc[:, :, :].rearrange("p b c -> p (b c)"), C("ident")).then_inc(lr_full, 1)
                            t.wait_ge(sq_ready, 1)
                            for c in range(4):
                                mm = t.matmul(ps[4 + c][:, 0:TOK], C("head_ones"), t2[:, c, :], start=True, stop=True)
                            mm.then_inc(kk_full, 1)
                            t.wait_ge(tg_ready, 2)
                            t.wait_ge(lo_in.sem, 48)
                            t.wait_ge(lr_ready, 1)
                            for n in range(12):
                                c = n % 4
                                if n >= 4:
                                    t.wait_ge(lo_act, n - 3)
                                if n < 4:
                                    mm = t.matmul(ps[c][:, 0:TOK], lora[0:64, c * P:(c + 1) * P], tw[:, :], start=True, stop=True)
                                elif n < 8:
                                    mm = t.matmul(ps[c][:, 0:TOK], lora[64:128, c * P:(c + 1) * P], rwT[64:128, 12, :], start=True, stop=True)
                                else:
                                    mm = t.matmul(ps[c][:, 0:TOK], g2[:, c * P:(c + 1) * P], sg[:, :], start=True, stop=True)
                                mm.then_inc(lo_full, 1)
                            t.wait_ge(kk_var, 1)
                            t.wait_ge(bo_ready, 1)
                            for c in range(4):
                                mm = t.matmul(ps[4 + c][:, 0:TOK], C("head_ones"), t2[:, c, :], start=True, stop=True)
                            mm.then_inc(bo_full, 1)
                            t.wait_ge(ops_ready, 2)
                            t.wait_ge(s_in.sem, 16 * NB)
                            for n in range(9):
                                lo, r = TILES[n % 3]
                                if n >= 2:
                                    t.wait_ge(row_free, n - 1)
                                src = (bF, kF, rwT)[n // 3]
                                for c in range(4):
                                    mm = t.transpose(ps[n % 2][0:r, c * P:(c + 1) * P], src[:, (8 if n >= 6 else 0) + c, lo:lo + r], C("ident"))
                                mm.then_inc(row_full, 1)
                                if n < NB:
                                    if n >= 2:
                                        t.wait_ge(st_free, n - 1)
                                    for c in range(4):
                                        mm = t.transpose(ps[2 + n % 2][:, c * RD:(c + 1) * RD], srow[:, n, c * P:(c + 1) * P], C("ident", RD, 0, RD))
                                    mm.then_inc(st_full, 1)

                BM = sbuf(rk, "BM", [P, 3, RH, 2, P])
                KM = sbuf(rk, "KM", [P, 3, RH, 2, P])
                XT = sbuf(rk, "XT", [P, 3, RH, P])
                with ExitStack() as st:
                    X = sbuf(st, "X", [P, RH, P])
                    T1 = sbuf(st, "T1", [P, RH, P])
                    prod_full, prod_free, xt_ready, x_full, x_ready, t_full, t_ready, d_full, d_ready = (sem(x) for x in (
                        "prod_full", "prod_free", "xt_ready", "x_turned", "x_ready", "t_full", "t_ready", "d_full", "d_ready"))
                    LEVELS = [[2, 4, 8, 16, 32], [2, 4, 8, 16, 32], [2, 4]]
                    with nc.Block() as block:
                        @block.tensor
                        def _(t):
                            n = xn = tn = dn = 0
                            for i, (lo, r) in enumerate(TILES):
                                for src in (bF, kF):
                                    for pr in range(4):
                                        if n >= 2:
                                            t.wait_ge(prod_free, n - 1)
                                        h0 = 64 * (pr % 2)
                                        for q in range(2):
                                            p2 = 2 * (pr // 2) + q
                                            mm = t.matmul(ps[n % 2][0:r, q * 256:(q + 1) * 256].rearrange("p (a t) -> p a t", a=2)[:, :, 0:r],
                                                          src[h0:h0 + 64, p2, lo:lo + r], AR[h0:h0 + 64, p2, :, lo:lo + r], start=True, stop=True)
                                        mm.then_inc(prod_full, 1)
                                        n += 1
                                for g in range(2):
                                    xn += 1
                                    t.wait_ge(xt_ready, xn)
                                    for q in range(4):
                                        mm = t.transpose(ps[2 + g][0:r, q * P:q * P + r], XT[0:r, i, 4 * g + q, 0:r], C("ident", r, 0, r))
                                    mm.then_inc(x_full, 1)
                                for li, s_ in enumerate(LEVELS[i]):
                                    lastlev = li == len(LEVELS[i]) - 1
                                    for g in range(2):
                                        t.wait_ge(x_ready, xn - 1 + g)
                                        if li:
                                            t.wait_ge(d_ready, dn - 1 + g)
                                        for q in range(4):
                                            h = 4 * g + q
                                            mm = t.matmul(ps[2 + g][0:r, q * P:q * P + r], BM[0:r, i, h, 0, 0:r], X[0:r, h, 0:r], start=True, stop=True)
                                        mm.then_inc(t_full, 1)
                                    for g in range(2):
                                        tn += 1
                                        t.wait_ge(t_ready, tn)
                                        for q in range(4):
                                            h = 4 * g + q
                                            if not lastlev:
                                                t.matmul(ps[4 + g][0:r, q * P:q * P + r], XT[0:r, i, h, 0:r], T1[0:r, h, 0:r], start=True, stop=True)
                                            mm = t.matmul(ps[6 + g][0:r, q * P:q * P + r], T1[0:r, h, 0:r], XT[0:r, i, h, 0:r], start=True, stop=True)
                                        mm.then_inc(d_full, 1)
                                        dn += 1

                        @block.vector
                        def _(v):
                            n = xn = tn = dn = 0
                            for i, (lo, r) in enumerate(TILES):
                                mask = "rw_T" if i < 2 else "sm_T"
                                m3 = C(mask, r).rearrange("p (o a t) -> p o a t", o=1, a=2)[:, :, :, 0:r]
                                for dst in (BM, KM):
                                    for pr in range(4):
                                        n += 1
                                        v.wait_ge(prod_full, n)
                                        for q in range(2):
                                            last = v.tensor_tensor(dst[0:r, i, 4 * (pr // 2) + 2 * q + pr % 2, :, 0:r],
                                                                   ps[(n - 1) % 2][0:r, q * 256:(q + 1) * 256].rearrange("p (a t) -> p a t", a=2)[:, :, 0:r],
                                                                   m3[:, 0], ALU.mult)
                                        dv(v, last)
                                        v.sem_inc(prod_free, 1)
                                dv(v, v.tensor_tensor(XT[0:r, i, :, 0:r], BM[0:r, i, :, 0, 0:r],
                                                      C("lev1_T", r, 0, r).rearrange("p (o t) -> p o t", o=1).to_broadcast([r, RH, r]), ALU.mult))
                                for g in range(2):
                                    dv(v, v.tensor_tensor(XT[0:r, i, 4 * g:4 * g + 4, 0:r], XT[0:r, i, 4 * g:4 * g + 4, 0:r],
                                                          C("ident", r, 0, r).rearrange("p (o t) -> p o t", o=1).to_broadcast([r, 4, r]), ALU.add))
                                    v.sem_inc(xt_ready, 1)
                                for g in range(2):
                                    xn += 1
                                    v.wait_ge(x_full, xn)
                                    dv(v, v.tensor_copy(X[0:r, 4 * g:4 * g + 4, 0:r], ps[2 + g][0:r, :].rearrange("p (q t) -> p q t", q=4)[:, :, 0:r]))
                                    v.sem_inc(x_ready, 1)
                                for li, s_ in enumerate(LEVELS[i]):
                                    lastlev = li == len(LEVELS[i]) - 1
                                    for g in range(2):
                                        tn += 1
                                        v.wait_ge(t_full, tn)
                                        v.tensor_tensor(T1[0:r, 4 * g:4 * g + 4, 0:r], ps[2 + g][0:r, :].rearrange("p (q t) -> p q t", q=4)[:, :, 0:r],
                                                        C(f"lev{s_}", r, 0, r).rearrange("p (o t) -> p o t", o=1).to_broadcast([r, 4, r]),
                                                        ALU.mult).then_inc(t_ready, 1)
                                    for g in range(2):
                                        dn += 1
                                        v.wait_ge(d_full, dn)
                                        if not lastlev:
                                            v.tensor_tensor(X[0:r, 4 * g:4 * g + 4, 0:r], X[0:r, 4 * g:4 * g + 4, 0:r],
                                                            ps[4 + g][0:r, :].rearrange("p (q t) -> p q t", q=4)[:, :, 0:r], ALU.add)
                                        dv(v, v.tensor_tensor(XT[0:r, i, 4 * g:4 * g + 4, 0:r], XT[0:r, i, 4 * g:4 * g + 4, 0:r],
                                                              ps[6 + g][0:r, :].rearrange("p (q t) -> p q t", q=4)[:, :, 0:r], ALU.add))
                                        v.sem_inc(d_ready, 1)

                with ExitStack() as st:
                    NCH = SEQ // RC
                    YB = (4, 7)
                    ST = sbuf(st, "ST", [P, NCH + 1, 4, RD])
                    rhs_s = sbuf(st, "rhs", [P, RDIM])
                    U = sbuf(st, "U", [P, RDIM])
                    SY = sbuf(st, "SY", [P, 4, 2, 64])
                    rhs2 = sbuf(st, "rhs2", [64, RDIM])
                    U2 = sbuf(st, "U2", [64, RDIM])
                    ub = sbuf(st, "ub", [64, 2, NB, RD])
                    vb = sbuf(st, "vb", [64, 2, NB, RD])
                    SN = S0T
                    NR = 3
                    srow2 = sbuf(st, "srow2", [RD, NR, RDIM])
                    row_out = [Signal(sem(f"row_out{n}")) for n in range(NR)]
                    y_copied = sem("y_copied")
                    (st0, r_full, r_ready, u_full, u_ready, s_full, s_ready, y_full, y_ready, sy_full, sy_ready, tr_full, mv_full, r2_ready,
                     u2_full, u2_ready, y2_full, y2_ready, blk_ready, n_full, n_ready, o_full, o_ready) = (sem(x) for x in (
                         "state0", "rhs_full", "rhs_ready", "u_full", "u_ready", "s_full", "s_ready", "y_full", "y_ready", "sy_full",
                         "sy_ready", "sy_turned", "mv_full", "rhs2_ready", "u2_full", "u2_ready", "y2_full", "y2_ready", "blk_ready",
                         "new_full", "new_ready", "row_full", "row_ready"))
                    with nc.Block() as block:
                        @block.tensor
                        def _(t):
                            def sample_reads():
                                for h in range(RH):
                                    h0, pr = 64 * (h % 2), h // 2
                                    out = ps[5 + h % 2][h0:h0 + 64, pr * P:(pr + 1) * P].rearrange("p (a t) -> p a t", a=2)
                                    for b in range(NB):
                                        mm = t.matmul(out[:, :, b * DS:(b + 1) * DS], S0T[h0:h0 + 64, b, pr, :],
                                                      AR[h0:h0 + 64, pr, :, SEQ + b * DS:SEQ + (b + 1) * DS], start=True, stop=True)
                                mm.then_inc(sy_full, 1)
                            sample_reads()
                            t.wait_ge(st0, 1)
                            for c in range(NCH):
                                i, off = c // 2, RC * (c % 2)
                                js = slice(off, off + RC)
                                if c:
                                    t.wait_ge(s_ready, c)
                                for h in range(RH):
                                    h0, pr = 64 * (h % 2), h // 2
                                    own = h % 2 == c % 2
                                    t.matmul(ps[h % 2][js, h * RD:(h + 1) * RD], AR[h0:h0 + 64, pr, 0, c * RC:(c + 1) * RC], ST[h0:h0 + 64, c, pr, :], start=True, stop=not own)
                                    mm = t.matmul(ps[c % 2][js, h * RD:(h + 1) * RD], KM[js, i, h, 0, js], rowV[js, i, h * RD:(h + 1) * RD], start=not own, stop=True)
                                mm.then_inc(r_full, 1)
                                t.wait_ge(r_ready, c + 1)
                                for h in range(RH):
                                    mm = t.matmul(ps[2][js, h * RD:(h + 1) * RD], XT[js, i, h, js], rhs_s[js, h * RD:(h + 1) * RD], start=True, stop=True)
                                mm.then_inc(u_full, 1)
                                t.wait_ge(u_ready, c + 1)
                                for h in range(RH):
                                    h0, pr = 64 * (h % 2), h // 2
                                    out = ps[3][h0:h0 + 64, pr * RD:(pr + 1) * RD]
                                    t.matmul(out, rowB[js, i, h * RD:(h + 1) * RD], U[js, h * RD:(h + 1) * RD], start=True, stop=False)
                                    mm = t.matmul(out, rowK[js, i, h * RD:(h + 1) * RD], rowV[js, i, h * RD:(h + 1) * RD], start=False, stop=True)
                                mm.then_inc(s_full, 1)
                                if c >= 1:
                                    t.wait_ge(y_ready, c)
                                for h in range(RH):
                                    h0, pr = 64 * (h % 2), h // 2
                                    own = h % 2 == c % 2
                                    out = ps[YB[c % 2]][h0:h0 + 64, pr * RC:(pr + 1) * RC]
                                    t.matmul(ps[YB[h % 2]][h0:h0 + 64, pr * RC:(pr + 1) * RC], ST[h0:h0 + 64, c, pr, :], AR[h0:h0 + 64, pr, 1, c * RC:(c + 1) * RC],
                                             start=True, stop=not own)
                                    t.matmul(out, U[js, h * RD:(h + 1) * RD], BM[js, i, h, 1, js], start=not own, stop=False)
                                    mm = t.matmul(out, rowV[js, i, h * RD:(h + 1) * RD], KM[js, i, h, 1, js], start=False, stop=True)
                                mm.then_inc(y_full, 1)
                            t.wait_ge(sy_ready, 2)
                            t.wait_ge(y_ready, NCH)
                            for pr in range(4):
                                mm = t.transpose(ps[6][0:64, pr * P:(pr + 1) * P], SY[:, pr, 0, :], C("ident"))
                            mm.then_inc(tr_full, 1)
                            for h in range(RH):
                                mm = t.matmul(ps[7][0:64, h * RD:(h + 1) * RD], KM[0:64, 2, h, 0, 0:64], rowV[0:64, 2, h * RD:(h + 1) * RD], start=True, stop=True)
                            mm.then_inc(mv_full, 1)
                            t.wait_ge(r2_ready, 1)
                            for h in range(RH):
                                mm = t.matmul(ps[6][0:64, h * RD:(h + 1) * RD], XT[0:64, 2, h, 0:64], rhs2[:, h * RD:(h + 1) * RD], start=True, stop=True)
                            mm.then_inc(u2_full, 1)
                            t.wait_ge(u2_ready, 1)
                            for h in range(RH):
                                h0, pr = 64 * (h % 2), h // 2
                                out = ps[7][h0:h0 + 64, pr * 64:(pr + 1) * 64]
                                t.matmul(out, U2[:, h * RD:(h + 1) * RD], BM[0:64, 2, h, 1, 0:64], start=True, stop=False)
                                mm = t.matmul(out, rowV[0:64, 2, h * RD:(h + 1) * RD], KM[0:64, 2, h, 1, 0:64], start=False, stop=True)
                            mm.then_inc(y2_full, 1)
                            for h in range(RH):
                                h0, pr = 64 * (h % 2), h // 2
                                t.wait_ge(blk_ready, h + 1)
                                if h % 2 == 0 and pr >= 2:
                                    t.wait_ge(n_ready, pr - 1)
                                out = ps[0 + pr % 2][h0:h0 + 64, :]
                                t.matmul(out, rowB[0:64, 2, h * RD:(h + 1) * RD], ub[:, h % 2, :, :].rearrange("p b v -> p (b v)"), start=True, stop=False)
                                mm = t.matmul(out, rowK[0:64, 2, h * RD:(h + 1) * RD], vb[:, h % 2, :, :].rearrange("p b v -> p (b v)"), start=False, stop=True)
                                mm.then_inc(n_full, 1)
                            t.wait_ge(s_ready, NCH)
                            t.wait_ge(n_ready, 4)
                            t.wait_ge(y_ready, NCH)
                            for n in range(1 + NB):
                                if n >= 2:
                                    t.wait_ge(o_ready, n - 1)
                                for pr in range(4):
                                    src = ST[:, NCH, pr, :] if n == 0 else SN[:, n - 1, pr, :]
                                    mm = t.transpose(ps[2 + n % 2][0:RD, pr * P:(pr + 1) * P], src, C("ident"))
                                mm.then_inc(o_full, 1)

                        @block.vector
                        def _(v):
                            dv(v, v.memset(ST[:, 0, :, :], 0.0))
                            v.sem_inc(st0, 1)
                            yv = mixT[:, 4:8, :]

                            def y_add(c):
                                h0 = 64 * ((c + 1) % 2)
                                v.wait_ge(y_copied, c + 1)
                                v.tensor_tensor(yv[h0:h0 + 64, :, c * RC:(c + 1) * RC], yv[h0:h0 + 64, :, c * RC:(c + 1) * RC],
                                                ps[YB[(c + 1) % 2]][h0:h0 + 64, 0:256].rearrange("p (c t) -> p c t", c=4), ALU.add).then_inc(y_ready, 1)
                            for c in range(NCH):
                                js = slice(RC * (c % 2), RC * (c % 2) + RC)
                                v.wait_ge(r_full, c + 1)
                                dv(v, v.tensor_copy(rhs_s[js, :], ps[c % 2][js, :]))
                                other = (c + 1) % 2
                                rv, pv_ = (x[js, :].rearrange("p (c a v) -> p c a v", c=4, a=2)[:, :, other, :] for x in (rhs_s, ps[other]))
                                v.tensor_tensor(rv, rv, pv_, ALU.add).then_inc(r_ready, 1)
                                v.wait_ge(u_full, c + 1)
                                v.tensor_copy(U[js, :], ps[2][js, :]).then_inc(u_ready, 1)
                                v.wait_ge(s_full, c + 1)
                                dv(v, v.tensor_tensor(ST[:, c + 1, :, :], ST[:, c, :, :], ps[3][:, 0:256].rearrange("p (c v) -> p c v", c=4), ALU.add))
                                dv(v, v.tensor_tensor(ST[:, c + 1, :, :], ST[:, c + 1, :, :], wend[:, :, c:c + 1].to_broadcast([P, 4, RD]), ALU.mult))
                                v.sem_inc(s_ready, 1)
                                if c:
                                    y_add(c - 1)
                            y_add(NCH - 1)
                            v.wait_ge(sy_ready, 2)
                            v.wait_ge(tr_full, 1)
                            dv(v, v.tensor_copy(rhs2[:, :], ps[6][0:64, :]))
                            v.wait_ge(mv_full, 1)
                            v.tensor_tensor(rhs2[:, :], rhs2[:, :], ps[7][0:64, :], ALU.add).then_inc(r2_ready, 1)
                            v.wait_ge(u2_full, 1)
                            dv(v, v.tensor_copy(U2[:, :], ps[6][0:64, :]))
                            v.sem_inc(u2_ready, 1)
                            v.wait_ge(y2_full, 1)
                            v.tensor_tensor(yv[:, :, SEQ:TOK], SY[:, :, 1, :], ps[7][:, 0:256].rearrange("p (c t) -> p c t", c=4), ALU.add)
                            sel = C("bsel", 64).rearrange("p (b o) -> p b o", o=1).to_broadcast([64, NB, RD])
                            for h in range(RH):
                                if h >= 2:
                                    v.wait_ge(n_full, h - 1)
                                v.tensor_tensor(ub[:, h % 2, :, :], U2[:, h * RD:(h + 1) * RD].rearrange("p (o v) -> p o v", o=1).to_broadcast([64, NB, RD]), sel, ALU.mult)
                                v.tensor_tensor(vb[:, h % 2, :, :], rowV[0:64, 2, h * RD:(h + 1) * RD].rearrange("p (o v) -> p o v", o=1).to_broadcast([64, NB, RD]), sel,
                                                ALU.mult).then_inc(blk_ready, 1)
                                if h % 2:
                                    pr = h // 2
                                    v.wait_ge(n_full, h + 1)
                                    dv(v, v.tensor_tensor(SN[:, :, pr, :], S0T[:, :, pr, :], ps[pr % 2][:, :].rearrange("p (b v) -> p b v", b=NB), ALU.add))
                                    dv(v, v.tensor_tensor(SN[:, :, pr, :], SN[:, :, pr, :], wends[:, pr, :].rearrange("p (b o) -> p b o", o=1).to_broadcast([P, NB, RD]), ALU.mult))
                                    v.sem_inc(n_ready, 1)

                        @block.scalar
                        def _(s):
                            s.wait_ge(sy_full, 1)
                            for q in range(2):
                                s.activation(SY[64 * q:64 * q + 64, :, :, :], ps[5 + q][64 * q:64 * q + 64, :].rearrange("p (c a t) -> p c a t", c=4, a=2),
                                             ACT.Copy).then_inc(sy_ready, 1)
                            for c in range(NCH):
                                s.wait_ge(y_full, c + 1)
                                s.activation(mixT[:, 4:8, c * RC:(c + 1) * RC], ps[YB[c % 2]][:, 0:256].rearrange("p (c t) -> p c t", c=4), ACT.Copy).then_inc(y_copied, 1)
                            for n in range(1 + NB):
                                s.wait_ge(o_full, n + 1)
                                if n >= NR:
                                    s.wait_ge(row_out[n % NR].sem, 16 * (n // NR))
                                s.activation(srow2[:, n % NR, :], ps[2 + n % 2][0:RD, :], ACT.Copy).then_inc(o_ready, 1)

                        @block.sync
                        def _(sp):
                            for n in range(1 + NB):
                                sp.wait_ge(o_ready, n + 1)
                                dst = O["new_rwkv_prompt"][0, 0] if n == 0 else O["new_rwkv_sample"][0, n - 1]
                                load(sp, dst.rearrange("h v k -> v h k"), srow2[:, n % NR, :].rearrange("v (h k) -> v h k", h=RH), row_out[n % NR])
                            for n in range(NR):
                                sp.wait_ge(row_out[n].sem, row_out[n].n)

                with ExitStack() as st:
                    y = mixT[:, 4:8, :]
                    yc = sbuf(st, "yc", [P, 4, TOK])
                    sq = sbuf(st, "ysq", [P, 4, TOK])
                    m_full, q_ready, v_full, v_ready, w_ready = (sem(x) for x in ("mean_full", "ysq_ready", "var_full", "var_ready", "yrstd_ready"))
                    with nc.Block() as block:
                        @block.tensor
                        def _(t):
                            for c in range(4):
                                mm = t.matmul(ps[c][:, 0:TOK], C("head_ones"), y[:, c, :], start=True, stop=True)
                                mm.then_inc(m_full, 1)
                            for c in range(4):
                                t.wait_ge(q_ready, c + 1)
                                t.matmul(ps[4 + c][:, 0:TOK], C("head_ones"), sq[:, c, :], start=True, stop=True).then_inc(v_full, 1)

                        @block.vector
                        def _(v):
                            for c in range(4):
                                v.wait_ge(m_full, c + 1)
                                dv(v, v.scalar_tensor_tensor(out=yc[:, c, :], in0=ps[c][:, 0:TOK], scalar=-1.0 / RD, in1=y[:, c, :], op0=ALU.mult, op1=ALU.add))
                                v.tensor_tensor(sq[:, c, :], yc[:, c, :], yc[:, c, :], ALU.mult).then_inc(q_ready, 1)
                            for c in range(4):
                                v.wait_ge(v_full, c + 1)
                                v.tensor_scalar(sq[:, c, :], ps[4 + c][:, 0:TOK], 1.0 / RD, LN_EPS, ALU.mult, ALU.add).then_inc(v_ready, 1)
                            for c in range(4):
                                v.wait_ge(w_ready, c + 1)
                                dv(v, v.reciprocal(sq[:, c, :], sq[:, c, :]))
                                dv(v, v.tensor_tensor(yc[:, c, :], yc[:, c, :], sq[:, c, :], ALU.mult))
                                dv(v, v.tensor_scalar(yc[:, c, :], yc[:, c, :], V("rwkv_ln_g", c), V("rwkv_ln_b", c), ALU.mult, ALU.add))
                                dv(v, v.tensor_tensor(yc[:, c, :], yc[:, c, :], bonus[:, c, :], ALU.add))
                                dv(v, v.tensor_tensor(y[:, c, :], yc[:, c, :], gT[:, c, :], ALU.mult))

                        @block.scalar
                        def _(s):
                            for c in range(4):
                                s.wait_ge(v_ready, c + 1)
                                s.activation(sq[:, c, :], sq[:, c, :], ACT.Sqrt).then_inc(w_ready, 1)

        def out_projection(name, w_dram):
            with ExitStack() as st:
                w = sbuf(st, name + "_w", [P, DC, D])
                w_in = [sem(f"{name}_w{g}") for g in range(2)]
                full = sem(name + "_full")
                with nc.Block() as block:
                    @block.sync
                    def _(sp):
                        src = w_dram.rearrange("(c p) n -> p c n", p=P)
                        for g in range(2):
                            sp.dma_start(w[:, :, g * 512:(g + 1) * 512], src[:, :, g * 512:(g + 1) * 512]).then_inc(w_in[g], 16)

                    @block.tensor
                    def _(t):
                        for m in range(DC):
                            if m % 4 == 0:
                                t.wait_ge(w_in[m // 4], 16)
                            for k in range(DC):
                                mm = t.matmul(ps[m][:, 0:TOK], w[:, k, m * P:(m + 1) * P], mixT[:, k, :], start=(k == 0), stop=(k == DC - 1))
                            mm.then_inc(full, 1)

                    @block.vector
                    def _(v):
                        for m in range(DC):
                            v.wait_ge(full, m + 1)
                            last = v.tensor_tensor(xT[:, m, :], xT[:, m, :], ps[m][:, 0:TOK], ALU.add)
                        dv(v, last)

        next_part()
        out_projection("out_even", A["w_out_even"][0])

        SLOT = 4096
        NS = 7
        with ExitStack() as st:
            ring = sbuf(st, "ring", [P, NS, SLOT])
            sq = sbuf(st, "sq", [P, DC, TOK])
            FC = DFF // P
            hid = sbuf(st, "hid", [P, FC, TOK])
            sil = sbuf(st, "sil", [P, 2, TOK])
            n_dve, n_pe, n_act = rms_steps("ffn", xT[:, :, :], DC, V("norm_ffn_even", 0, 8), hT, D, scratch=sq)
            landed = [sem(f"ffn_landed{n}") for n in range(NS)]
            h_ready, gu_full, sil_ready, hid_ready, dn_full = (sem(x) for x in ("ffn_h", "gu_full", "sil_ready", "hid_ready", "down_full"))
            GU = DFF // 256
            DN = -(-FC // 4)
            with nc.Block() as block:
                @block.sync
                def _(sp):
                    gu = A["ffn_w_gu_even"][0].rearrange("(c p) (a n) -> p c a n", p=P, a=2)
                    dn = A["ffn_w_down_even"][0].rearrange("(c p) n -> p c n", p=P)
                    for g in range(GU + DN):
                        if g >= NS:
                            sp.wait_ge(gu_full, 2 * (g - NS + 1))
                        if g < GU:
                            for a in range(2):
                                sp.dma_start(ring[:, g % NS, :].rearrange("p (c a n) -> p c a n", c=DC, a=2)[:, :, a, :],
                                             gu[:, :, a, g * 256:(g + 1) * 256]).then_inc(landed[g % NS], 16)
                        else:
                            k = 4 * (g - GU)
                            m = min(4, FC - k)
                            sp.dma_start(ring[:, g % NS, 0:m * D].rearrange("p (c n) -> p c n", c=m), dn[:, k:k + m, :]).then_inc(landed[g % NS], 16)


                @block.tensor
                def _(t):
                    n_pe(t)
                    t.wait_ge(h_ready, 1)
                    amount = [0] * NS

                    def wait_slot(g):
                        amount[g % NS] += 32 if g < GU else 16
                        t.wait_ge(landed[g % NS], amount[g % NS])
                    for g in range(GU):
                        wait_slot(g)
                        w = ring[:, g % NS, :].rearrange("p (c a n) -> p c a n", c=DC, a=2)
                        for j in range(2):
                            n = 2 * g + j
                            if n >= 3:
                                t.wait_ge(hid_ready, n - 2)
                            for a in range(2):
                                for k in range(DC):
                                    mm = t.matmul(ps[2 * (n % 3) + a][:, 0:TOK], w[:, k, a, j * P:(j + 1) * P], hT[:, k, :], start=(k == 0), stop=(k == DC - 1))
                            mm.then_inc(gu_full, 1)
                    t.wait_ge(hid_ready, FC)
                    for g in range(GU, GU + DN):
                        wait_slot(g)
                        for q in range(min(4, FC - 4 * (g - GU))):
                            k = 4 * (g - GU) + q
                            for m in range(DC):
                                mm = t.matmul(ps[m][:, 0:TOK], ring[:, g % NS, q * D + m * P:q * D + (m + 1) * P], hid[:, k, :], start=(k == 0), stop=(k == FC - 1))
                                if k == FC - 1:
                                    mm.then_inc(dn_full, 1)

                @block.scalar
                def _(s):
                    n_act(s)
                    for n in range(FC):
                        s.wait_ge(gu_full, n + 1)
                        if n >= 2:
                            s.wait_ge(hid_ready, n - 1)
                        s.activation(sil[:, n % 2, :], ps[2 * (n % 3)][:, 0:TOK], ACT.Silu).then_inc(sil_ready, 1)

                @block.vector
                def _(v):
                    n_dve(v)
                    v.sem_inc(h_ready, 1)
                    for n in range(FC):
                        v.wait_ge(sil_ready, n + 1)
                        v.tensor_tensor(hid[:, n, :], sil[:, n % 2, :], ps[2 * (n % 3) + 1][:, 0:TOK], ALU.mult).then_inc(hid_ready, 1)
                    for m in range(DC):
                        v.wait_ge(dn_full, m + 1)
                        last = v.tensor_tensor(xT[:, m, :], xT[:, m, :], ps[m][:, 0:TOK], ALU.add)
                    dv(v, last)

        with ExitStack() as od:
            qT = sbuf(od, "qT", [P, GH, TOK])
            kT = sbuf(od, "kT", [P, GH, TOK])
            gS = sbuf(od, "gS", [P, DC, TOK])
            xaT = sbuf(od, "xaT", [GRANK, TOK])
            rowV = sbuf(od, "rowV", [P, 3, GV])
            with ExitStack() as st:
                win = sbuf(st, "win_odd", [P, DC, ODD_IN])
                sq = sbuf(st, "sq", [P, DC, TOK])
                cuts = [0, GK, 2 * GK, 2 * GK + GV, ODD_IN]
                win_in = [sem("wodd_in") for _ in range(4)]
                n_dve, n_pe, n_act = rms_steps("oddn", xT[:, :, :], DC, V("norm_mix_odd", 0, 8), hT, D, scratch=sq)
                h_ready, v_full, v_taken = sem("odd_h"), sem("v_full"), sem("v_taken")
                cols = [(k * P, P) for k in range(8)] + [(2 * GK + GV + k * P, P) for k in range(8)] + [(ODD_IN - GRANK, GRANK)]
                dest = [qT[:, k, :] for k in range(4)] + [kT[:, k, :] for k in range(4)] + [gS[:, k, :] for k in range(8)] + [xaT[:, :]]
                lin = Linear("podd", 17, [0, 1, 2, 3])
                with nc.Block() as block:
                    @block.sync
                    def _(sp):
                        w = A["w_in_odd"][0].rearrange("(c p) n -> p c n", p=P)
                        for g in (0, 1, 3, 2):
                            sp.dma_start(win[:, :, cuts[g]:cuts[g + 1]], w[:, :, cuts[g]:cuts[g + 1]]).then_inc(win_in[g], 16)


                    @block.vector
                    def _(v):
                        n_dve(v)
                        v.sem_inc(h_ready, 1)
                        lin.run_dve(v, lambda t: (v.tensor_copy(dest[t], lin.out(t, cols[t][1])) if t < 8 else
                                                  v.tensor_copy(dest[t], lin.out(t, cols[t][1]))))
                        for n in range(1, 6, 2):
                            v.wait_ge(v_full, n + 1)
                            r = TILES[n // 2][1]
                            last = v.tensor_copy(rowV[0:r, n // 2, 512:1024], ps[4 + n % 2][0:r, :])
                            last.then_inc(v_taken, 1)

                    @block.scalar
                    def _(s):
                        n_act(s)
                        lin.run_act(s, lambda t: s.activation(dest[t], lin.out(t, cols[t][1]), ACT.Copy))
                        for n in range(0, 6, 2):
                            s.wait_ge(v_full, n + 1)
                            r = TILES[n // 2][1]
                            s.activation(rowV[0:r, n // 2, 0:512], ps[4 + n % 2][0:r, :], ACT.Copy).then_inc(v_taken, 1)

                    @block.tensor
                    def _(t):
                        n_pe(t)
                        t.wait_ge(h_ready, 1)

                        def wready(i):
                            if i in (0, 4, 8):
                                t.wait_ge(win_in[{0: 0, 4: 1, 8: 3}[i]], 16)
                        lin.pe(t, lambda i, k: win[:, k, cols[i][0]:cols[i][0] + cols[i][1]], DC, lambda k: hT[:, k, :], wready)
                        t.wait_ge(win_in[2], 16)
                        for n in range(6):
                            lo, r = TILES[n // 2]
                            if n >= 2:
                                t.wait_ge(v_taken, 2 * (n // 2))
                            for k in range(DC):
                                mm = t.matmul(ps[4 + n % 2][0:r, :], hT[:, k, lo:lo + r], win[:, k, 2 * GK + (n % 2) * 512:2 * GK + (n % 2 + 1) * 512],
                                              start=(k == 0), stop=(k == DC - 1))
                            mm.then_inc(v_full, 1)

            with ExitStack() as st:
                AT = sbuf(st, "AT", [P, 3, GH, P])
                qb = sbuf(st, "qb", [P, GH, TOK])
                rowE = sbuf(st, "rowE", [P, 3, GK])
                bend = sbuf(st, "bend", [P, GH, SEQ // GC])
                bends = sbuf(st, "bends", [P, GH, NB])
                Ss = sbuf(st, "Ss", [P, NB, GH, DV])
                ss_in = Signal(sem("ss_in"))
                oT = mixT
                with ExitStack() as s2:
                    ga2 = sbuf(s2, "ga2", [GRANK, GK])
                    t1, t2, t3, t4 = (sbuf(s2, f"g{n}", [P, GH, TOK]) for n in range(4))
                    ga_in, z_full, ab_ready, ln_ready, ex_in, ex_out, mm_ready, at_full, at_free, row_full, row_free, o_full, o_free, sg_ready = (sem(x) for x in (
                        "ga_in", "z_full", "absz_ready", "ln_ready", "gexp_in", "gexp_out", "gops_ready", "at_full", "at_free",
                        "grow_full", "grow_free", "o_full", "o_free", "silu_ready"))
                    with nc.Block() as block:
                        @block.sync
                        def _(sp):
                            sp.dma_start(ga2[:, :], A["gla_a2"][0]).then_inc(ga_in, 16)
                            for b in range(NB):
                                load(sp, Ss[:, b, :, :], A["state_gla"][0, b].rearrange("h k v -> k h v"), ss_in)

                        @block.vector
                        def _(v):
                            v.wait_ge(z_full, 1)
                            for c in range(GH):
                                last = v.tensor_scalar(t1[:, c, :], ps[c][:, 0:TOK], V("gla_ab", c), None, ALU.add)
                            dv(v, last)
                            dv(v, v.scalar_tensor_tensor(out=t2[:, :, :], in0=t1[:, :, :], scalar=-1.0, in1=t1[:, :, :], op0=ALU.mult, op1=ALU.max))
                            v.sem_inc(ab_ready, 1)
                            v.wait_ge(ln_ready, 1)
                            dv(v, v.scalar_tensor_tensor(out=t1[:, :, :], in0=t1[:, :, :], scalar=0.0, in1=t2[:, :, :], op0=ALU.min, op1=ALU.subtract))
                            for c in range(GH):
                                last = v.tensor_tensor_scan(t2[:, c, :], C("reset_gla"), t1[:, c, :], 0.0, ALU.mult, ALU.add)
                            dv(v, last)
                            b32 = t2[:, :, :].rearrange("p h (c t) -> p (h c) t", t=GC)
                            dv(v, v.tensor_tensor(t3[:, :, :].rearrange("p h (c t) -> p (h c) t", t=GC), b32,
                                                  b32[:, :, GC // 2 - 1:GC // 2].to_broadcast([P, GH * TOK // GC, GC]), ALU.subtract))
                            dv(v, v.tensor_scalar(t3[:, :, :], t3[:, :, :], 80.0 * 16, -80.0 * 16, ALU.min, ALU.max))
                            for h in range(GH):
                                bp = t2[:, h, 0:SEQ].rearrange("p (c t) -> p c t", t=GC)
                                v.tensor_tensor(t4[:, h, 0:SEQ].rearrange("p (c t) -> p c t", t=GC), bp[:, :, GC - 1:GC].to_broadcast([P, SEQ // GC, GC]), bp, ALU.subtract)
                                bs = t2[:, h, SEQ:TOK].rearrange("p (c t) -> p c t", t=DS)
                                last = v.tensor_tensor(t4[:, h, SEQ:TOK].rearrange("p (c t) -> p c t", t=DS), bs[:, :, DS - 1:DS].to_broadcast([P, NB, DS]), bs, ALU.subtract)
                            dv(v, last)
                            v.sem_inc(ex_in, 1)
                            v.wait_ge(ex_out, 1)
                            dv(v, v.scalar_tensor_tensor(out=t1[:, :, :], in0=qT[:, :, :], scalar=float(DK ** -0.5), in1=t1[:, :, :], op0=ALU.mult, op1=ALU.mult))
                            v.wait_ge(ex_out, 2)
                            dv(v, v.tensor_tensor(t3[:, :, :], kT[:, :, :], t3[:, :, :], ALU.mult))
                            v.sem_inc(mm_ready, 1)
                            v.wait_ge(ex_out, 3)
                            dv(v, v.tensor_tensor(t4[:, :, :], kT[:, :, :], t4[:, :, :], ALU.mult))
                            v.sem_inc(mm_ready, 1)
                            v.wait_ge(ex_out, 4)
                            v.tensor_copy(bend[:, :, :], t2[:, :, GC - 1:SEQ:GC])
                            v.tensor_copy(bends[:, :, :], t2[:, :, SEQ + DS - 1:TOK:DS])
                            dv(v, v.scalar_tensor_tensor(out=qb[:, :, :], in0=qT[:, :, :], scalar=float(DK ** -0.5), in1=t2[:, :, :], op0=ALU.mult, op1=ALU.mult))
                            for i, (lo, r) in enumerate(TILES):
                                v.wait_ge(at_full, i + 1)
                                m = C("gla_T", r, 0, r) if i < 2 else C("sm_T", r, P, P + r)
                                v.tensor_tensor(AT[0:r, i, :, 0:r], ps[4 + i % 2][0:r, :].rearrange("p (h t) -> p h t", h=GH)[:, :, 0:r],
                                                m.rearrange("p (o t) -> p o t", o=1).to_broadcast([r, GH, r]), ALU.mult).then_inc(at_free, 1)
                            for n in range(DC):
                                v.wait_ge(o_full, n + 1)
                                v.tensor_copy(oT[:, n, :], ps[n % 4][:, 0:TOK]).then_inc(o_free, 1)

                        @block.scalar
                        def _(s):
                            s.wait_ge(ab_ready, 1)
                            ac(s, s.activation(t2[:, :, :], t2[:, :, :], ACT.Exp, scale=-1.0))
                            ac(s, s.activation(t2[:, :, :], t2[:, :, :], ACT.Ln, bias=C("ones")[:, 0:1]))
                            s.sem_inc(ln_ready, 1)
                            s.wait_ge(ex_in, 1)
                            s.activation(t1[:, :, :], t3[:, :, :], ACT.Exp, scale=1.0 / 16).then_inc(ex_out, 1)
                            ac(s, s.activation(t3[:, :, :], t3[:, :, :], ACT.Exp, scale=-1.0 / 16))
                            s.sem_inc(ex_out, 1)
                            s.activation(t4[:, :, :], t4[:, :, :], ACT.Exp, scale=1.0 / 16).then_inc(ex_out, 1)
                            s.activation(t2[:, :, :], t2[:, :, :], ACT.Exp, scale=1.0 / 16).then_inc(ex_out, 1)
                            for i, (lo, r) in enumerate(TILES):
                                s.wait_ge(row_full, i + 1)
                                s.activation(rowE[0:r, i, :], ps[6 + i % 2][0:r, :], ACT.Copy).then_inc(row_free, 1)
                            ac(s, s.activation(gS[:, :, :], gS[:, :, :], ACT.Silu))

                        @block.tensor
                        def _(t):
                            t.wait_ge(ga_in, 16)
                            for c in range(GH):
                                mm = t.matmul(ps[c][:, 0:TOK], ga2[:, c * P:(c + 1) * P], xaT[:, :], start=True, stop=True)
                            mm.then_inc(z_full, 1)
                            t.wait_ge(mm_ready, 1)
                            for i, (lo, r) in enumerate(TILES):
                                if i >= 2:
                                    t.wait_ge(at_free, i - 1)
                                for h in range(GH):
                                    mm = t.matmul(ps[4 + i % 2][0:r, h * P:h * P + r], t3[:, h, lo:lo + r], t1[:, h, lo:lo + r], start=True, stop=True)
                                mm.then_inc(at_full, 1)
                            t.wait_ge(mm_ready, 2)
                            for i, (lo, r) in enumerate(TILES):
                                if i >= 2:
                                    t.wait_ge(row_free, i - 1)
                                for h in range(GH):
                                    mm = t.transpose(ps[6 + i % 2][0:r, h * P:(h + 1) * P], t4[:, h, lo:lo + r], C("ident"))
                                mm.then_inc(row_full, 1)
                            t.wait_ge(at_free, 3)
                            for n in range(DC):
                                if n >= 4:
                                    t.wait_ge(o_free, n - 3)
                                for i, (lo, r) in enumerate(TILES):
                                    mm = t.matmul(ps[n % 4][:, lo:lo + r], rowV[0:r, i, n * P:(n + 1) * P], AT[0:r, i, n // 2, 0:r], start=True, stop=True)
                                mm.then_inc(o_full, 1)

                S = sbuf(st, "S", [P, 2, GH, DV])
                vb = sbuf(st, "vb", [64, 2, 2, 512])
                in_full, in_free, up_full, up_ready, so_full, vb_ready, sn_full, sn_ready, s0_ready, so_taken = (sem(x) for x in (
                    "inter_full", "inter_free", "update_full", "update_ready", "sample_inter", "vblk_ready", "snew_full", "snew_ready", "gs0", "sample_taken"))
                NG = SEQ // GC
                with nc.Block() as block:
                    @block.tensor
                    def _(t):
                        t.wait_ge(s0_ready, 1)
                        for c in range(NG):
                            i, js = c // 4, slice(GC * (c % 4), GC * (c % 4) + GC)
                            if c:
                                t.wait_ge(up_ready, c)
                            for h in range(GH):
                                mm = t.matmul(ps[h // 2][:, (h % 2) * DV:(h % 2 + 1) * DV], rowE[js, i, h * DK:(h + 1) * DK],
                                              rowV[js, i, h * DV:(h + 1) * DV], start=True, stop=True, tile_position=(GC * (c % 4), 0))
                            mm.then_inc(up_full, 1)
                            if c >= 2:
                                t.wait_ge(in_free, c - 1)
                            for n in range(DC):
                                mm = t.matmul(ps[2 + c % 2][:, n * GC:(n + 1) * GC], S[:, c % 2, n // 2, (n % 2) * P:(n % 2 + 1) * P],
                                              qb[:, n // 2, c * GC:(c + 1) * GC], start=True, stop=True)
                            mm.then_inc(in_full, 1)
                        t.wait_ge(ss_in.sem, 16 * NB)
                        for n in range(DC):
                            for b in range(NB):
                                mm = t.matmul(ps[4][:, n * 64 + b * DS:n * 64 + (b + 1) * DS], Ss[:, b, n // 2, (n % 2) * P:(n % 2 + 1) * P],
                                              qb[:, n // 2, SEQ + b * DS:SEQ + (b + 1) * DS], start=True, stop=True)
                        mm.then_inc(so_full, 1)
                        t.wait_ge(so_taken, 1)
                        for n in range(16):
                            t.wait_ge(vb_ready, n + 1)
                            if n >= 2:
                                t.wait_ge(sn_ready, n - 1)
                            t.matmul(ps[5 + n % 2][:, :], rowE[0:64, 2, (n // 4) * DK:(n // 4 + 1) * DK], vb[:, n % 2, 0, :], start=True, stop=True).then_inc(sn_full, 1)

                    @block.vector
                    def _(v):
                        dv(v, v.memset(S[:, 0, :, :], 0.0))
                        v.sem_inc(s0_ready, 1)
                        for c in range(NG):
                            v.wait_ge(up_full, c + 1)
                            if c:
                                v.wait_ge(in_full, c)
                            for h in range(GH):
                                last = v.scalar_tensor_tensor(out=S[:, (c + 1) % 2, h, :], in0=S[:, c % 2, h, :], scalar=bend[:, h, c:c + 1],
                                                              in1=ps[h // 2][:, (h % 2) * DV:(h % 2 + 1) * DV], op0=ALU.mult, op1=ALU.add)
                            dv(v, last)
                            v.sem_inc(up_ready, 1)
                            v.wait_ge(in_full, c + 1)
                            v.tensor_tensor(oT[:, :, c * GC:(c + 1) * GC], oT[:, :, c * GC:(c + 1) * GC],
                                            ps[2 + c % 2][:, 0:256].rearrange("p (n t) -> p n t", n=DC), ALU.add).then_inc(in_free, 1)
                        v.wait_ge(so_full, 1)
                        v.tensor_tensor(oT[:, :, SEQ:TOK], oT[:, :, SEQ:TOK], ps[4][:, :].rearrange("p (n t) -> p n t", n=DC), ALU.add).then_inc(so_taken, 1)
                        v.wait_ge(ss_in.sem, 16 * NB)
                        for n in range(16 + 1):
                            if n < 16:
                                h, b = n // 4, 2 * (n % 4)
                                if n >= 2:
                                    v.wait_ge(sn_full, n - 1)
                                for x in range(2):
                                    last = v.tensor_scalar(vb[:, n % 2, 0, x * DV:(x + 1) * DV], rowV[0:64, 2, h * DV:(h + 1) * DV],
                                                           C("bsel", 64, b + x, b + x + 1), None, ALU.mult)
                                last.then_inc(vb_ready, 1)
                            if n:
                                m = n - 1
                                h, b = m // 4, 2 * (m % 4)
                                v.wait_ge(sn_full, m + 1)
                                for x in range(2):
                                    last = v.scalar_tensor_tensor(out=Ss[:, b + x, h, :], in0=Ss[:, b + x, h, :], scalar=bends[:, h, b + x:b + x + 1],
                                                                  in1=ps[5 + m % 2][:, x * DV:(x + 1) * DV], op0=ALU.mult, op1=ALU.add)
                                last.then_inc(sn_ready, 1)

                    @block.sync
                    def _(sp):
                        sp.wait_ge(up_ready, NG)
                        store(sp, O["new_gla_prompt"][0, 0].rearrange("h k v -> k h v"), S[:, NG % 2, :, :])
                        sp.wait_ge(sn_ready, 16)
                        for b in range(NB):
                            store(sp, O["new_gla_sample"][0, b].rearrange("h k v -> k h v"), Ss[:, b, :, :])
                        sp.wait_ge(stored.sem, stored.n)

            with ExitStack() as st:
                sq = sbuf(st, "osq", [P, DC, TOK])
                rs = sbuf(st, "ors", [P, GH, TOK])
                q_ready, f, v_ready, w_ready = (sem(x) for x in ("osq_ready", "osum_full", "ovar_ready", "orstd_ready"))
                with nc.Block() as block:
                    @block.vector
                    def _(v):
                        dv(v, v.tensor_tensor(sq[:, :, :], mixT[:, :, :], mixT[:, :, :], ALU.mult))
                        v.sem_inc(q_ready, 1)
                        for h in range(GH):
                            v.wait_ge(f, h + 1)
                            v.tensor_scalar(rs[:, h, :], ps[h][:, 0:TOK], 1.0 / DV, EPS, ALU.mult, ALU.add).then_inc(v_ready, 1)
                        for n in range(DC):
                            if n % 2 == 0:
                                v.wait_ge(w_ready, n // 2 + 1)
                                dv(v, v.reciprocal(rs[:, n // 2, :], rs[:, n // 2, :]))
                            dv(v, v.scalar_tensor_tensor(out=mixT[:, n, :], in0=mixT[:, n, :], scalar=V("gla_norm", n), in1=rs[:, n // 2, :], op0=ALU.mult, op1=ALU.mult))
                            dv(v, v.tensor_tensor(mixT[:, n, :], mixT[:, n, :], gS[:, n, :], ALU.mult))

                    @block.tensor
                    def _(t):
                        t.wait_ge(q_ready, 1)
                        for h in range(GH):
                            for q in range(2):
                                mm = t.matmul(ps[h][:, 0:TOK], C("ones"), sq[:, 2 * h + q, :], start=(q == 0), stop=(q == 1))
                            mm.then_inc(f, 1)

                    @block.scalar
                    def _(s):
                        for h in range(GH):
                            s.wait_ge(v_ready, h + 1)
                            s.activation(rs[:, h, :], rs[:, h, :], ACT.Sqrt).then_inc(w_ready, 1)

        next_part()
        out_projection("out_odd", A["w_out_odd"][0])

        with ExitStack() as mo:
            rowH = sbuf(mo, "rowH", [P, 3, D])
            slotno = sbuf(mo, "slotno", [P, 3, MAXJOB])
            gate = sbuf(mo, "gate", [P, 3, MAXJOB])
            jobs = sbuf(mo, "jobs", [1, MAXJOB], I32)
            njobs = sbuf(mo, "njobs", [1, 8], I32)
            with ExitStack() as st:
                sq = sbuf(st, "sq", [P, DC, TOK])
                wr = sbuf(st, "router", [P, DC, NE])
                lg = sbuf(st, "logits", [P, 3, NE])
                cmp = sbuf(st, "cmp", [P, NE, NE])
                eq = sbuf(st, "eq", [P, NE, NE])
                rank = sbuf(st, "rank", [P, 3, NE])
                mask = sbuf(st, "mask", [P, 3, NE])
                gt = sbuf(st, "gt", [P, 3, NE])
                top = sbuf(st, "top", [P, 3, 8])
                slot = sbuf(st, "slot", [P, 3, NE])
                cnt = sbuf(st, "cnt", [P, NE])
                over = sbuf(st, "over", [P, 16])
                order = sbuf(st, "order", [P, 16])
                OH = sbuf(st, "OH", [P, 8, 16])
                tmp = sbuf(st, "tmp", [P, 8, 16])
                s16 = sbuf(st, "s16", [P, 16])
                g16 = sbuf(st, "g16", [P, 16])
                red = sbuf(st, "red", [P, 8])
                hit = sbuf(st, "hit", [P, 8])
                wr_in = Signal(sem("router_in"))
                n_dve, n_pe, n_act = rms_steps("moen", xT[:, :, :], DC, V("norm_ffn_odd", 0, 8), hT, D, scratch=sq)
                h_ready, lg_full, ex_in, ex_out, mk_ready, sl_full, rh_full, rh_act, rh_dve = (sem(x) for x in (
                    "moe_h", "logits_full", "gate_exp_in", "gate_exp_out", "mask_ready", "slots_full", "rowh_full", "rowh_act", "rowh_dve"))
                with nc.Block() as block:
                    @block.sync
                    def _(sp):
                        load(sp, wr[:, :, :], A["moe_router"][0].rearrange("(c p) e -> p c e", p=P), wr_in)


                    @block.tensor
                    def _(t):
                        n_pe(t)
                        t.wait_ge(h_ready, 1)
                        t.wait_ge(wr_in.sem, 16)
                        for i, (lo, r) in enumerate(TILES):
                            for k in range(DC):
                                mm = t.matmul(ps[0][0:r, i * NE:(i + 1) * NE], hT[:, k, lo:lo + r], wr[:, k, :], start=(k == 0), stop=(k == DC - 1))
                        mm.then_inc(lg_full, 1)
                        for n in range(6):
                            lo, r = TILES[n // 2]
                            if n >= 4:
                                t.wait_ge(rh_act if n % 2 == 0 else rh_dve, (n - 4) // 2 + 1)
                            for q in range(4):
                                mm = t.transpose(ps[2 + n % 4][0:r, q * P:(q + 1) * P], hT[:, 4 * (n % 2) + q, lo:lo + r], C("ident"))
                            mm.then_inc(rh_full, 1)
                        t.wait_ge(mk_ready, 1)
                        for i, (lo, r) in enumerate(TILES):
                            for k in range(i + 1):
                                rk_ = TILES[k][1]
                                lhs = C("before", r, 0, r) if k == i else C("ones", rk_, 0, r)
                                t.matmul(ps[1][0:r, i * NE:(i + 1) * NE], lhs, mask[0:rk_, k, :], start=(k == 0), stop=(k == i))
                        for k in range(3):
                            rk_ = TILES[k][1]
                            mm = t.matmul(ps[1][:, 3 * NE:4 * NE], C("ones", rk_), mask[0:rk_, k, :], start=(k == 0), stop=(k == 2))
                        mm.then_inc(sl_full, 1)

                    @block.scalar
                    def _(s):
                        n_act(s)
                        for n in range(0, 6, 2):
                            s.wait_ge(rh_full, n + 1)
                            r = TILES[n // 2][1]
                            s.activation(rowH[0:r, n // 2, 0:512], ps[2 + n % 4][0:r, :], ACT.Copy).then_inc(rh_act, 1)
                        s.wait_ge(ex_in, 1)
                        for i, (lo, r) in enumerate(TILES):
                            s.activation(gt[0:r, i, :], gt[0:r, i, :], ACT.Exp)
                            ins = s.activation(top[0:r, i, 1:2], top[0:r, i, 1:2], ACT.Exp)
                        ac(s, ins)
                        s.sem_inc(ex_out, 1)

                    @block.vector
                    def _(v):
                        n_dve(v)
                        v.sem_inc(h_ready, 1)
                        v.wait_ge(lg_full, 1)
                        for i, (lo, r) in enumerate(TILES):
                            last = v.tensor_copy(lg[0:r, i, :], ps[0][0:r, i * NE:(i + 1) * NE])
                        dv(v, last)
                        for i, (lo, r) in enumerate(TILES):
                            L = lg[0:r, i, :]
                            le = L.rearrange("p (e o) -> p e o", o=1).to_broadcast([r, NE, NE])
                            lo_ = L.rearrange("p (o f) -> p o f", o=1).to_broadcast([r, NE, NE])
                            v.max(top[0:r, i, :], L)
                            v.tensor_tensor(cmp[0:r, :, :], lo_, le, ALU.is_gt)
                            dv(v, v.tensor_tensor(eq[0:r, :, :], lo_, le, ALU.is_equal))
                            dv(v, v.tensor_tensor(eq[0:r, :, :], eq[0:r, :, :], C("tie", r).rearrange("p (e f) -> p e f", e=NE), ALU.mult))
                            dv(v, v.tensor_tensor(cmp[0:r, :, :], cmp[0:r, :, :], eq[0:r, :, :], ALU.add))
                            dv(v, v.tensor_reduce(rank[0:r, i, :], cmp[0:r, :, :], AX_X, ALU.add))
                            v.tensor_scalar(mask[0:r, i, :], rank[0:r, i, :], 1.5, None, ALU.is_lt)
                            v.tensor_scalar(gt[0:r, i, :], L, top[0:r, i, 0:1], None, ALU.subtract)
                            dv(v, v.tensor_scalar(top[0:r, i, 1:2], top[0:r, i, 1:2], top[0:r, i, 0:1], None, ALU.subtract))
                        v.sem_inc(mk_ready, 1)
                        v.sem_inc(ex_in, 1)
                        for n in range(1, 6, 2):
                            v.wait_ge(rh_full, n + 1)
                            r = TILES[n // 2][1]
                            v.tensor_copy(rowH[0:r, n // 2, 512:1024], ps[2 + n % 4][0:r, :]).then_inc(rh_dve, 1)
                        v.wait_ge(ex_out, 1)
                        for i, (lo, r) in enumerate(TILES):
                            dv(v, v.tensor_scalar(top[0:r, i, 1:2], top[0:r, i, 1:2], 1.0, None, ALU.add))
                            dv(v, v.reciprocal(top[0:r, i, 2:3], top[0:r, i, 1:2]))
                            dv(v, v.scalar_tensor_tensor(out=gt[0:r, i, :], in0=gt[0:r, i, :], scalar=top[0:r, i, 2:3], in1=mask[0:r, i, :], op0=ALU.mult, op1=ALU.mult))
                        v.wait_ge(sl_full, 1)
                        dv(v, v.tensor_copy(cnt[:, :], ps[1][:, 3 * NE:4 * NE]))
                        for i, (lo, r) in enumerate(TILES):
                            dv(v, v.tensor_scalar(slot[0:r, i, :], ps[1][0:r, i * NE:(i + 1) * NE], FAR, None, ALU.subtract))
                            dv(v, v.tensor_tensor(slot[0:r, i, :], slot[0:r, i, :], mask[0:r, i, :], ALU.mult))
                            dv(v, v.tensor_scalar(slot[0:r, i, :], slot[0:r, i, :], FAR, None, ALU.add))
                        for q in range(2):
                            last = v.tensor_tensor(over[:, q * NE:(q + 1) * NE], cnt[:, :], C("part")[:, q * NE:(q + 1) * NE], ALU.is_gt)
                        dv(v, last)
                        dv(v, v.tensor_tensor_scan(order[:, :], C("ones", P, 0, 16), over[:, :], 0.0, ALU.mult, ALU.add))
                        dv(v, v.tensor_scalar(njobs[0:1, 0:1], order[0:1, 15:16], float(NE), None, ALU.add))
                        dv(v, v.tensor_tensor(order[:, :], order[:, :], over[:, :], ALU.mult))
                        dv(v, v.tensor_scalar(order[:, :], order[:, :], 1.0, None, ALU.subtract))
                        dv(v, v.tensor_tensor(OH[:, :, :], order[:, :].rearrange("p (o c) -> p o c", o=1).to_broadcast([P, 8, 16]),
                                              C("jobno").rearrange("p (j c) -> p j c", j=8), ALU.is_equal))
                        dv(v, v.tensor_tensor(tmp[:, :, :], OH[:, :, :], C("expert").rearrange("p (o c) -> p o c", o=1).to_broadcast([P, 8, 16]), ALU.mult))
                        dv(v, v.tensor_reduce(red[:, :], tmp[:, :, :], AX_X, ALU.add))
                        v.tensor_copy(jobs[0:1, 8:16], red[0:1, :])
                        v.tensor_copy(jobs[0:1, 0:8], C("expert", 1, 0, 8))
                        dv(v, v.tensor_reduce(hit[:, :], OH[:, :, :], AX_X, ALU.add))
                        for i, (lo, r) in enumerate(TILES):
                            v.tensor_copy(slotno[0:r, i, 0:NE], slot[0:r, i, :])
                            v.tensor_copy(gate[0:r, i, 0:NE], gt[0:r, i, :])
                            for q in range(2):
                                v.tensor_tensor(s16[0:r, q * NE:(q + 1) * NE], slot[0:r, i, :], C("part", r)[:, q * NE:(q + 1) * NE], ALU.subtract)
                                last = v.tensor_copy(g16[0:r, q * NE:(q + 1) * NE], gt[0:r, i, :])
                            dv(v, last)
                            dv(v, v.tensor_scalar(s16[0:r, :], s16[0:r, :], FAR, None, ALU.subtract))
                            dv(v, v.tensor_tensor(tmp[0:r, :, :], OH[0:r, :, :], s16[0:r, :].rearrange("p (o c) -> p o c", o=1).to_broadcast([r, 8, 16]), ALU.mult))
                            dv(v, v.tensor_reduce(red[0:r, :], tmp[0:r, :, :], AX_X, ALU.add))
                            dv(v, v.tensor_scalar(slotno[0:r, i, NE:16], red[0:r, :], FAR, None, ALU.add))
                            dv(v, v.tensor_tensor(tmp[0:r, :, :], OH[0:r, :, :], g16[0:r, :].rearrange("p (o c) -> p o c", o=1).to_broadcast([r, 8, 16]), ALU.mult))
                            dv(v, v.tensor_reduce(gate[0:r, i, NE:16], tmp[0:r, :, :], AX_X, ALU.add))

            with ExitStack() as st:
                NSM = 7
                GUP, DNP = DFE // 256, DFE // 512
                PIECES = GUP + DNP
                assert PIECES % NSM == 0
                TURN = PIECES // NSM
                FT = DFE // P
                ring = sbuf(st, "ring", [P, NSM, SLOT])
                sel = sbuf(st, "sel", [P, 3, P])
                selg = sbuf(st, "selg", [P, 3, P])
                selT = sbuf(st, "selT", [P, TOK])
                xg = sbuf(st, "xg", [P, DC, P])
                sil = sbuf(st, "sil", [P, 2, 256])
                hrow = sbuf(st, "hrow", [P, 2, 256])
                hidT = sbuf(st, "hidT", [P, FT, P])
                Y = sbuf(st, "Y", [P, D])
                landed = [sem(f"landed{n}") for n in range(NSM)]
                used = [sem(f"slot_used{n}") for n in range(NSM)]
                (sel_ready, selg_ready, xg_full, xg_ready, st_full, st_ready, sil_ready, h_ready, ht_full, ht_ready,
                 dn_full, y_ready, yo_full, yo_added) = (sem(x) for x in (
                     "sel_ready", "selg_ready", "gathered", "xg_ready", "sel_turned", "selT_ready", "silu_ready", "hidden_ready",
                     "hidden_turned", "hidT_ready", "down_done", "y_ready", "scattered", "y_added"))
                with nc.Block() as block:
                    @block.sync
                    def _(sp):
                        n = sp.value_load(njobs[0:1, 0:1], min_val=NE, max_val=NE + 4)
                        with sp.Fori(0, n) as j:
                            e = sp.value_load(jobs[0:1, bass.ds(j, 1)], min_val=0, max_val=NE - 1)
                            gu = A["moe_w_gu"][0, bass.ds(e, 1)].rearrange("e (c p) (a n) -> p (e c) a n", p=P, a=2)
                            dn = A["moe_w_down"][0, bass.ds(e, 1)].rearrange("e (c p) n -> p (e c) n", p=P)
                            first = sp.snap(TURN * j + 1)
                            for g in range(PIECES):
                                s_ = g % NSM
                                src = None
                                if g < GUP:
                                    for a in range(2):
                                        sp.wait_ge(used[s_], first + g // NSM)
                                        sp.dma_start(ring[:, s_, :].rearrange("p (c a n) -> p c a n", c=DC, a=2)[:, :, a, :],
                                                     gu[:, :, a, g * 256:(g + 1) * 256]).then_inc(landed[s_], 16)
                                else:
                                    q = g - GUP
                                    sp.wait_ge(used[s_], first + g // NSM)
                                    sp.dma_start(ring[:, s_, :].rearrange("p (c n) -> p c n", c=4), dn[:, 4 * q:4 * q + 4, :]).then_inc(landed[s_], 32)

                    @block.tensor
                    def _(t):
                        n = t.value_load(njobs[0:1, 0:1], min_val=NE, max_val=NE + 4)
                        for s_ in range(NSM):
                            t.sem_inc(used[s_], 1)

                        def gather(value):
                            t.wait_ge(sel_ready, value)
                            for c in range(DC):
                                for i, (lo, r) in enumerate(TILES):
                                    mm = t.matmul(ps[6 + c // 4][:, (c % 4) * P:(c % 4 + 1) * P], rowH[0:r, i, c * P:(c + 1) * P], sel[0:r, i, :],
                                                  start=(i == 0), stop=(i == 2))
                                if c % 4 == 3:
                                    mm.then_inc(xg_full, 1)
                        gather(1)
                        with t.Fori(0, n) as j:
                            def turned(p):
                                t.wait_ge(h_ready, GUP * j + (p + 1))
                                if p >= 2:
                                    t.wait_ge(ht_ready, GUP * j + (p - 1))
                                for q in range(2):
                                    mm = t.transpose(ps[2 + p % 2][:, q * P:(q + 1) * P], hrow[:, p % 2, q * P:(q + 1) * P], C("ident"))
                                mm.then_inc(ht_full, 1)
                            t.wait_ge(xg_ready, 2 * j + 2)
                            for g in range(GUP):
                                s_ = g % NSM
                                t.wait_ge(landed[s_], 32 * TURN * j + 32 * (g // NSM + 1))
                                if g >= 2:
                                    t.wait_ge(h_ready, GUP * j + (g - 1))
                                w = ring[:, s_, :].rearrange("p (c n) -> p c n", c=DC)
                                for k in range(DC):
                                    mm = t.matmul(ps[g % 2][:, :], xg[:, k, :], w[:, k, :], start=(k == 0), stop=(k == DC - 1))
                                mm.then_inc(used[s_], 1)
                                if g == 1:
                                    t.wait_ge(selg_ready, j + 1)
                                    for i, (lo, r) in enumerate(TILES):
                                        mm = t.transpose(ps[4][:, lo:lo + r], selg[0:r, i, :], C("ident", r, 0, r))
                                    mm.then_inc(st_full, 1)
                                if g >= 1:
                                    turned(g - 1)
                            turned(GUP - 1)
                            t.wait_ge(st_ready, j + 1)
                            t.wait_ge(ht_ready, GUP * j + GUP)
                            for g in range(GUP, PIECES):
                                s_ = g % NSM
                                t.wait_ge(landed[s_], 32 * TURN * j + 32 * (g // NSM + 1))
                                for q in range(4):
                                    k = 4 * (g - GUP) + q
                                    for m in range(2):
                                        mm = t.matmul(ps[4 + m][:, :], hidT[:, k, :], ring[:, s_, q * D + m * 512:q * D + (m + 1) * 512],
                                                      start=(k == 0), stop=(k == FT - 1))
                                mm.then_inc(used[s_], 1)
                            gather(j + 2)
                            t.wait_ge(y_ready, 2 * j + 2)
                            for c in range(DC):
                                if c >= 2:
                                    t.wait_ge(yo_added, DC * j + (c - 1))
                                t.matmul(ps[2 + c % 2][:, 0:TOK], Y[:, c * P:(c + 1) * P], selT[:, :], start=True, stop=True).then_inc(yo_full, 1)

                    @block.scalar
                    def _(s):
                        n = s.value_load(njobs[0:1, 0:1], min_val=NE, max_val=NE + 4)
                        with s.Fori(0, n) as j:
                            for g in range(GUP):
                                s.wait_ge(used[g % NSM], TURN * j + (g // NSM + 2))
                                if g >= 2:
                                    s.wait_ge(h_ready, GUP * j + (g - 1))
                                s.activation(sil[:, g % 2, :], ps[g % 2][:, 0:256], ACT.Silu).then_inc(sil_ready, 1)
                                if g >= 1:
                                    s.wait_ge(ht_full, GUP * j + g)
                                    s.activation(hidT[:, 2 * g - 2:2 * g, :], ps[2 + (g - 1) % 2][:, 0:256].rearrange("p (q t) -> p q t", q=2),
                                                 ACT.Copy).then_inc(ht_ready, 1)
                            s.wait_ge(ht_full, GUP * j + GUP)
                            s.activation(hidT[:, FT - 2:FT, :], ps[2 + (GUP - 1) % 2][:, 0:256].rearrange("p (q t) -> p q t", q=2), ACT.Copy).then_inc(ht_ready, 1)
                            s.wait_ge(used[(PIECES - 1) % NSM], TURN * j + (TURN + 1))
                            s.activation(Y[:, 0:512], ps[4][:, :], ACT.Copy).then_inc(y_ready, 1)

                    @block.vector
                    def _(v):
                        n = v.value_load(njobs[0:1, 0:1], min_val=NE, max_val=NE + 4)

                        def select(dst, col, second):
                            for i, (lo, r) in enumerate(TILES):
                                last = v.tensor_scalar(dst[0:r, i, :], C("slots", r), slotno[0:r, i, col], second(i, r), ALU.is_equal, ALU.mult)
                            return last

                        def gather_out(value):
                            for c in range(2):
                                v.wait_ge(xg_full, value + c)
                                v.tensor_copy(xg[:, 4 * c:4 * c + 4, :], ps[6 + c][:, :].rearrange("p (q t) -> p q t", q=4)).then_inc(xg_ready, 1)
                        select(sel, slice(0, 1), lambda i, r: 1.0).then_inc(sel_ready, 1)
                        gather_out(1)
                        with v.Fori(0, n) as j:
                            select(selg, bass.ds(j, 1), lambda i, r: gate[0:r, i, bass.ds(j, 1)]).then_inc(selg_ready, 1)
                            select(sel, bass.ds(j + 1, 1), lambda i, r: 1.0).then_inc(sel_ready, 1)
                            for g in range(GUP):
                                v.wait_ge(sil_ready, GUP * j + (g + 1))
                                if g >= 2:
                                    v.wait_ge(ht_full, GUP * j + (g - 1))
                                v.tensor_tensor(hrow[:, g % 2, :], sil[:, g % 2, :], ps[g % 2][:, 256:512], ALU.mult).then_inc(h_ready, 1)
                                if g == 2:
                                    v.wait_ge(st_full, j + 1)
                                    v.tensor_copy(selT[:, :], ps[4][:, 0:TOK]).then_inc(st_ready, 1)
                            v.wait_ge(used[(PIECES - 1) % NSM], TURN * j + (TURN + 1))
                            v.tensor_copy(Y[:, 512:1024], ps[5][:, :]).then_inc(y_ready, 1)
                            gather_out(2 * j + 3)
                            for c in range(DC):
                                v.wait_ge(yo_full, DC * j + (c + 1))
                                v.tensor_tensor(xT[:, c, :], xT[:, c, :], ps[2 + c % 2][:, 0:TOK], ALU.add).then_inc(yo_added, 1)

        with ExitStack() as st:
            sq = sbuf(st, "sq", [P, DC, TOK])
            yrow = sbuf(st, "yrow", [P, 3, D])
            n_dve, n_pe, n_act = rms_steps("fin", xT[:, :, :], DC, V("final_norm", 0, 8), hT, D, scratch=sq)
            h_ready, full, f_act, f_dve = (sem(x) for x in ("fin_h", "yrow_full", "yrow_act", "yrow_dve"))
            with nc.Block() as block:

                @block.tensor
                def _(t):
                    n_pe(t)
                    t.wait_ge(h_ready, 1)
                    for n in range(6):
                        lo, r = TILES[n // 2]
                        if n >= 4:
                            t.wait_ge(f_act if n % 2 == 0 else f_dve, 1)
                        for q in range(4):
                            mm = t.transpose(ps[n % 4][0:r, q * P:(q + 1) * P], hT[:, 4 * (n % 2) + q, lo:lo + r], C("ident"))
                        mm.then_inc(full, 1)

                @block.scalar
                def _(s):
                    n_act(s)
                    for n in range(0, 6, 2):
                        s.wait_ge(full, n + 1)
                        r = TILES[n // 2][1]
                        s.activation(yrow[0:r, n // 2, 0:512], ps[n % 4][0:r, :], ACT.Copy).then_inc(f_act, 1)

                @block.vector
                def _(v):
                    n_dve(v)
                    v.sem_inc(h_ready, 1)
                    for n in range(1, 6, 2):
                        v.wait_ge(full, n + 1)
                        r = TILES[n // 2][1]
                        v.tensor_copy(yrow[0:r, n // 2, 512:1024], ps[n % 4][0:r, :]).then_inc(f_dve, 1)

                @block.sync
                def _(sp):
                    for i, (lo, r) in enumerate(TILES):
                        sp.wait_ge(f_act, i + 1)
                        sp.wait_ge(f_dve, i + 1)
                        dst = (O["y_prompt"][0, lo:lo + r, :] if i < 2 else O["y_sample"].rearrange("b t d -> (b t) d"))
                        store(sp, dst, yrow[0:r, i, :])
                    sp.wait_ge(stored.sem, stored.n)


_OUTS = [("y_prompt", (1, SEQ, D)), ("y_sample", (NB, DS, D)), ("new_mla_prompt", (1, 1, SEQ, LAT)), ("new_mla_sample", (1, NB, DS, LAT)),
         ("new_rwkv_prompt", (1, 1, RH, RD, RD)), ("new_rwkv_sample", (1, NB, RH, RD, RD)), ("new_shift_prompt", (1, 1, RPROJ)),
         ("new_shift_sample", (1, NB, RPROJ)), ("new_gla_prompt", (1, 1, GH, DK, DV)), ("new_gla_sample", (1, NB, GH, DK, DV))]


def kernel(**inputs):
    import concourse.bacc as bacc
    from concourse.bass_utils import run_bass_kernel_spmd as run

    nc = bacc.Bacc("TRN2", target_bir_lowering=False, num_devices=1)
    arrays, A, O = {}, {}, {}
    for name, a in list(inputs.items()) + [("consts", constants()[1])]:
        a = np.ascontiguousarray(a)
        arrays[f"in_{name}"] = a
        A[name] = nc.dram_tensor(f"in_{name}", a.shape, mybir.dt.from_np(a.dtype), kind="ExternalInput").ap()
    for name, shape in _OUTS:
        O[name] = nc.dram_tensor(f"out_{name}", shape, F32, kind="ExternalOutput").ap()
    model(nc, A, O)
    r = run(nc, [arrays], core_ids=[0])
    return tuple(r.results[0][f"out_{name}"] for name, _ in _OUTS)
```

```python
from contextlib import ExitStack

import numpy as np

import concourse.bass as bass
from concourse import mybir

F32 = mybir.dt.float32
F32R = mybir.dt.float32r
I32 = mybir.dt.int32
ALU = mybir.AluOpType
ACT = mybir.ActivationFunctionType
AX_X = mybir.AxisListType.X

P = 128
D = 1024
DC = D // P
SEQ, NB, DS = 256, 8, 8
TOK = SEQ + NB * DS
TILES = [(0, P), (P, P), (2 * P, NB * DS)]
PAST, PAGE = 2048, 128
NPAGE = PAST // PAGE
H = 8
NOPE, ROPE, VD = 64, 32, 64
QR, KVR = 384, 256
LAT = KVR + ROPE
SCALE = float((NOPE + ROPE) ** -0.5)
RH, RD = 8, 64
RDIM = RH * RD
RPROJ = 3 * RDIM + 64 + 64 + 128
RT = RPROJ // P
EVEN_IN = QR + LAT + RPROJ
GH, DK, DV = 4, 128, 256
GRANK = 16
GK, GV = GH * DK, GH * DV
ODD_IN = 2 * GK + 2 * GV + GRANK
DFF, DFE = 2816, 3584
NE = 8
RC, GC = 64, 32
EPS = 1e-6
LN_EPS = 64e-5
HALF_E = float(np.exp(np.float32(-0.5)))
FAR = 1.0e4
MAXJOB = 16

VEC = {}
_at = 0
for _name, _n in [("norm_mix_even", 8), ("norm_ffn_even", 8), ("mla_q_norm", 3), ("mla_kv_norm", 2),
                  ("rwkv_mu", RT), ("rwkv_w0", 4), ("rwkv_a0", 4), ("rwkv_k_k", 4), ("rwkv_k_a", 4),
                  ("rwkv_r_k", 4), ("rwkv_ln_g", 4), ("rwkv_ln_b", 4), ("norm_mix_odd", 8),
                  ("norm_ffn_odd", 8), ("gla_ab", 4), ("gla_norm", 8), ("final_norm", 8)]:
    VEC[_name] = (_at, _n)
    _at += _n
NVEC = _at


def constants():
    p = np.arange(P)
    i, j = p[:, None], p[None, :]
    f = {}
    f["ident"] = (i == j)
    f["ones"] = np.ones((P, P))
    f["head_ones"] = (i // 64 == j // 64)
    f["rw_T"] = np.concatenate([(i // RC == j // RC) & (i < j), (i // RC == j // RC) & (i <= j)], 1)
    s8T = np.zeros((P, 2 * P))
    s8T[:64, 0:64] = ((i // DS == j // DS) & (i < j))[:64, :64]
    s8T[:64, P:P + 64] = ((i // DS == j // DS) & (i <= j))[:64, :64]
    f["sm_T"] = s8T
    for s in (1, 2, 4, 8, 16, 32):
        low = (i // (2 * s) == j // (2 * s)) & (i % (2 * s) >= s) & (j % (2 * s) < s)
        f[f"lev{s}"] = low
        if s == 1:
            f["lev1_T"] = low.T
    f["causal"] = np.where(i <= j, 0.0, -1e30)
    f["own"] = np.where((i % DS >= np.arange(DS)[None, :]), 0.0, -1e30)
    f["gla_T"] = (i // GC == j // GC) & (i <= j)
    pos = np.arange(TOK)
    for name, c in (("reset_rw", RC), ("reset_gla", GC)):
        start = np.where(pos < SEQ, pos % c == 0, (pos - SEQ) % DS == 0)
        f[name] = np.broadcast_to(np.where(start, 0.0, 1.0)[None], (P, TOK))
    place = np.where(pos < SEQ, pos, PAST + (pos - SEQ) % DS).astype(np.float32)
    inv = (np.float32(10000.0) ** (-np.arange(0, ROPE, 2, dtype=np.float32) / np.float32(ROPE))).astype(np.float32)
    ang = (place[None, :] * inv[:, None]).astype(np.float32)
    for name, t in (("cos", np.cos(ang)), ("sin", np.sin(ang))):
        full = np.zeros((P, TOK), np.float32)
        full[:32] = np.concatenate([t, t], 0)
        f[name] = full
    rot = np.zeros((P, ROPE))
    for a in range(16):
        rot[a + 16, a] = -1.0
        rot[a, a + 16] = 1.0
    f["rot"] = rot
    bsel = np.zeros((P, NB))
    bsel[:64] = (i[:64] // DS == np.arange(NB)[None, :])
    f["bsel"] = bsel
    f["before"] = (i < j)
    f["slots"] = np.broadcast_to(j, (P, P))
    e = np.arange(NE)
    f["tie"] = np.broadcast_to((e[None, :] < e[:, None]).reshape(1, 64), (P, 64))
    c = np.arange(16)
    f["part"] = np.broadcast_to((128.0 * (1 + c // 8))[None], (P, 16))
    f["expert"] = np.broadcast_to((c % 8)[None], (P, 16))
    f["jobno"] = np.broadcast_to(np.repeat(np.arange(8), 16)[None], (P, 128))
    cols, at, parts = {}, 0, []
    for k, a in f.items():
        a = np.ascontiguousarray(a, dtype=np.float32)
        cols[k] = (at, a.shape[1])
        at += a.shape[1]
        parts.append(a)
    return cols, np.concatenate(parts, 1)


class Signal:
    def __init__(self, sem):
        self.sem, self.n = sem, 0


def done(eng, ins, sig):
    ins.then_inc(sig.sem, 1)
    sig.n += 1
    eng.wait_ge(sig.sem, sig.n)
    return sig.n


def model(nc, A, O):
    ctx = ExitStack()
    names = [0]

    layer_sems = []

    def sem(name):
        names[0] += 1
        layer_sems.append(nc.alloc_semaphore(f"{name}_{names[0]}"))
        return layer_sems[-1]

    def next_part():
        nc.all_engine_barrier()
        nc.clear_and_free_semaphores(layer_sems)
        layer_sems.clear()
        nc.all_engine_barrier()

    def sbuf(scope, name, shape, dt=F32):
        names[0] += 1
        return scope.enter_context(nc.sbuf_tensor(f"{name}_{names[0]}", shape, dt))

    with ctx:
        CC, _ = constants()
        consts = sbuf(ctx, "consts", [P, sum(n for _, n in CC.values())])

        def C(name, rows=P, lo=0, hi=None):
            at, n = CC[name]
            return consts[0:rows, at + lo:at + (n if hi is None else hi)]

        vecs = sbuf(ctx, "vecs", [P, NVEC])

        def V(name, k=0, n=1):
            return vecs[:, VEC[name][0] + k:VEC[name][0] + k + n]

        xT = sbuf(ctx, "xT", [P, DC, TOK])
        hT = sbuf(ctx, "hT", [P, DC, TOK])
        mixT = sbuf(ctx, "mixT", [P, DC, TOK])
        rstd = sbuf(ctx, "rstd", [P, TOK])
        ps = [ctx.enter_context(nc.psum_tensor(f"bank{b}", [P, 512], F32)) for b in range(8)]
        dve_order, act_order, pool_order, stored = (Signal(ctx.enter_context(nc.semaphore(x))) for x in (
            "dve_order", "act_order", "pool_order", "stored"))

        def dv(v, ins):
            done(v, ins, dve_order)

        def ac(s, ins):
            done(s, ins, act_order)

        def po(g, ins):
            done(g, ins, pool_order)

        def store(eng, dst, src):
            eng.dma_start(dst, src).then_inc(stored.sem, 16)
            stored.n += 16

        def load(eng, dst, src, sig):
            eng.dma_start(dst, src).then_inc(sig.sem, 16)
            sig.n += 16

        class Linear:
            def __init__(self, name, tiles, banks):
                self.full, self.act, self.dve = sem(name + "_full"), sem(name + "_act"), sem(name + "_dve")
                self.tiles, self.banks = tiles, banks
                assert len(banks) % 2 == 0

            def pe(self, pe, weights, chunks, rhs, ready=None, rows=None):
                nb = len(self.banks)
                for t in range(self.tiles):
                    if ready:
                        ready(t)
                    if t >= nb:
                        pe.wait_ge(self.act if t % 2 == 0 else self.dve, (t - nb) // 2 + 1)
                    for k in range(chunks):
                        w = weights(t, k)
                        n = w.shape[1] if len(w.shape) == 2 else w.shape[1] * w.shape[2]
                        mm = pe.matmul(ps[self.banks[t % nb]][0:n, 0:TOK], w, rhs(k), start=(k == 0), stop=(k == chunks - 1))
                    mm.then_inc(self.full, 1)

            def out(self, t, rows=P):
                return ps[self.banks[t % len(self.banks)]][0:rows, 0:TOK]

            def run_act(self, s, body):
                for t in range(0, self.tiles, 2):
                    s.wait_ge(self.full, t + 1)
                    body(t).then_inc(self.act, 1)

            def run_dve(self, v, body):
                for t in range(1, self.tiles, 2):
                    v.wait_ge(self.full, t + 1)
                    body(t).then_inc(self.dve, 1)

        def rms_steps(name, src, chunks, gain, dst, width, eps=EPS, bank=7, scratch=None):
            sq_ready, sum_ready, var_ready, rstd_ready = (sem(f"{name}_{x}") for x in ("sq", "sum", "var", "rstd"))

            def dve(v):
                dv(v, v.tensor_tensor(scratch[:, 0:chunks, :], src, src, ALU.mult))
                v.sem_inc(sq_ready, 1)
                v.wait_ge(sum_ready, 1)
                v.tensor_scalar(rstd[:, :], ps[bank][:, 0:TOK], 1.0 / width, eps, ALU.mult, ALU.add).then_inc(var_ready, 1)
                v.wait_ge(rstd_ready, 1)
                dv(v, v.reciprocal(rstd[:, :], rstd[:, :]))
                for k in range(chunks):
                    last = v.scalar_tensor_tensor(out=dst[:, k, :], in0=src[:, k, :], scalar=gain[:, k:k + 1],
                                                  in1=rstd[:, :], op0=ALU.mult, op1=ALU.mult)
                dv(v, last)

            def pe(t):
                t.wait_ge(sq_ready, 1)
                for k in range(chunks):
                    mm = t.matmul(ps[bank][:, 0:TOK], C("ones"), scratch[:, k, :], start=(k == 0), stop=(k == chunks - 1))
                mm.then_inc(sum_ready, 1)

            def act(s):
                s.wait_ge(var_ready, 1)
                s.activation(rstd[:, :], rstd[:, :], ACT.Sqrt).then_inc(rstd_ready, 1)

            return dve, pe, act

        def product(t, out, w_hi, w_lo, x_hi, x_lo, start, stop):
            t.matmul(out, w_hi, x_hi, start=start, stop=False)
            t.matmul(out, w_hi, x_lo, start=False, stop=False)
            return t.matmul(out, w_lo, x_hi, start=False, stop=stop)

        def projection(name, w_dram, pieces, outs, src, norm=None):
            NS, NSP, NBK = 4, 3, 8
            with ExitStack() as st:
                ring = sbuf(st, name + "_ring", [P, NS, DC * 256])
                whi = sbuf(st, name + "_w_hi", [P, NSP, DC * 256], F32R)
                wlo = sbuf(st, name + "_w_lo", [P, NSP, DC * 256], F32R)
                xhi = sbuf(st, name + "_x_hi", [P, DC, TOK], F32R)
                xlo = sbuf(st, name + "_x_lo", [P, DC, TOK], F32R)
                landed = [sem(f"{name}_landed{i}") for i in range(NS)]
                x_split, hi_ready, split, full = (sem(f"{name}_{x}") for x in ("x_split", "hi_ready", "piece_split", "full"))
                taken = {"act": sem(name + "_act"), "dve": sem(name + "_dve")}
                before = [sum(o[4] == outs[n][4] for o in outs[:n]) for n in range(len(outs))]

                def view(buf, slot, i):
                    n = pieces[i][1]
                    return buf[:, slot, 0:DC * n].rearrange("p (c n) -> p c n", c=DC)

                def shape(n):
                    _, _, width, tile, _, _ = outs[n]
                    return ps[n % NBK][0:width, 0:TOK] if tile is None else ps[n % NBK][0:TILES[tile][1], 0:width]

                def take(eng, which, pieces_from, pieces_to):
                    for n, (piece, _, _, _, who, fn) in enumerate(outs):
                        if who == which and pieces_from <= piece < pieces_to:
                            eng.wait_ge(full, n + 1)
                            fn(eng, shape(n)).then_inc(taken[who], 1)

                with nc.Block() as block:
                    @block.sync
                    def _(sp):
                        w = w_dram.rearrange("(c p) n -> p c n", p=P)
                        for i, (at, n) in enumerate(pieces):
                            if i >= NS:
                                sp.wait_ge(split, i - NS + 1)
                            sp.dma_start(view(ring, i % NS, i), w[:, :, at:at + n]).then_inc(landed[i % NS], 16)

                    @block.scalar
                    def _(s):
                        if norm:
                            norm[2](s)
                        for i in range(len(pieces)):
                            if i >= NSP:
                                s.wait_ge(full, sum(o[0] <= i - NSP for o in outs))
                            s.wait_ge(landed[i % NS], 16 * (i // NS + 1))
                            s.activation(view(whi, i % NSP, i), view(ring, i % NS, i), ACT.Copy).then_inc(hi_ready, 1)
                            take(s, "act", i - 2, i - 1)
                        take(s, "act", len(pieces) - 2, len(pieces))

                    @block.vector
                    def _(v):
                        if norm:
                            norm[0](v)
                        for i in range(len(pieces)):
                            if i < 2:
                                part = slice(DC // 2 * i, DC // 2 * (i + 1))
                                dv(v, v.tensor_copy(xhi[:, part, :], src[:, part, :]))
                                v.tensor_tensor(xlo[:, part, :], src[:, part, :], xhi[:, part, :].bitcast(F32), ALU.subtract).then_inc(x_split, 1)
                            v.wait_ge(hi_ready, i + 1)
                            v.tensor_tensor(view(wlo, i % NSP, i), view(ring, i % NS, i), view(whi, i % NSP, i).bitcast(F32), ALU.subtract).then_inc(split, 1)
                            take(v, "dve", i - 2, i - 1)
                        take(v, "dve", len(pieces) - 2, len(pieces))

                    @block.tensor
                    def _(t):
                        if norm:
                            norm[1](t)
                        for n, (piece, at, width, tile, _, _) in enumerate(outs):
                            if n == 0 or outs[n - 1][0] != piece:
                                t.wait_ge(split, piece + 1)
                            if n >= NBK:
                                t.wait_ge(taken[outs[n - NBK][4]], before[n - NBK] + 1)
                            for k in range(DC):
                                if n == 0 and k % (DC // 2) == 0:
                                    t.wait_ge(x_split, k // (DC // 2) + 1)
                                w_hi, w_lo = (view(b, piece % NSP, piece)[:, k, at:at + width] for b in (whi, wlo))
                                if tile is None:
                                    mm = product(t, shape(n), w_hi, w_lo, xhi[:, k, :], xlo[:, k, :], k == 0, k == DC - 1)
                                else:
                                    toks = slice(TILES[tile][0], TILES[tile][0] + TILES[tile][1])
                                    mm = product(t, shape(n), xhi[:, k, toks], xlo[:, k, toks], w_hi, w_lo, k == 0, k == DC - 1)
                            mm.then_inc(full, 1)

        def copy_to(dst):
            return lambda eng, bank: eng.activation(dst, bank, ACT.Copy) if eng is nc.scalar else eng.tensor_copy(dst, bank)

        with ExitStack() as st:
            xtok = sbuf(st, "xtok", [P, 3, D])
            vrow = sbuf(st, "vrow", [P, P])
            consts_in, rows_in, x_in = Signal(sem("consts_in")), Signal(sem("rows_in")), Signal(sem("x_in"))
            turned, x_act, x_dve, vec_full = sem("turned"), sem("x_act"), sem("x_dve"), sem("vec_full")
            with nc.Block() as block:
                @block.sync
                def _(sp):
                    load(sp, consts[:, :], A["consts"], consts_in)
                    load(sp, xtok[:, 0:2, :], A["x_prompt"][0].rearrange("(t p) d -> p t d", p=P), x_in)
                    load(sp, xtok[0:64, 2, :], A["x_sample"].rearrange("b t d -> (b t) d"), x_in)

                @block.scalar
                def _(s):
                    for k, (at, n) in VEC.items():
                        a = A[k]
                        flat = {1: "a -> a", 2: "a b -> (a b)", 3: "a b c -> (a b c)"}[len(a.shape)]
                        a = a.rearrange(flat) if len(a.shape) > 1 else a
                        load(s, vrow[at:at + n, :], a.rearrange("(c p) -> c p", p=P), rows_in)
                    for g in range(0, 6, 2):
                        s.wait_ge(turned, g + 1)
                        t, half = g // 2, g % 2
                        r = TILES[t][1]
                        s.activation(xT[:, 4 * half:4 * half + 4, TILES[t][0]:TILES[t][0] + r],
                                     ps[g % 4][:, :].rearrange("p (c t) -> p c t", c=4)[:, :, 0:r], ACT.Copy).then_inc(x_act, 1)

                @block.tensor
                def _(t):
                    t.wait_ge(consts_in.sem, 16)
                    t.wait_ge(x_in.sem, 32)
                    for g in range(6):
                        if g >= 4:
                            t.wait_ge(x_act if g % 2 == 0 else x_dve, 1)
                        i, half = g // 2, g % 2
                        r = TILES[i][1]
                        for c in range(4):
                            mm = t.transpose(ps[g % 4][:, c * P:c * P + r], xtok[0:r, i, (4 * half + c) * P:(4 * half + c + 1) * P],
                                             C("ident", r, 0, r))
                        mm.then_inc(turned, 1)
                    t.wait_ge(rows_in.sem, 16 * len(VEC))
                    t.transpose(ps[4][:, 0:NVEC], vrow[0:NVEC, :], C("ident", NVEC, 0, NVEC)).then_inc(vec_full, 1)

                @block.vector
                def _(v):
                    for g in range(1, 6, 2):
                        v.wait_ge(turned, g + 1)
                        t, half = g // 2, g % 2
                        r = TILES[t][1]
                        v.tensor_copy(xT[:, 4 * half:4 * half + 4, TILES[t][0]:TILES[t][0] + r],
                                      ps[g % 4][:, :].rearrange("p (c t) -> p c t", c=4)[:, :, 0:r]).then_inc(x_dve, 1)
                    v.wait_ge(vec_full, 1)
                    dv(v, v.tensor_copy(vecs[:, :], ps[4][:, 0:NVEC]))

        with ExitStack() as ev:
            kvT = sbuf(ev, "kvT", [P, 2, TOK])
            kpe = sbuf(ev, "kpe", [ROPE, TOK])
            qcT = sbuf(ev, "qcT", [P, 3, TOK])
            rwT = sbuf(ev, "rwT", [P, RT, TOK])
            with ExitStack() as st:
                sq = sbuf(st, "sq", [P, DC, TOK])
                norm = rms_steps("mixn", xT[:, :, :], DC, V("norm_mix_even", 0, 8), hT, D, scratch=sq)
                at_rw = QR + LAT
                pieces = [(0, 256), (256, 256), (512, at_rw - 512)] + [(at_rw + c, 256) for c in range(0, RT * P, 256)]
                tiles = ([(k // 2, k % 2 * P, P) for k in range(5)] + [(2, P, ROPE)] + [(3 + k // 2, k % 2 * P, P) for k in range(RT)])
                dest = [qcT[:, k, :] for k in range(3)] + [kvT[:, k, :] for k in range(2)] + [kpe[:, :]] + [rwT[:, k, :] for k in range(RT)]
                projection("proj", A["w_in_even"][0], pieces,
                           [t + (None, ("act", "dve")[n % 2], copy_to(dest[n])) for n, t in enumerate(tiles)], hT, norm)

            with ExitStack() as ml:
                latT = sbuf(ml, "latT", [P, 2, TOK])
                kroT = sbuf(ml, "kroT", [ROPE, TOK])
                latK = sbuf(ml, "latK", [P, 3, LAT])
                qlT = sbuf(ml, "qlT", [P, 2, H, TOK])
                qpT = sbuf(ml, "qpT", [ROPE, H, TOK])
                uv = sbuf(ml, "uv", [P, 2, H * VD])
                uv_in = Signal(sem("uv_in"))
                with ExitStack() as st:
                    cqT = sbuf(st, "cqT", [P, 3, TOK])
                    sq = sbuf(st, "sq", [P, 3, TOK])
                    uqn = sbuf(st, "uqn", [P, 3, H * NOPE])
                    uqp = sbuf(st, "uqp", [P, 3, H * ROPE])
                    small_in = Signal(sem("small_in"))
                    uk = sbuf(st, "uk", [P, 2, H * NOPE])
                    ukT = sbuf(st, "ukT", [P, 4, KVR])
                    qnT = sbuf(st, "qnT", [P, 4, TOK])
                    qpe = sbuf(st, "qpe", [ROPE, H, TOK])
                    qsw = sbuf(st, "qsw", [ROPE, H, TOK])
                    ksw = sbuf(st, "ksw", [ROPE, TOK])
                    a_dve, a_pe, a_act = rms_steps("qn", qcT[:, :, :], 3, V("mla_q_norm", 0, 3), cqT, QR, bank=7, scratch=sq)
                    b_dve, b_pe, b_act = rms_steps("kvn", kvT[:, :, :], 2, V("mla_kv_norm", 0, 2), latT, KVR, bank=6, scratch=sq)
                    uk_in, ukt_full, ukt_ready = Signal(sem("uk_in")), sem("ukt_full"), sem("ukt_ready")
                    cq_ready, rot_full, rot_free, kro_full, kro_ready, lk_full, lk_ready = (
                        sem(x) for x in ("cq_ready", "rot_full", "rot_free", "kro_full", "kro_ready", "lk_full", "lk_ready"))
                    qlin, qlin_out = Linear("q", 12, [0, 1, 2, 3]), None
                    klin = Linear("ql", 2 * H, [0, 1, 2, 3])
                    qdest = [qnT[:, k, :] for k in range(4)] + [qpe[:, h, :] for h in range(H)]
                    with nc.Block() as block:
                        @block.sync
                        def _(sp):
                            load(sp, uk[:, :, :], A["mla_w_uk"][0].rearrange("(c p) h n -> p c (h n)", p=P), uk_in)
                            for c in range(3):
                                w = A["mla_w_uq"][0, c * P:(c + 1) * P, :].rearrange("p (h n) -> p h n", h=H)
                                load(sp, uqn[:, c, :].rearrange("p (h n) -> p h n", h=H), w[:, :, 0:NOPE], small_in)
                                load(sp, uqp[:, c, :].rearrange("p (h n) -> p h n", h=H), w[:, :, NOPE:NOPE + ROPE], small_in)
                            load(sp, uv[:, :, :], A["mla_w_uv"][0].rearrange("(c p) h n -> p c (h n)", p=P), uv_in)
                            sp.wait_ge(lk_ready, 3)
                            store(sp, O["new_mla_prompt"][0, 0].rearrange("(t p) c -> p t c", p=P), latK[:, 0:2, :])
                            store(sp, O["new_mla_sample"][0].rearrange("b t c -> (b t) c"), latK[0:64, 2, :])
                            sp.wait_ge(stored.sem, stored.n)

                        @block.gpsimd
                        def _(g):
                            g.wait_ge(qlin.act, 6)
                            g.wait_ge(qlin.dve, 6)
                            for h in range(H):
                                last = g.tensor_tensor(qpT[:, h, :], qpe[:, h, :], C("cos", ROPE), ALU.mult)
                            po(g, last)
                            g.wait_ge(rot_free, H + 1)
                            po(g, g.tensor_tensor(qpT[:, :, :], qpT[:, :, :], qsw[:, :, :], ALU.add))

                        @block.vector
                        def _(v):
                            a_dve(v)
                            v.sem_inc(cq_ready, 1)
                            b_dve(v)
                            v.sem_inc(cq_ready, 1)
                            v.wait_ge(ukt_full, 1)
                            for g in range(2):
                                last = v.tensor_copy(ukT[:, 2 * g:2 * g + 2, :], ps[4 + g][:, :].rearrange("p (a c) -> p a c", a=2))
                            dv(v, last)
                            v.sem_inc(ukt_ready, 1)
                            qlin.run_dve(v, lambda t: v.tensor_copy(qdest[t], qlin.out(t, P if t < 4 else ROPE)))
                            for h in range(H + 1):
                                v.wait_ge(rot_full, h + 1)
                                dst = ksw[:, :] if h == H else qsw[:, h, :]
                                v.tensor_tensor(dst, ps[4 + h % 2][0:ROPE, 0:TOK], C("sin", ROPE), ALU.mult).then_inc(rot_free, 1)
                            dv(v, v.tensor_tensor(kroT[:, :], kpe[:, :], C("cos", ROPE), ALU.mult))
                            v.wait_ge(rot_free, H + 1)
                            dv(v, v.tensor_tensor(kroT[:, :], kroT[:, :], ksw[:, :], ALU.add))
                            v.sem_inc(kro_ready, 1)
                            klin.run_dve(v, lambda t: v.tensor_copy(qlT[:, t % 2, t // 2, :], klin.out(t)))

                        @block.scalar
                        def _(s):
                            a_act(s)
                            b_act(s)
                            qlin.run_act(s, lambda t: s.activation(qdest[t], qlin.out(t, P if t < 4 else ROPE), ACT.Copy))
                            klin.run_act(s, lambda t: s.activation(qlT[:, t % 2, t // 2, :], klin.out(t), ACT.Copy))
                            for i, (lo, r) in enumerate(TILES):
                                s.wait_ge(lk_full, i + 1)
                                s.activation(latK[0:r, i, :], ps[4 + i][0:r, 0:LAT], ACT.Copy).then_inc(lk_ready, 1)

                        @block.tensor
                        def _(t):
                            a_pe(t)
                            t.wait_ge(uk_in.sem, 16)
                            for pr in range(4):
                                for c in range(2):
                                    mm = t.transpose(ps[4 + pr // 2][:, (pr % 2) * KVR + c * P:(pr % 2) * KVR + (c + 1) * P],
                                                     uk[:, c, pr * P:(pr + 1) * P], C("ident"))
                            mm.then_inc(ukt_full, 1)
                            t.wait_ge(cq_ready, 1)
                            b_pe(t)
                            t.wait_ge(small_in.sem, 96)

                            def wq(i, k):
                                return uqn[:, k, i * P:(i + 1) * P] if i < 4 else uqp[:, k, (i - 4) * ROPE:(i - 3) * ROPE]
                            qlin.pe(t, wq, 3, lambda k: cqT[:, k, :])
                            t.wait_ge(qlin.act, 6)
                            t.wait_ge(qlin.dve, 6)
                            t.wait_ge(ukt_ready, 1)
                            for h in range(H + 1):
                                if h >= 2:
                                    t.wait_ge(rot_free, h - 1)
                                t.matmul(ps[4 + h % 2][0:ROPE, 0:TOK], C("rot", ROPE), kpe[:, :] if h == H else qpe[:, h, :],
                                         start=True, stop=True).then_inc(rot_full, 1)
                            def wk(i, k):
                                h, c = i // 2, i % 2
                                return ukT[(h % 2) * 64:(h % 2) * 64 + 64, h // 2, c * P:(c + 1) * P]
                            nb = 4
                            for i in range(2 * H):
                                h = i // 2
                                if i >= nb:
                                    t.wait_ge(klin.act if i % 2 == 0 else klin.dve, (i - nb) // 2 + 1)
                                t.matmul(ps[klin.banks[i % nb]][:, 0:TOK], wk(i, 0), qnT[(h % 2) * 64:(h % 2) * 64 + 64, h // 2, :],
                                         start=True, stop=True).then_inc(klin.full, 1)
                            t.wait_ge(kro_ready, 1)
                            t.wait_ge(cq_ready, 2)
                            for i, (lo, r) in enumerate(TILES):
                                for c in range(2):
                                    t.transpose(ps[4 + i][0:r, c * P:(c + 1) * P], latT[:, c, lo:lo + r], C("ident"))
                                t.transpose(ps[4 + i][0:r, KVR:LAT], kroT[:, lo:lo + r], C("ident", ROPE, 0, ROPE)).then_inc(lk_full, 1)

                with ExitStack() as st:
                    olB = sbuf(st, "olB", [P, H, TOK])
                    olT = [hT, olB]
                    NPB = 3
                    page_in = [sem(f"page_in{b}") for b in range(NPB)]
                    NQ = H * DS
                    pgs = [sbuf(st, f"pages{b}", [P, NPAGE, LAT]) for b in range(NPB)]
                    pgT = sbuf(st, "pgT", [P, 2, NPAGE * P])
                    pgR = mixT[0:ROPE, :, :].rearrange("p c t -> p (c t)")[:, 0:NPAGE * P]
                    sc = sbuf(st, "scores", [P, NPAGE + 1, NQ])
                    pr = sbuf(st, "probs", [P, NPAGE + 1, NQ])
                    tmax = qcT[:, :, :].rearrange("p c t -> p (c t)")[:, 0:512]
                    qmax = sbuf(st, "qmax", [P, 4])
                    mrep = kvT[:, :, :].rearrange("p c t -> p (c t)")[:, 0:512].rearrange("p (n t) -> p n t", n=4)
                    mall = sbuf(st, "mall", [P, 512])
                    rsum = sbuf(st, "rsum", [P, 512])
                    table = sbuf(st, "page_table", [1, NB * NPAGE], I32)
                    table_in = Signal(sem("table_in"))
                    Prow = mixT[64:128, :, :].rearrange("p c t -> p (c t)")[:, 0:NPAGE * P + 64]
                    orow = mixT[64:128, :, :].rearrange("p c t -> p (c t)")[:, NPAGE * P + 64:NPAGE * P + 64 + KVR]
                    qsl = sc[:, 0:16, :].rearrange("p (c b) q -> p c b q", c=2)
                    qsp = mall[0:ROPE, :].rearrange("p (b q) -> p b q", b=NB)
                    srows = sbuf(st, "srows", [P, 8 + 5 + 5 + 4])
                    snew, mx, esum, m1 = srows[64:128, 0:8], srows[64:128, 8:13], srows[64:128, 13:18], srows[64:128, 18:22]
                    (q_packed, s_full, mx_ready, ex_ready, pt_full, pt_dve, pt_act, v_full, o_ready, ot_full, ol_ready, np_zero) = (sem(x) for x in (
                        "q_packed", "sscore_full", "smax_ready", "sexp_ready", "probs_turned", "probsT_dve", "probsT_act", "values_full",
                        "orow_ready", "orow_turned", "olat_ready", "newkeys_zeroed"))
                    (u_score, u_mcol, u_tr, u_rep, u_mrow, u_sub, u_exp, u_pv, u_out, pg_tr, pg_act, pg_dve) = (
                        sem(x) for x in ("u_score", "u_mcol", "u_tr", "u_rep", "u_mrow", "u_sub", "u_exp", "u_pv", "u_out",
                                         "pg_turned", "pg_act", "pg_dve"))
                    NT = 12

                    def turned_group(q):
                        part, quad = q % 3, q // 3
                        dst = pgT[:, part, quad * 512:(quad + 1) * 512] if part < 2 else pgR[:, quad * 512:(quad + 1) * 512]
                        return part, quad, dst, P if part < 2 else ROPE
                    psc = sc[:, :, :].rearrange("p a b -> p (a b)")
                    ppr = pr[:, :, :].rearrange("p a b -> p (a b)")
                    UNITS = [("p", g) for g in range(4)] + [("s", b) for b in range(NB)]
                    with nc.Block() as block:
                        @block.sync
                        def _(sp):
                            load(sp, table[:, :], A["page_table"].rearrange("(o b) n -> o (b n)", o=1), table_in)
                            sp.wait_ge(table_in.sem, 16)
                            for b in range(NB):
                                _, rows = nc.values_load_multi_w_load_instructions(
                                    table[0:1, b * NPAGE:(b + 1) * NPAGE], engines=(mybir.EngineType.SP,), min_val=0,
                                    max_val=A["cache_mla"].shape[1] - 1)
                                for n in range(NPAGE):
                                    row = rows[n]
                                    if b >= NPB and n == 0:
                                        sp.wait_ge(v_full, b - NPB + 1)
                                        sp.nop()
                                    sp.dma_start(pgs[b % NPB][:, n, :], A["cache_mla"][0, bass.ds(row, 1)].rearrange("o p c -> (o p) c"))\
                                      .then_inc(page_in[b % NPB], 16)

                        @block.tensor
                        def _(t):
                            def turn(b, groups):
                                if b == NB:
                                    return
                                if groups[0] == 0:
                                    t.wait_ge(page_in[b % NPB], 16 * NPAGE * (b // NPB + 1))
                                for q in groups:
                                    n = NT * b + q
                                    part, quad, _, rows = turned_group(q)
                                    if n >= 2:
                                        t.wait_ge(pg_act if n % 2 == 0 else pg_dve, (n - 2) // 2 + 1)
                                    for x in range(4):
                                        src = pgs[b % NPB][:, 4 * quad + x, :]
                                        src = src[:, part * P:(part + 1) * P] if part < 2 else src[:, KVR:LAT]
                                        mm = t.transpose(ps[5 + n % 2][0:rows, x * P:(x + 1) * P], src, C("ident"))
                                    mm.then_inc(pg_tr, 1)

                            def scores(b):
                                t.wait_ge(pg_act, NT // 2 * (b + 1))
                                t.wait_ge(pg_dve, NT // 2 * (b + 1))
                                if b:
                                    t.wait_ge(pt_dve, b)
                                    t.wait_ge(pt_act, b)
                                for k in range(5):
                                    for c in range(3):
                                        lhs = qsl[:, c, b, :] if c < 2 else qsp[:, b, :]
                                        if k < 4:
                                            rhs = pgT[:, c, k * 512:(k + 1) * 512] if c < 2 else pgR[:, k * 512:(k + 1) * 512]
                                        else:
                                            new = slice(SEQ + b * DS, SEQ + (b + 1) * DS)
                                            rhs = latT[:, c, new] if c < 2 else kroT[:, new]
                                        mm = t.matmul(ps[k][64:128, 0:rhs.shape[1]], lhs, rhs, start=(c == 0), stop=(c == 2))
                                mm.then_inc(s_full, 1)

                            def turn_probs(b):
                                t.wait_ge(ex_ready, b + 1)
                                for n in range(NPAGE + 1):
                                    out = ps[n // 8][:, (n % 8) * NQ:(n % 8 + 1) * NQ] if n < NPAGE else ps[4][0:64, P:P + NQ]
                                    w = P if n < NPAGE else 64
                                    mm = t.transpose(out, Prow[:, n * P:n * P + w], C("ident")[64:128, 64:128])
                                mm.then_inc(pt_full, 1)

                            def values(b):
                                t.wait_ge(pt_dve, b + 1)
                                t.wait_ge(pt_act, b + 1)
                                if b:
                                    t.wait_ge(ol_ready, b)
                                for n in range(NPAGE + 1):
                                    rows = P if n < NPAGE else 64
                                    rhs = pgs[b % NPB][:, n, 0:KVR] if n < NPAGE else latK[0:64, 2, 0:KVR]
                                    mm = t.matmul(ps[7][64:128, 0:KVR], pr[0:rows, n, :], rhs, start=(n == 0), stop=(n == NPAGE))
                                mm.then_inc(v_full, 1)

                            def turn_out(b):
                                t.wait_ge(o_ready, b + 1)
                                for c in range(2):
                                    mm = t.transpose(ps[7][:, KVR + c * NQ:KVR + (c + 1) * NQ], orow[:, c * P:(c + 1) * P], C("ident")[64:128, 64:128])
                                mm.then_inc(ot_full, 1)
                            for u, (kind, g) in enumerate(UNITS):
                                if kind == "p":
                                    W = 512
                                    if u:
                                        t.wait_ge(u_sub, u)
                                    for bank, cols, kb, q0, nq in ((0, 0, 0, 0, 256), (1, 0, 1, P, P)):
                                        for c in range(3):
                                            lhs = latT[:, c, kb * P:(kb + 1) * P] if c < 2 else kroT[:, kb * P:(kb + 1) * P]
                                            rhs = (qlT[:, c, 2 * g:2 * g + 2, q0:q0 + nq] if c < 2 else qpT[:, 2 * g:2 * g + 2, q0:q0 + nq])
                                            mm = t.matmul(ps[bank][:, 0:2 * nq], lhs, rhs, start=(c == 0), stop=(c == 2))
                                    mm.then_inc(u_score, 1)
                                    t.wait_ge(u_mcol, u + 1)
                                    for n in range(4):
                                        mm = t.transpose(ps[3][:, n * P:(n + 1) * P], tmax[:, n * P:(n + 1) * P], C("ident"))
                                    mm.then_inc(u_tr, 1)
                                    t.wait_ge(u_rep, u + 1)
                                    for n in range(4):
                                        mm = t.matmul(ps[4][:, n * P:(n + 1) * P], mrep[:, n, :], C("ident"), start=True, stop=True)
                                    mm.then_inc(u_mrow, 1)
                                    t.wait_ge(u_exp, u + 1)
                                    t.matmul(ps[5][:, 0:512], C("ones"), ppr[:, 0:512], start=True, stop=False)
                                    for h in range(2):
                                        t.matmul(ps[5][:, h * 256 + P:h * 256 + 256], C("ones"), ppr[:, 512 + h * P:512 + (h + 1) * P],
                                                 start=False, stop=(h == 1))
                                    for c in range(2):
                                        t.matmul(ps[6 + c][:, 0:512], latK[:, 0, c * P:(c + 1) * P], ppr[:, 0:512], start=True, stop=False)
                                        for h in range(2):
                                            mm = t.matmul(ps[6 + c][:, h * 256 + P:h * 256 + 256], latK[:, 1, c * P:(c + 1) * P],
                                                          ppr[:, 512 + h * P:512 + (h + 1) * P], start=False, stop=(h == 1))
                                    mm.then_inc(u_pv, 1)
                                else:
                                    b = g
                                    if b == 0:
                                        t.wait_ge(u_out, 4)
                                        turn(0, range(NT))
                                        t.wait_ge(q_packed, 1)
                                    scores(b)
                                    if b:
                                        turn_out(b - 1)
                                    turn(b + 1, range(0, 10))
                                    turn_probs(b)
                                    turn(b + 1, range(10, NT))
                                    values(b)
                            turn_out(NB - 1)

                        @block.vector
                        def _(v):
                            def turned_out(b, groups):
                                for q in groups if b < NB else []:
                                    _, _, dst, rows = turned_group(q)
                                    v.wait_ge(pg_tr, NT * b + q + 1)
                                    v.tensor_copy(dst, ps[6][0:rows, :]).then_inc(pg_dve, 1)

                            def scale_out(b):
                                v.wait_ge(v_full, b + 1)
                                dv(v, v.tensor_reduce(m1[:, 1:2], esum, AX_X, ALU.add))
                                dv(v, v.reciprocal(m1[:, 2:3], m1[:, 1:2]))
                                v.tensor_scalar(orow, ps[7][64:128, 0:KVR], m1[:, 2:3], None, ALU.mult).then_inc(o_ready, 1)

                            def lat_out(b):
                                v.wait_ge(ot_full, b + 1)
                                for c in range(2):
                                    last = v.tensor_copy(olT[c][:, :, SEQ + b * DS:SEQ + (b + 1) * DS],
                                                         ps[7][:, KVR + c * NQ:KVR + (c + 1) * NQ].rearrange("p (h q) -> p h q", h=H))
                                dv(v, last)
                                v.sem_inc(ol_ready, 1)
                            for u, (kind, g) in enumerate(UNITS):
                                if kind == "p":
                                    v.wait_ge(u_score, u + 1)
                                    s0 = ps[0][:, 0:512].rearrange("p (h q) -> p h q", h=2)
                                    d0 = psc[:, 0:512].rearrange("p (h q) -> p h q", h=2)
                                    d1 = psc[:, 512:768].rearrange("p (h q) -> p h q", h=2)
                                    s1 = ps[1][:, 0:256].rearrange("p (h q) -> p h q", h=2)
                                    v.tensor_copy(d0[:, :, P:256], s0[:, :, P:256])
                                    for h in range(2):
                                        v.tensor_tensor(d0[:, h, 0:P], s0[:, h, 0:P], C("causal"), ALU.add)
                                        last = v.tensor_tensor(d1[:, h, :], s1[:, h, :], C("causal"), ALU.add)
                                    dv(v, last)
                                    tm = tmax[:, :].rearrange("p (h q) -> p h q", h=2)
                                    v.tensor_copy(tm[:, :, 0:P], d0[:, :, 0:P])
                                    dv(v, v.tensor_tensor(tm[:, :, P:256], d0[:, :, P:256], d1, ALU.max))
                                    v.sem_inc(u_mcol, 1)
                                    v.wait_ge(u_tr, u + 1)
                                    dv(v, v.tensor_reduce(qmax[:, 0:4], ps[3][:, :].rearrange("p (n k) -> p n k", n=4), AX_X, ALU.max))
                                    for n in range(4):
                                        last = v.tensor_scalar(mrep[:, n, :], C("ones"), qmax[:, n:n + 1], None, ALU.mult)
                                    last.then_inc(u_rep, 1)
                                    v.wait_ge(u_mrow, u + 1)
                                    dv(v, v.tensor_copy(mall[:, :], ps[4][:, :]))
                                    m3 = mall[:, :].rearrange("p (h q) -> p h q", h=2)
                                    dv(v, v.tensor_tensor(psc[:, 0:512], psc[:, 0:512], mall[:, :], ALU.subtract))
                                    dv(v, v.tensor_tensor(d1, d1, m3[:, :, P:256], ALU.subtract))
                                    v.sem_inc(u_sub, 1)
                                    v.wait_ge(u_pv, u + 1)
                                    dv(v, v.reciprocal(rsum[:, :], ps[5][:, :]))
                                    for c in range(2):
                                        last = v.tensor_tensor(olT[c][:, 2 * g:2 * g + 2, 0:SEQ],
                                                               ps[6 + c][:, :].rearrange("p (h q) -> p h q", h=2),
                                                               rsum[:, :].rearrange("p (h q) -> p h q", h=2), ALU.mult)
                                    dv(v, last)
                                    v.sem_inc(u_out, 1)
                                else:
                                    b = g
                                    if b == 0:
                                        v.wait_ge(u_exp, 4)
                                        for c in range(2):
                                            v.tensor_copy(qsl[:, c, :, :].rearrange("p b (h t) -> p b h t", h=H),
                                                          qlT[:, c, :, SEQ:TOK].rearrange("p h (b t) -> p b h t", b=NB))
                                        dv(v, v.tensor_copy(qsp.rearrange("p b (h t) -> p b h t", h=H), qpT[:, :, SEQ:TOK].rearrange("p h (b t) -> p b h t", b=NB)))
                                        v.sem_inc(q_packed, 1)
                                        turned_out(0, range(1, NT, 2))
                                    else:
                                        scale_out(b - 1)
                                    v.wait_ge(s_full, b + 1)
                                    for k in range(4):
                                        v.tensor_reduce(mx[:, k:k + 1], ps[k][64:128, :], AX_X, ALU.max)
                                    v.memset(Prow[:, NPAGE * P:NPAGE * P + 64], 0.0)
                                    dv(v, v.tensor_tensor(snew, ps[4][64:128, 0:DS], C("own")[64:128, :], ALU.add))
                                    dv(v, v.tensor_reduce(mx[:, 4:5], snew, AX_X, ALU.max))
                                    dv(v, v.tensor_reduce(m1[:, 3:4], mx, AX_X, ALU.max))
                                    dv(v, v.tensor_scalar(m1[:, 0:1], m1[:, 3:4], -SCALE, None, ALU.mult))
                                    v.sem_inc(mx_ready, 1)
                                    if b:
                                        lat_out(b - 1)
                                    turned_out(b + 1, range(1, 10, 2))
                                    v.wait_ge(pt_full, b + 1)
                                    v.tensor_copy(pr[:, 0:8, :], ps[0][:, :].rearrange("p (n q) -> p n q", n=8))
                                    v.tensor_copy(pr[0:64, NPAGE, :], ps[4][0:64, P:P + NQ]).then_inc(pt_dve, 1)
                                    turned_out(b + 1, range(11, NT, 2))
                            scale_out(NB - 1)
                            lat_out(NB - 1)

                        @block.scalar
                        def _(s):
                            def turned_out(b, groups):
                                for q in groups if b < NB else []:
                                    _, _, dst, rows = turned_group(q)
                                    s.wait_ge(pg_tr, NT * b + q + 1)
                                    s.activation(dst, ps[5][0:rows, :], ACT.Copy).then_inc(pg_act, 1)
                            for u, (kind, g) in enumerate(UNITS):
                                if kind == "p":
                                    s.wait_ge(u_sub, u + 1)
                                    s.activation(ppr[:, 0:768], psc[:, 0:768], ACT.Exp, scale=SCALE).then_inc(u_exp, 1)
                                else:
                                    if g == 0:
                                        turned_out(0, range(0, NT, 2))
                                    turned_out(g + 1, range(0, 4, 2))
                                    s.wait_ge(mx_ready, g + 1)
                                    for k in range(4):
                                        s.activation(Prow[:, k * 512:(k + 1) * 512], ps[k][64:128, :], ACT.Exp, bias=m1[:, 0:1], scale=SCALE,
                                                     accum_out=esum[:, k:k + 1])
                                    s.activation(Prow[:, NPAGE * P + g * DS:NPAGE * P + (g + 1) * DS], snew, ACT.Exp, bias=m1[:, 0:1], scale=SCALE,
                                                 accum_out=esum[:, 4:5]).then_inc(ex_ready, 1)
                                    turned_out(g + 1, range(4, 10, 2))
                                    s.wait_ge(pt_full, g + 1)
                                    s.activation(pr[:, 8:16, :], ps[1][:, :].rearrange("p (n q) -> p n q", n=8), ACT.Copy).then_inc(pt_act, 1)
                                    turned_out(g + 1, range(10, NT, 2))

                    full, out_a, out_d = sem("ov_full"), sem("ov_act"), sem("ov_dve")
                    with nc.Block() as block:
                        @block.tensor
                        def _(t):
                            t.wait_ge(uv_in.sem, 16)
                            for h in range(H):
                                for c in range(2):
                                    mm = t.matmul(ps[h // 2][(h % 2) * 64:(h % 2) * 64 + 64, 0:TOK], uv[:, c, h * VD:(h + 1) * VD],
                                                  olT[c][:, h, :], start=(c == 0), stop=(c == 1))
                                mm.then_inc(full, 1)

                        @block.vector
                        def _(v):
                            for g in (0, 1):
                                v.wait_ge(full, 2 * g + 2)
                                dv(v, v.tensor_copy(mixT[:, g, :], ps[g][:, 0:TOK]))

                        @block.scalar
                        def _(s):
                            for g in (2, 3):
                                s.wait_ge(full, 2 * g + 2)
                                ac(s, s.activation(mixT[:, g, :], ps[g][:, 0:TOK], ACT.Copy))

            AR = hT[:, :, :].rearrange("p (c a) t -> p c a t", a=2)
            with ExitStack() as rk:
                bF = sbuf(rk, "bF", [P, 4, TOK])
                kF = sbuf(rk, "kF", [P, 4, TOK])
                gT = sbuf(rk, "gT", [P, 4, TOK])
                bonus = sbuf(rk, "bonus", [P, 4, TOK])
                rowB = sbuf(rk, "rowB", [P, 3, RDIM])
                rowK = sbuf(rk, "rowK", [P, 3, RDIM])
                rowV = sbuf(rk, "rowV", [P, 3, RDIM])
                wend = sbuf(rk, "wend", [P, 4, 4])
                wends = sbuf(rk, "wends", [P, 4, NB])
                S0T = sbuf(rk, "S0T", [P, NB, 4, RD])
                with ExitStack() as st:
                    shrow = sbuf(st, "shrow", [NB, RPROJ])
                    shT = sbuf(st, "shT", [P, RT, NB])
                    srow = sbuf(st, "srow", [RD, NB, RDIM])
                    lora = sbuf(st, "lora", [P, RDIM])
                    g2 = sbuf(st, "g2", [P, RDIM])
                    lastc = sbuf(st, "last_cols", [P, 1 + NB, RT])
                    lastr = sbuf(st, "last_rows", [(1 + NB) * RT, P])
                    dif = sbuf(st, "dif", [P, RT, TOK])
                    tw = sbuf(st, "tw", [64, TOK])
                    sg = sbuf(st, "sg", [P, TOK])
                    t1, t2, t3, t4, t5 = (dif[:, 4 * n:4 * n + 4, :] if n < 3 else sbuf(st, f"t{n}", [P, 4, TOK])[:, :, :] for n in range(5))
                    sh_in, s_in, lo_in = Signal(sem("shift_in")), Signal(sem("state_in")), Signal(sem("lora_in"))
                    (sh_full, lc_ready, lr_full, lr_ready, st_full, st_free, xs_ready, tg_ready, lo_full, lo_act, lo_dve, sq_ready,
                     kk_full, kk_var, kk_rstd, ex_in, ex_out, bo_ready, bo_full, ops_ready, row_full, row_free) = (sem(x) for x in (
                         "shift_turned", "last_ready", "last_turned", "last_rows_ready", "state_turned", "state_taken", "xs_ready",
                         "tanh_ready", "lora_full", "lora_act", "lora_dve", "kk_sq", "kk_sum", "kk_var", "kk_rstd", "exp_in",
                         "exp_out", "bonus_in", "bonus_sum", "operands_ready", "rows_turned", "rows_taken"))
                    with nc.Block() as block:
                        @block.sync
                        def _(sp):
                            load(sp, shrow[:, :], A["state_rwkv_shift"][0], sh_in)
                            load(sp, lora[0:64, :], A["rwkv_w2"][0], lo_in)
                            load(sp, lora[64:128, :], A["rwkv_a2"][0], lo_in)
                            load(sp, g2[:, :], A["rwkv_g2"][0], lo_in)
                            for b in range(NB):
                                load(sp, srow[:, b, :].rearrange("v (h k) -> v h k", h=RH), A["state_rwkv"][0, b].rearrange("h v k -> v h k"), s_in)
                            sp.wait_ge(lr_ready, 1)
                            store(sp, O["new_shift_prompt"][0].rearrange("b (c p) -> (b c) p", p=P), lastr[0:RT, :])
                            store(sp, O["new_shift_sample"][0].rearrange("b (c p) -> (b c) p", p=P), lastr[RT:(1 + NB) * RT, :])
                            sp.wait_ge(stored.sem, stored.n)

                        @block.vector
                        def _(v):
                            v.tensor_copy(lastc[:, 0, :], rwT[:, :, SEQ - 1])
                            dv(v, v.tensor_copy(lastc[:, 1:1 + NB, :], rwT[:, :, SEQ + DS - 1:TOK:DS].rearrange("p c b -> p b c")))
                            v.sem_inc(lc_ready, 1)
                            v.wait_ge(sh_full, 1)
                            dv(v, v.tensor_copy(shT[:, :, :], ps[0][:, 0:RT * NB].rearrange("p (c b) -> p c b", c=RT)))
                            rs = rwT[:, :, SEQ:TOK].rearrange("p c (b t) -> p c b t", b=NB)
                            ds = dif[:, :, SEQ:TOK].rearrange("p c (b t) -> p c b t", b=NB)
                            v.tensor_tensor(dif[:, :, 1:SEQ], rwT[:, :, 0:SEQ - 1], rwT[:, :, 1:SEQ], ALU.subtract)
                            v.tensor_scalar(dif[:, :, 0], rwT[:, :, 0], -1.0, None, ALU.mult)
                            v.tensor_tensor(ds[:, :, :, 1:DS], rs[:, :, :, 0:DS - 1], rs[:, :, :, 1:DS], ALU.subtract)
                            dv(v, v.tensor_tensor(ds[:, :, :, 0], shT[:, :, :], rs[:, :, :, 0], ALU.subtract))
                            for c in range(RT):
                                last = v.scalar_tensor_tensor(out=rwT[:, c, :], in0=dif[:, c, :], scalar=V("rwkv_mu", c), in1=rwT[:, c, :],
                                                              op0=ALU.mult, op1=ALU.add)
                            dv(v, last)
                            v.sem_inc(xs_ready, 1)
                            v.wait_ge(lr_full, 1)
                            v.tensor_copy(lastr[:, :], ps[1][0:(1 + NB) * RT, 0:P]).then_inc(lr_ready, 1)
                            kk, rT, kT, vT = t1, rwT[:, 0:4, :], rwT[:, 4:8, :], rwT[:, 8:12, :]
                            for c in range(4):
                                last = v.tensor_scalar(kk[:, c, :], kT[:, c, :], V("rwkv_k_k", c), None, ALU.mult)
                            dv(v, last)
                            dv(v, v.tensor_tensor(t2, kk, kk, ALU.mult))
                            v.sem_inc(sq_ready, 1)
                            v.wait_ge(kk_full, 1)
                            for c in range(4):
                                last = v.tensor_scalar(t2[:, c, :], ps[4 + c][:, 0:TOK], 1e-24, None, ALU.max)
                            dv(v, last)
                            v.sem_inc(kk_var, 1)
                            v.wait_ge(lo_act, 4)
                            for c in range(4):
                                last = v.tensor_tensor_scan(t4[:, c, :], C("reset_rw"), t3[:, c, :], 0.0, ALU.mult, ALU.add)
                            dv(v, last)
                            dv(v, v.tensor_tensor(t3, t4, t3, ALU.subtract))
                            v.sem_inc(ex_in, 1)
                            v.wait_ge(lo_act, 8)
                            for c in range(4):
                                last = v.tensor_scalar(bF[:, c, :], t5[:, c, :], 1.0, V("rwkv_k_a", c), ALU.subtract, ALU.mult)
                            dv(v, last)
                            dv(v, v.scalar_tensor_tensor(out=kT, in0=bF[:, :, :], scalar=1.0, in1=kT, op0=ALU.add, op1=ALU.mult))
                            v.wait_ge(kk_rstd, 1)
                            dv(v, v.reciprocal(t2, t2))
                            dv(v, v.tensor_tensor(kk, kk, t2, ALU.mult))
                            for c in range(4):
                                last = v.scalar_tensor_tensor(out=t2[:, c, :], in0=rT[:, c, :], scalar=V("rwkv_r_k", c), in1=kT[:, c, :],
                                                              op0=ALU.mult, op1=ALU.mult)
                            dv(v, last)
                            v.sem_inc(bo_ready, 1)
                            for c in range(4):
                                v.wait_ge(lo_full, 9 + c)
                                last = v.tensor_copy(gT[:, c, :], ps[c][:, 0:TOK])
                            dv(v, last)
                            v.wait_ge(ex_out, 3)
                            v.scalar_tensor_tensor(out=AR[:, :, 0, :], in0=kk, scalar=-1.0, in1=t3, op0=ALU.mult, op1=ALU.mult)
                            v.tensor_tensor(AR[:, :, 1, :], rT, bonus[:, :, :], ALU.mult)
                            v.tensor_copy(wend[:, :, :], bonus[:, :, RC - 1:SEQ:RC])
                            v.tensor_copy(wends[:, :, :], bonus[:, :, SEQ + DS - 1:TOK:DS])
                            dv(v, v.tensor_tensor(bF[:, :, :], kk, t5, ALU.mult))
                            dv(v, v.tensor_tensor(bF[:, :, :], bF[:, :, :], kF[:, :, :], ALU.mult))
                            dv(v, v.tensor_tensor(kF[:, :, :], kT, kF[:, :, :], ALU.mult))
                            v.sem_inc(ops_ready, 1)
                            v.wait_ge(bo_full, 1)
                            for c in range(4):
                                last = v.tensor_tensor(bonus[:, c, :], ps[4 + c][:, 0:TOK], vT[:, c, :], ALU.mult)
                            dv(v, last)
                            v.sem_inc(ops_ready, 1)
                            for n in range(9):
                                v.wait_ge(row_full, n + 1)
                                r = TILES[n % 3][1]
                                v.tensor_copy((rowB, rowK, rowV)[n // 3][0:r, n % 3, :], ps[n % 2][0:r, :]).then_inc(row_free, 1)

                        @block.scalar
                        def _(s):
                            s.wait_ge(xs_ready, 1)
                            s.activation(tw[:, :], rwT[0:64, 12, :], ACT.Tanh).then_inc(tg_ready, 1)
                            s.activation(sg[:, :], rwT[:, 13, :], ACT.Sigmoid).then_inc(tg_ready, 1)
                            for n in range(8):
                                s.wait_ge(lo_full, n + 1)
                                c = n % 4
                                dst, bias = (t3, "rwkv_w0") if n < 4 else (t5, "rwkv_a0")
                                ac(s, s.activation(dst[:, c, :], ps[c][:, 0:TOK], ACT.Sigmoid, bias=V(bias, c)))
                                s.sem_inc(lo_act, 1)
                            s.wait_ge(kk_var, 1)
                            ac(s, s.activation(t2, t2, ACT.Sqrt))
                            s.sem_inc(kk_rstd, 1)
                            s.wait_ge(ex_in, 1)
                            s.activation(bonus[:, :, :], t4, ACT.Exp, scale=-HALF_E).then_inc(ex_out, 1)
                            s.activation(kF[:, :, :], t4, ACT.Exp, scale=HALF_E).then_inc(ex_out, 1)
                            s.activation(t3, t3, ACT.Exp, scale=-HALF_E).then_inc(ex_out, 1)
                            for q in range(8):
                                s.wait_ge(st_full, q + 1)
                                s.activation(S0T[:, q, :, :], ps[2 + q % 2][:, 0:256].rearrange("p (c v) -> p c v", c=4), ACT.Copy).then_inc(st_free, 1)

                        @block.tensor
                        def _(t):
                            t.wait_ge(sh_in.sem, 16)
                            for c in range(RT):
                                mm = t.transpose(ps[0][:, c * NB:(c + 1) * NB], shrow[:, c * P:(c + 1) * P], C("ident", NB, 0, NB))
                            mm.then_inc(sh_full, 1)
                            t.wait_ge(lc_ready, 1)
                            t.transpose(ps[1][0:(1 + NB) * RT, 0:P], lastc[:, :, :].rearrange("p b c -> p (b c)"), C("ident")).then_inc(lr_full, 1)
                            t.wait_ge(sq_ready, 1)
                            for c in range(4):
                                mm = t.matmul(ps[4 + c][:, 0:TOK], C("head_ones"), t2[:, c, :], start=True, stop=True)
                            mm.then_inc(kk_full, 1)
                            t.wait_ge(tg_ready, 2)
                            t.wait_ge(lo_in.sem, 48)
                            t.wait_ge(lr_ready, 1)
                            for n in range(12):
                                c = n % 4
                                if n >= 4:
                                    t.wait_ge(lo_act, n - 3)
                                if n < 4:
                                    mm = t.matmul(ps[c][:, 0:TOK], lora[0:64, c * P:(c + 1) * P], tw[:, :], start=True, stop=True)
                                elif n < 8:
                                    mm = t.matmul(ps[c][:, 0:TOK], lora[64:128, c * P:(c + 1) * P], rwT[64:128, 12, :], start=True, stop=True)
                                else:
                                    mm = t.matmul(ps[c][:, 0:TOK], g2[:, c * P:(c + 1) * P], sg[:, :], start=True, stop=True)
                                mm.then_inc(lo_full, 1)
                            t.wait_ge(kk_var, 1)
                            t.wait_ge(bo_ready, 1)
                            for c in range(4):
                                mm = t.matmul(ps[4 + c][:, 0:TOK], C("head_ones"), t2[:, c, :], start=True, stop=True)
                            mm.then_inc(bo_full, 1)
                            t.wait_ge(ops_ready, 2)
                            t.wait_ge(s_in.sem, 16 * NB)
                            for n in range(9):
                                lo, r = TILES[n % 3]
                                if n >= 2:
                                    t.wait_ge(row_free, n - 1)
                                src = (bF, kF, rwT)[n // 3]
                                for c in range(4):
                                    mm = t.transpose(ps[n % 2][0:r, c * P:(c + 1) * P], src[:, (8 if n >= 6 else 0) + c, lo:lo + r], C("ident"))
                                mm.then_inc(row_full, 1)
                                if n < NB:
                                    if n >= 2:
                                        t.wait_ge(st_free, n - 1)
                                    for c in range(4):
                                        mm = t.transpose(ps[2 + n % 2][:, c * RD:(c + 1) * RD], srow[:, n, c * P:(c + 1) * P], C("ident", RD, 0, RD))
                                    mm.then_inc(st_full, 1)

                BM = sbuf(rk, "BM", [P, 3, RH, 2, P])
                KM = sbuf(rk, "KM", [P, 3, RH, 2, P])
                XT = sbuf(rk, "XT", [P, 3, RH, P])
                with ExitStack() as st:
                    X = sbuf(st, "X", [P, RH, P])
                    T1 = sbuf(st, "T1", [P, RH, P])
                    prod_full, prod_free, xt_ready, x_full, x_ready, t_full, t_ready, d_full, d_ready = (sem(x) for x in (
                        "prod_full", "prod_free", "xt_ready", "x_turned", "x_ready", "t_full", "t_ready", "d_full", "d_ready"))
                    LEVELS = [[2, 4, 8, 16, 32], [2, 4, 8, 16, 32], [2, 4]]
                    with nc.Block() as block:
                        @block.tensor
                        def _(t):
                            n = xn = tn = dn = 0
                            for i, (lo, r) in enumerate(TILES):
                                for src in (bF, kF):
                                    for pr in range(4):
                                        if n >= 2:
                                            t.wait_ge(prod_free, n - 1)
                                        h0 = 64 * (pr % 2)
                                        for q in range(2):
                                            p2 = 2 * (pr // 2) + q
                                            mm = t.matmul(ps[n % 2][0:r, q * 256:(q + 1) * 256].rearrange("p (a t) -> p a t", a=2)[:, :, 0:r],
                                                          src[h0:h0 + 64, p2, lo:lo + r], AR[h0:h0 + 64, p2, :, lo:lo + r], start=True, stop=True)
                                        mm.then_inc(prod_full, 1)
                                        n += 1
                                for g in range(2):
                                    xn += 1
                                    t.wait_ge(xt_ready, xn)
                                    for q in range(4):
                                        mm = t.transpose(ps[2 + g][0:r, q * P:q * P + r], XT[0:r, i, 4 * g + q, 0:r], C("ident", r, 0, r))
                                    mm.then_inc(x_full, 1)
                                for li, s_ in enumerate(LEVELS[i]):
                                    lastlev = li == len(LEVELS[i]) - 1
                                    for g in range(2):
                                        t.wait_ge(x_ready, xn - 1 + g)
                                        if li:
                                            t.wait_ge(d_ready, dn - 1 + g)
                                        for q in range(4):
                                            h = 4 * g + q
                                            mm = t.matmul(ps[2 + g][0:r, q * P:q * P + r], BM[0:r, i, h, 0, 0:r], X[0:r, h, 0:r], start=True, stop=True)
                                        mm.then_inc(t_full, 1)
                                    for g in range(2):
                                        tn += 1
                                        t.wait_ge(t_ready, tn)
                                        for q in range(4):
                                            h = 4 * g + q
                                            if not lastlev:
                                                t.matmul(ps[4 + g][0:r, q * P:q * P + r], XT[0:r, i, h, 0:r], T1[0:r, h, 0:r], start=True, stop=True)
                                            mm = t.matmul(ps[6 + g][0:r, q * P:q * P + r], T1[0:r, h, 0:r], XT[0:r, i, h, 0:r], start=True, stop=True)
                                        mm.then_inc(d_full, 1)
                                        dn += 1

                        @block.vector
                        def _(v):
                            n = xn = tn = dn = 0
                            for i, (lo, r) in enumerate(TILES):
                                mask = "rw_T" if i < 2 else "sm_T"
                                m3 = C(mask, r).rearrange("p (o a t) -> p o a t", o=1, a=2)[:, :, :, 0:r]
                                for dst in (BM, KM):
                                    for pr in range(4):
                                        n += 1
                                        v.wait_ge(prod_full, n)
                                        for q in range(2):
                                            last = v.tensor_tensor(dst[0:r, i, 4 * (pr // 2) + 2 * q + pr % 2, :, 0:r],
                                                                   ps[(n - 1) % 2][0:r, q * 256:(q + 1) * 256].rearrange("p (a t) -> p a t", a=2)[:, :, 0:r],
                                                                   m3[:, 0], ALU.mult)
                                        dv(v, last)
                                        v.sem_inc(prod_free, 1)
                                dv(v, v.tensor_tensor(XT[0:r, i, :, 0:r], BM[0:r, i, :, 0, 0:r],
                                                      C("lev1_T", r, 0, r).rearrange("p (o t) -> p o t", o=1).to_broadcast([r, RH, r]), ALU.mult))
                                for g in range(2):
                                    dv(v, v.tensor_tensor(XT[0:r, i, 4 * g:4 * g + 4, 0:r], XT[0:r, i, 4 * g:4 * g + 4, 0:r],
                                                          C("ident", r, 0, r).rearrange("p (o t) -> p o t", o=1).to_broadcast([r, 4, r]), ALU.add))
                                    v.sem_inc(xt_ready, 1)
                                for g in range(2):
                                    xn += 1
                                    v.wait_ge(x_full, xn)
                                    dv(v, v.tensor_copy(X[0:r, 4 * g:4 * g + 4, 0:r], ps[2 + g][0:r, :].rearrange("p (q t) -> p q t", q=4)[:, :, 0:r]))
                                    v.sem_inc(x_ready, 1)
                                for li, s_ in enumerate(LEVELS[i]):
                                    lastlev = li == len(LEVELS[i]) - 1
                                    for g in range(2):
                                        tn += 1
                                        v.wait_ge(t_full, tn)
                                        v.tensor_tensor(T1[0:r, 4 * g:4 * g + 4, 0:r], ps[2 + g][0:r, :].rearrange("p (q t) -> p q t", q=4)[:, :, 0:r],
                                                        C(f"lev{s_}", r, 0, r).rearrange("p (o t) -> p o t", o=1).to_broadcast([r, 4, r]),
                                                        ALU.mult).then_inc(t_ready, 1)
                                    for g in range(2):
                                        dn += 1
                                        v.wait_ge(d_full, dn)
                                        if not lastlev:
                                            v.tensor_tensor(X[0:r, 4 * g:4 * g + 4, 0:r], X[0:r, 4 * g:4 * g + 4, 0:r],
                                                            ps[4 + g][0:r, :].rearrange("p (q t) -> p q t", q=4)[:, :, 0:r], ALU.add)
                                        dv(v, v.tensor_tensor(XT[0:r, i, 4 * g:4 * g + 4, 0:r], XT[0:r, i, 4 * g:4 * g + 4, 0:r],
                                                              ps[6 + g][0:r, :].rearrange("p (q t) -> p q t", q=4)[:, :, 0:r], ALU.add))
                                        v.sem_inc(d_ready, 1)

                with ExitStack() as st:
                    NCH = SEQ // RC
                    YB = (4, 7)
                    ST = sbuf(st, "ST", [P, NCH + 1, 4, RD])
                    rhs_s = sbuf(st, "rhs", [P, RDIM])
                    U = sbuf(st, "U", [P, RDIM])
                    SY = sbuf(st, "SY", [P, 4, 2, 64])
                    rhs2 = sbuf(st, "rhs2", [64, RDIM])
                    U2 = sbuf(st, "U2", [64, RDIM])
                    ub = sbuf(st, "ub", [64, 2, NB, RD])
                    vb = sbuf(st, "vb", [64, 2, NB, RD])
                    SN = S0T
                    NR = 3
                    srow2 = sbuf(st, "srow2", [RD, NR, RDIM])
                    row_out = [Signal(sem(f"row_out{n}")) for n in range(NR)]
                    y_copied = sem("y_copied")
                    (st0, r_full, r_ready, u_full, u_ready, s_full, s_ready, y_full, y_ready, sy_full, sy_ready, tr_full, mv_full, r2_ready,
                     u2_full, u2_ready, y2_full, y2_ready, blk_ready, n_full, n_ready, o_full, o_ready) = (sem(x) for x in (
                         "state0", "rhs_full", "rhs_ready", "u_full", "u_ready", "s_full", "s_ready", "y_full", "y_ready", "sy_full",
                         "sy_ready", "sy_turned", "mv_full", "rhs2_ready", "u2_full", "u2_ready", "y2_full", "y2_ready", "blk_ready",
                         "new_full", "new_ready", "row_full", "row_ready"))
                    with nc.Block() as block:
                        @block.tensor
                        def _(t):
                            def sample_reads():
                                for h in range(RH):
                                    h0, pr = 64 * (h % 2), h // 2
                                    out = ps[5 + h % 2][h0:h0 + 64, pr * P:(pr + 1) * P].rearrange("p (a t) -> p a t", a=2)
                                    for b in range(NB):
                                        mm = t.matmul(out[:, :, b * DS:(b + 1) * DS], S0T[h0:h0 + 64, b, pr, :],
                                                      AR[h0:h0 + 64, pr, :, SEQ + b * DS:SEQ + (b + 1) * DS], start=True, stop=True)
                                mm.then_inc(sy_full, 1)
                            sample_reads()
                            t.wait_ge(st0, 1)
                            for c in range(NCH):
                                i, off = c // 2, RC * (c % 2)
                                js = slice(off, off + RC)
                                if c:
                                    t.wait_ge(s_ready, c)
                                for h in range(RH):
                                    h0, pr = 64 * (h % 2), h // 2
                                    own = h % 2 == c % 2
                                    t.matmul(ps[h % 2][js, h * RD:(h + 1) * RD], AR[h0:h0 + 64, pr, 0, c * RC:(c + 1) * RC], ST[h0:h0 + 64, c, pr, :], start=True, stop=not own)
                                    mm = t.matmul(ps[c % 2][js, h * RD:(h + 1) * RD], KM[js, i, h, 0, js], rowV[js, i, h * RD:(h + 1) * RD], start=not own, stop=True)
                                mm.then_inc(r_full, 1)
                                t.wait_ge(r_ready, c + 1)
                                for h in range(RH):
                                    mm = t.matmul(ps[2][js, h * RD:(h + 1) * RD], XT[js, i, h, js], rhs_s[js, h * RD:(h + 1) * RD], start=True, stop=True)
                                mm.then_inc(u_full, 1)
                                t.wait_ge(u_ready, c + 1)
                                for h in range(RH):
                                    h0, pr = 64 * (h % 2), h // 2
                                    out = ps[3][h0:h0 + 64, pr * RD:(pr + 1) * RD]
                                    t.matmul(out, rowB[js, i, h * RD:(h + 1) * RD], U[js, h * RD:(h + 1) * RD], start=True, stop=False)
                                    mm = t.matmul(out, rowK[js, i, h * RD:(h + 1) * RD], rowV[js, i, h * RD:(h + 1) * RD], start=False, stop=True)
                                mm.then_inc(s_full, 1)
                                if c >= 1:
                                    t.wait_ge(y_ready, c)
                                for h in range(RH):
                                    h0, pr = 64 * (h % 2), h // 2
                                    own = h % 2 == c % 2
                                    out = ps[YB[c % 2]][h0:h0 + 64, pr * RC:(pr + 1) * RC]
                                    t.matmul(ps[YB[h % 2]][h0:h0 + 64, pr * RC:(pr + 1) * RC], ST[h0:h0 + 64, c, pr, :], AR[h0:h0 + 64, pr, 1, c * RC:(c + 1) * RC],
                                             start=True, stop=not own)
                                    t.matmul(out, U[js, h * RD:(h + 1) * RD], BM[js, i, h, 1, js], start=not own, stop=False)
                                    mm = t.matmul(out, rowV[js, i, h * RD:(h + 1) * RD], KM[js, i, h, 1, js], start=False, stop=True)
                                mm.then_inc(y_full, 1)
                            t.wait_ge(sy_ready, 2)
                            t.wait_ge(y_ready, NCH)
                            for pr in range(4):
                                mm = t.transpose(ps[6][0:64, pr * P:(pr + 1) * P], SY[:, pr, 0, :], C("ident"))
                            mm.then_inc(tr_full, 1)
                            for h in range(RH):
                                mm = t.matmul(ps[7][0:64, h * RD:(h + 1) * RD], KM[0:64, 2, h, 0, 0:64], rowV[0:64, 2, h * RD:(h + 1) * RD], start=True, stop=True)
                            mm.then_inc(mv_full, 1)
                            t.wait_ge(r2_ready, 1)
                            for h in range(RH):
                                mm = t.matmul(ps[6][0:64, h * RD:(h + 1) * RD], XT[0:64, 2, h, 0:64], rhs2[:, h * RD:(h + 1) * RD], start=True, stop=True)
                            mm.then_inc(u2_full, 1)
                            t.wait_ge(u2_ready, 1)
                            for h in range(RH):
                                h0, pr = 64 * (h % 2), h // 2
                                out = ps[7][h0:h0 + 64, pr * 64:(pr + 1) * 64]
                                t.matmul(out, U2[:, h * RD:(h + 1) * RD], BM[0:64, 2, h, 1, 0:64], start=True, stop=False)
                                mm = t.matmul(out, rowV[0:64, 2, h * RD:(h + 1) * RD], KM[0:64, 2, h, 1, 0:64], start=False, stop=True)
                            mm.then_inc(y2_full, 1)
                            for h in range(RH):
                                h0, pr = 64 * (h % 2), h // 2
                                t.wait_ge(blk_ready, h + 1)
                                if h % 2 == 0 and pr >= 2:
                                    t.wait_ge(n_ready, pr - 1)
                                out = ps[0 + pr % 2][h0:h0 + 64, :]
                                t.matmul(out, rowB[0:64, 2, h * RD:(h + 1) * RD], ub[:, h % 2, :, :].rearrange("p b v -> p (b v)"), start=True, stop=False)
                                mm = t.matmul(out, rowK[0:64, 2, h * RD:(h + 1) * RD], vb[:, h % 2, :, :].rearrange("p b v -> p (b v)"), start=False, stop=True)
                                mm.then_inc(n_full, 1)
                            t.wait_ge(s_ready, NCH)
                            t.wait_ge(n_ready, 4)
                            t.wait_ge(y_ready, NCH)
                            for n in range(1 + NB):
                                if n >= 2:
                                    t.wait_ge(o_ready, n - 1)
                                for pr in range(4):
                                    src = ST[:, NCH, pr, :] if n == 0 else SN[:, n - 1, pr, :]
                                    mm = t.transpose(ps[2 + n % 2][0:RD, pr * P:(pr + 1) * P], src, C("ident"))
                                mm.then_inc(o_full, 1)

                        @block.vector
                        def _(v):
                            dv(v, v.memset(ST[:, 0, :, :], 0.0))
                            v.sem_inc(st0, 1)
                            yv = mixT[:, 4:8, :]

                            def y_add(c):
                                h0 = 64 * ((c + 1) % 2)
                                v.wait_ge(y_copied, c + 1)
                                v.tensor_tensor(yv[h0:h0 + 64, :, c * RC:(c + 1) * RC], yv[h0:h0 + 64, :, c * RC:(c + 1) * RC],
                                                ps[YB[(c + 1) % 2]][h0:h0 + 64, 0:256].rearrange("p (c t) -> p c t", c=4), ALU.add).then_inc(y_ready, 1)
                            for c in range(NCH):
                                js = slice(RC * (c % 2), RC * (c % 2) + RC)
                                v.wait_ge(r_full, c + 1)
                                dv(v, v.tensor_copy(rhs_s[js, :], ps[c % 2][js, :]))
                                other = (c + 1) % 2
                                rv, pv_ = (x[js, :].rearrange("p (c a v) -> p c a v", c=4, a=2)[:, :, other, :] for x in (rhs_s, ps[other]))
                                v.tensor_tensor(rv, rv, pv_, ALU.add).then_inc(r_ready, 1)
                                v.wait_ge(u_full, c + 1)
                                v.tensor_copy(U[js, :], ps[2][js, :]).then_inc(u_ready, 1)
                                v.wait_ge(s_full, c + 1)
                                dv(v, v.tensor_tensor(ST[:, c + 1, :, :], ST[:, c, :, :], ps[3][:, 0:256].rearrange("p (c v) -> p c v", c=4), ALU.add))
                                dv(v, v.tensor_tensor(ST[:, c + 1, :, :], ST[:, c + 1, :, :], wend[:, :, c:c + 1].to_broadcast([P, 4, RD]), ALU.mult))
                                v.sem_inc(s_ready, 1)
                                if c:
                                    y_add(c - 1)
                            y_add(NCH - 1)
                            v.wait_ge(sy_ready, 2)
                            v.wait_ge(tr_full, 1)
                            dv(v, v.tensor_copy(rhs2[:, :], ps[6][0:64, :]))
                            v.wait_ge(mv_full, 1)
                            v.tensor_tensor(rhs2[:, :], rhs2[:, :], ps[7][0:64, :], ALU.add).then_inc(r2_ready, 1)
                            v.wait_ge(u2_full, 1)
                            dv(v, v.tensor_copy(U2[:, :], ps[6][0:64, :]))
                            v.sem_inc(u2_ready, 1)
                            v.wait_ge(y2_full, 1)
                            v.tensor_tensor(yv[:, :, SEQ:TOK], SY[:, :, 1, :], ps[7][:, 0:256].rearrange("p (c t) -> p c t", c=4), ALU.add)
                            sel = C("bsel", 64).rearrange("p (b o) -> p b o", o=1).to_broadcast([64, NB, RD])
                            for h in range(RH):
                                if h >= 2:
                                    v.wait_ge(n_full, h - 1)
                                v.tensor_tensor(ub[:, h % 2, :, :], U2[:, h * RD:(h + 1) * RD].rearrange("p (o v) -> p o v", o=1).to_broadcast([64, NB, RD]), sel, ALU.mult)
                                v.tensor_tensor(vb[:, h % 2, :, :], rowV[0:64, 2, h * RD:(h + 1) * RD].rearrange("p (o v) -> p o v", o=1).to_broadcast([64, NB, RD]), sel,
                                                ALU.mult).then_inc(blk_ready, 1)
                                if h % 2:
                                    pr = h // 2
                                    v.wait_ge(n_full, h + 1)
                                    dv(v, v.tensor_tensor(SN[:, :, pr, :], S0T[:, :, pr, :], ps[pr % 2][:, :].rearrange("p (b v) -> p b v", b=NB), ALU.add))
                                    dv(v, v.tensor_tensor(SN[:, :, pr, :], SN[:, :, pr, :], wends[:, pr, :].rearrange("p (b o) -> p b o", o=1).to_broadcast([P, NB, RD]), ALU.mult))
                                    v.sem_inc(n_ready, 1)

                        @block.scalar
                        def _(s):
                            s.wait_ge(sy_full, 1)
                            for q in range(2):
                                s.activation(SY[64 * q:64 * q + 64, :, :, :], ps[5 + q][64 * q:64 * q + 64, :].rearrange("p (c a t) -> p c a t", c=4, a=2),
                                             ACT.Copy).then_inc(sy_ready, 1)
                            for c in range(NCH):
                                s.wait_ge(y_full, c + 1)
                                s.activation(mixT[:, 4:8, c * RC:(c + 1) * RC], ps[YB[c % 2]][:, 0:256].rearrange("p (c t) -> p c t", c=4), ACT.Copy).then_inc(y_copied, 1)
                            for n in range(1 + NB):
                                s.wait_ge(o_full, n + 1)
                                if n >= NR:
                                    s.wait_ge(row_out[n % NR].sem, 16 * (n // NR))
                                s.activation(srow2[:, n % NR, :], ps[2 + n % 2][0:RD, :], ACT.Copy).then_inc(o_ready, 1)

                        @block.sync
                        def _(sp):
                            for n in range(1 + NB):
                                sp.wait_ge(o_ready, n + 1)
                                dst = O["new_rwkv_prompt"][0, 0] if n == 0 else O["new_rwkv_sample"][0, n - 1]
                                load(sp, dst.rearrange("h v k -> v h k"), srow2[:, n % NR, :].rearrange("v (h k) -> v h k", h=RH), row_out[n % NR])
                            for n in range(NR):
                                sp.wait_ge(row_out[n].sem, row_out[n].n)

                with ExitStack() as st:
                    y = mixT[:, 4:8, :]
                    yc = sbuf(st, "yc", [P, 4, TOK])
                    sq = sbuf(st, "ysq", [P, 4, TOK])
                    m_full, q_ready, v_full, v_ready, w_ready = (sem(x) for x in ("mean_full", "ysq_ready", "var_full", "var_ready", "yrstd_ready"))
                    with nc.Block() as block:
                        @block.tensor
                        def _(t):
                            for c in range(4):
                                mm = t.matmul(ps[c][:, 0:TOK], C("head_ones"), y[:, c, :], start=True, stop=True)
                                mm.then_inc(m_full, 1)
                            for c in range(4):
                                t.wait_ge(q_ready, c + 1)
                                t.matmul(ps[4 + c][:, 0:TOK], C("head_ones"), sq[:, c, :], start=True, stop=True).then_inc(v_full, 1)

                        @block.vector
                        def _(v):
                            for c in range(4):
                                v.wait_ge(m_full, c + 1)
                                dv(v, v.scalar_tensor_tensor(out=yc[:, c, :], in0=ps[c][:, 0:TOK], scalar=-1.0 / RD, in1=y[:, c, :], op0=ALU.mult, op1=ALU.add))
                                v.tensor_tensor(sq[:, c, :], yc[:, c, :], yc[:, c, :], ALU.mult).then_inc(q_ready, 1)
                            for c in range(4):
                                v.wait_ge(v_full, c + 1)
                                v.tensor_scalar(sq[:, c, :], ps[4 + c][:, 0:TOK], 1.0 / RD, LN_EPS, ALU.mult, ALU.add).then_inc(v_ready, 1)
                            for c in range(4):
                                v.wait_ge(w_ready, c + 1)
                                dv(v, v.reciprocal(sq[:, c, :], sq[:, c, :]))
                                dv(v, v.tensor_tensor(yc[:, c, :], yc[:, c, :], sq[:, c, :], ALU.mult))
                                dv(v, v.tensor_scalar(yc[:, c, :], yc[:, c, :], V("rwkv_ln_g", c), V("rwkv_ln_b", c), ALU.mult, ALU.add))
                                dv(v, v.tensor_tensor(yc[:, c, :], yc[:, c, :], bonus[:, c, :], ALU.add))
                                dv(v, v.tensor_tensor(y[:, c, :], yc[:, c, :], gT[:, c, :], ALU.mult))

                        @block.scalar
                        def _(s):
                            for c in range(4):
                                s.wait_ge(v_ready, c + 1)
                                s.activation(sq[:, c, :], sq[:, c, :], ACT.Sqrt).then_inc(w_ready, 1)

        def out_projection(name, w_dram):
            def add_to(dst):
                return lambda v, bank: v.tensor_tensor(dst, dst, bank, ALU.add)
            projection(name, w_dram, [(c, 256) for c in range(0, D, 256)],
                       [(m // 2, m % 2 * P, P, None, "dve", add_to(xT[:, m, :])) for m in range(DC)], mixT)

        next_part()
        out_projection("out_even", A["w_out_even"][0])

        with ExitStack() as st:
            HALF = 2048
            NS = 4
            NSP = 3
            KG = DC // 2
            FC = DFF // P
            GU = DFF // 256
            PIECES = 2 * GU + FC // 2
            assert FC % 2 == 0
            ring = sbuf(st, "ring", [P, NS, HALF])
            whi = sbuf(st, "w_hi", [P, NSP, HALF], F32R)
            wlo = sbuf(st, "w_lo", [P, NSP, HALF], F32R)
            xhi = sbuf(st, "x_hi", [P, DC, TOK], F32R)
            xlo = sbuf(st, "x_lo", [P, DC, TOK], F32R)
            hhi = sbuf(st, "hid_hi", [P, FC, TOK], F32R)
            hlo = sbuf(st, "hid_lo", [P, FC, TOK], F32R)
            hid = sbuf(st, "hid", [P, TOK])
            sil = sbuf(st, "sil", [P, 2, TOK])
            n_dve, n_pe, n_act = rms_steps("ffn", xT[:, :, :], DC, V("norm_ffn_even", 0, 8), hT, D, scratch=mixT)
            landed = [sem(f"ffn_landed{n}") for n in range(NS)]
            x_split, hi_ready, split, used, sil_ready, hid_ready, dn_full = (sem(x) for x in (
                "ffn_x_split", "hi_ready", "piece_split", "piece_used", "sil_ready", "hid_ready", "down_full"))
            with nc.Block() as block:
                @block.sync
                def _(sp):
                    gu = A["ffn_w_gu_even"][0].rearrange("(c p) (a n) -> p c a n", p=P, a=2)
                    dn = A["ffn_w_down_even"][0].rearrange("(c p) n -> p c n", p=P)
                    for i in range(PIECES):
                        if i >= NS:
                            sp.wait_ge(split, i - NS + 1)
                        if i < 2 * GU:
                            g, half = divmod(i, 2)
                            for a in range(2):
                                sp.dma_start(ring[:, i % NS, :].rearrange("p (c a n) -> p c a n", c=KG, a=2)[:, :, a, :],
                                             gu[:, KG * half:KG * (half + 1), a, g * 256:(g + 1) * 256]).then_inc(landed[i % NS], 16)
                        else:
                            k = 2 * (i - 2 * GU)
                            sp.dma_start(ring[:, i % NS, :].rearrange("p (c n) -> p c n", c=2), dn[:, k:k + 2, :]).then_inc(landed[i % NS], 32)

                @block.tensor
                def _(t):
                    n_pe(t)
                    for i in range(2 * GU):
                        g, half = divmod(i, 2)
                        if g == 0:
                            t.wait_ge(x_split, half + 1)
                        t.wait_ge(split, i + 1)
                        if half == 0 and g >= 2:
                            t.wait_ge(hid_ready, 2 * (g - 1))
                        w_hi, w_lo = (x[:, i % NSP, :].rearrange("p (c a n) -> p c a n", c=KG, a=2) for x in (whi, wlo))
                        for j in range(2):
                            for a in range(2):
                                for q in range(KG):
                                    k = KG * half + q
                                    mm = product(t, ps[4 * (g % 2) + 2 * j + a][:, 0:TOK], w_hi[:, q, a, j * P:(j + 1) * P], w_lo[:, q, a, j * P:(j + 1) * P],
                                                 xhi[:, k, :], xlo[:, k, :], k == 0, k == DC - 1)
                        mm.then_inc(used, 1)
                    t.wait_ge(hid_ready, FC)
                    for i in range(2 * GU, PIECES):
                        t.wait_ge(split, i + 1)
                        for q in range(2):
                            k = 2 * (i - 2 * GU) + q
                            for m in range(DC):
                                cols = slice(q * D + m * P, q * D + (m + 1) * P)
                                mm = product(t, ps[m][:, 0:TOK], whi[:, i % NSP, cols], wlo[:, i % NSP, cols], hhi[:, k, :], hlo[:, k, :], k == 0, k == FC - 1)
                                if k == FC - 1 and m < DC - 1:
                                    mm.then_inc(dn_full, 1)
                        mm.then_inc(used, 1)

                @block.scalar
                def _(s):
                    n_act(s)
                    for i in range(PIECES):
                        if i >= NSP:
                            s.wait_ge(used, i - NSP + 1)
                        g = i // 2 - 2
                        if i % 2 == 0 and 0 <= g < GU:
                            for j in range(2):
                                n = 2 * g + j
                                if n >= 2:
                                    s.wait_ge(hid_ready, n - 1)
                                s.activation(sil[:, j, :], ps[4 * (g % 2) + 2 * j][:, 0:TOK], ACT.Silu).then_inc(sil_ready, 1)
                        s.wait_ge(landed[i % NS], 32 * (i // NS + 1))
                        s.activation(whi[:, i % NSP, :], ring[:, i % NS, :], ACT.Copy).then_inc(hi_ready, 1)

                @block.vector
                def _(v):
                    n_dve(v)
                    for i in range(PIECES):
                        g = i // 2 - 2
                        if i % 2 == 0 and 0 <= g < GU:
                            for j in range(2):
                                n = 2 * g + j
                                v.wait_ge(sil_ready, n + 1)
                                dv(v, v.tensor_tensor(hid[:, :], sil[:, j, :], ps[4 * (g % 2) + 2 * j + 1][:, 0:TOK], ALU.mult))
                                dv(v, v.tensor_copy(hhi[:, n, :], hid[:, :]))
                                v.tensor_tensor(hlo[:, n, :], hid[:, :], hhi[:, n, :].bitcast(F32), ALU.subtract).then_inc(hid_ready, 1)
                                v.wait_ge(hid_ready, n + 1)
                        if i < 2:
                            part = slice(KG * i, KG * (i + 1))
                            dv(v, v.tensor_copy(xhi[:, part, :], hT[:, part, :]))
                            v.tensor_tensor(xlo[:, part, :], hT[:, part, :], xhi[:, part, :].bitcast(F32), ALU.subtract).then_inc(x_split, 1)
                        v.wait_ge(hi_ready, i + 1)
                        v.tensor_tensor(wlo[:, i % NSP, :], ring[:, i % NS, :], whi[:, i % NSP, :].bitcast(F32), ALU.subtract).then_inc(split, 1)
                    for m in range(DC):
                        if m < DC - 1:
                            v.wait_ge(dn_full, m + 1)
                        else:
                            v.wait_ge(used, PIECES)
                        last = v.tensor_tensor(xT[:, m, :], xT[:, m, :], ps[m][:, 0:TOK], ALU.add)
                    dv(v, last)

        with ExitStack() as od:
            qT = sbuf(od, "qT", [P, GH, TOK])
            kT = sbuf(od, "kT", [P, GH, TOK])
            gS = sbuf(od, "gS", [P, DC, TOK])
            xaT = sbuf(od, "xaT", [GRANK, TOK])
            rowV = sbuf(od, "rowV", [P, 3, GV])
            with ExitStack() as st:
                sq = sbuf(st, "sq", [P, DC, TOK])
                norm = rms_steps("oddn", xT[:, :, :], DC, V("norm_mix_odd", 0, 8), hT, D, scratch=sq)
                at_v, at_g = 2 * GK, 2 * GK + GV
                pieces = [(c, 256) for c in list(range(0, at_v, 256)) + list(range(at_g, at_g + GV, 256)) + list(range(at_v, at_g, 256))]
                pieces.append((ODD_IN - GRANK, GRANK))
                dest = [qT[:, k, :] for k in range(4)] + [kT[:, k, :] for k in range(4)] + [gS[:, k, :] for k in range(8)]
                outs = [(k // 2, k % 2 * P, P, None, dest[k]) for k in range(16)]
                outs += [(8 + g, 0, 256, i, rowV[0:TILES[i][1], i, g * 256:(g + 1) * 256]) for g in range(4) for i in range(3)]
                outs.append((12, 0, GRANK, None, xaT[:, :]))
                projection("podd", A["w_in_odd"][0], pieces,
                           [o[:4] + (("act", "dve")[n % 2], copy_to(o[4])) for n, o in enumerate(outs)], hT, norm)

            with ExitStack() as st:
                AT = sbuf(st, "AT", [P, 3, GH, P])
                qb = sbuf(st, "qb", [P, GH, TOK])
                rowE = sbuf(st, "rowE", [P, 3, GK])
                bend = sbuf(st, "bend", [P, GH, SEQ // GC])
                bends = sbuf(st, "bends", [P, GH, NB])
                Ss = sbuf(st, "Ss", [P, NB, GH, DV])
                ss_in = Signal(sem("ss_in"))
                oT = mixT
                with ExitStack() as s2:
                    ga2 = sbuf(s2, "ga2", [GRANK, GK])
                    t1, t2, t3, t4 = (sbuf(s2, f"g{n}", [P, GH, TOK]) for n in range(4))
                    ga_in, z_full, ab_ready, ln_ready, ex_in, ex_out, mm_ready, at_full, at_free, row_full, row_free, o_full, o_free, sg_ready = (sem(x) for x in (
                        "ga_in", "z_full", "absz_ready", "ln_ready", "gexp_in", "gexp_out", "gops_ready", "at_full", "at_free",
                        "grow_full", "grow_free", "o_full", "o_free", "silu_ready"))
                    with nc.Block() as block:
                        @block.sync
                        def _(sp):
                            sp.dma_start(ga2[:, :], A["gla_a2"][0]).then_inc(ga_in, 16)
                            for b in range(NB):
                                load(sp, Ss[:, b, :, :], A["state_gla"][0, b].rearrange("h k v -> k h v"), ss_in)

                        @block.vector
                        def _(v):
                            v.wait_ge(z_full, 1)
                            for c in range(GH):
                                last = v.tensor_scalar(t1[:, c, :], ps[c][:, 0:TOK], V("gla_ab", c), None, ALU.add)
                            dv(v, last)
                            dv(v, v.scalar_tensor_tensor(out=t2[:, :, :], in0=t1[:, :, :], scalar=-1.0, in1=t1[:, :, :], op0=ALU.mult, op1=ALU.max))
                            v.sem_inc(ab_ready, 1)
                            v.wait_ge(ln_ready, 1)
                            dv(v, v.scalar_tensor_tensor(out=t1[:, :, :], in0=t1[:, :, :], scalar=0.0, in1=t2[:, :, :], op0=ALU.min, op1=ALU.subtract))
                            for c in range(GH):
                                last = v.tensor_tensor_scan(t2[:, c, :], C("reset_gla"), t1[:, c, :], 0.0, ALU.mult, ALU.add)
                            dv(v, last)
                            b32 = t2[:, :, :].rearrange("p h (c t) -> p (h c) t", t=GC)
                            dv(v, v.tensor_tensor(t3[:, :, :].rearrange("p h (c t) -> p (h c) t", t=GC), b32,
                                                  b32[:, :, GC // 2 - 1:GC // 2].to_broadcast([P, GH * TOK // GC, GC]), ALU.subtract))
                            dv(v, v.tensor_scalar(t3[:, :, :], t3[:, :, :], 80.0 * 16, -80.0 * 16, ALU.min, ALU.max))
                            for h in range(GH):
                                bp = t2[:, h, 0:SEQ].rearrange("p (c t) -> p c t", t=GC)
                                v.tensor_tensor(t4[:, h, 0:SEQ].rearrange("p (c t) -> p c t", t=GC), bp[:, :, GC - 1:GC].to_broadcast([P, SEQ // GC, GC]), bp, ALU.subtract)
                                bs = t2[:, h, SEQ:TOK].rearrange("p (c t) -> p c t", t=DS)
                                last = v.tensor_tensor(t4[:, h, SEQ:TOK].rearrange("p (c t) -> p c t", t=DS), bs[:, :, DS - 1:DS].to_broadcast([P, NB, DS]), bs, ALU.subtract)
                            dv(v, last)
                            v.sem_inc(ex_in, 1)
                            v.wait_ge(ex_out, 1)
                            dv(v, v.scalar_tensor_tensor(out=t1[:, :, :], in0=qT[:, :, :], scalar=float(DK ** -0.5), in1=t1[:, :, :], op0=ALU.mult, op1=ALU.mult))
                            v.wait_ge(ex_out, 2)
                            dv(v, v.tensor_tensor(t3[:, :, :], kT[:, :, :], t3[:, :, :], ALU.mult))
                            v.sem_inc(mm_ready, 1)
                            v.wait_ge(ex_out, 3)
                            dv(v, v.tensor_tensor(t4[:, :, :], kT[:, :, :], t4[:, :, :], ALU.mult))
                            v.sem_inc(mm_ready, 1)
                            v.wait_ge(ex_out, 4)
                            v.tensor_copy(bend[:, :, :], t2[:, :, GC - 1:SEQ:GC])
                            v.tensor_copy(bends[:, :, :], t2[:, :, SEQ + DS - 1:TOK:DS])
                            dv(v, v.scalar_tensor_tensor(out=qb[:, :, :], in0=qT[:, :, :], scalar=float(DK ** -0.5), in1=t2[:, :, :], op0=ALU.mult, op1=ALU.mult))
                            for i, (lo, r) in enumerate(TILES):
                                v.wait_ge(at_full, i + 1)
                                m = C("gla_T", r, 0, r) if i < 2 else C("sm_T", r, P, P + r)
                                v.tensor_tensor(AT[0:r, i, :, 0:r], ps[4 + i % 2][0:r, :].rearrange("p (h t) -> p h t", h=GH)[:, :, 0:r],
                                                m.rearrange("p (o t) -> p o t", o=1).to_broadcast([r, GH, r]), ALU.mult).then_inc(at_free, 1)
                            for n in range(DC):
                                v.wait_ge(o_full, n + 1)
                                v.tensor_copy(oT[:, n, :], ps[n % 4][:, 0:TOK]).then_inc(o_free, 1)

                        @block.scalar
                        def _(s):
                            s.wait_ge(ab_ready, 1)
                            ac(s, s.activation(t2[:, :, :], t2[:, :, :], ACT.Exp, scale=-1.0))
                            ac(s, s.activation(t2[:, :, :], t2[:, :, :], ACT.Ln, bias=C("ones")[:, 0:1]))
                            s.sem_inc(ln_ready, 1)
                            s.wait_ge(ex_in, 1)
                            s.activation(t1[:, :, :], t3[:, :, :], ACT.Exp, scale=1.0 / 16).then_inc(ex_out, 1)
                            ac(s, s.activation(t3[:, :, :], t3[:, :, :], ACT.Exp, scale=-1.0 / 16))
                            s.sem_inc(ex_out, 1)
                            s.activation(t4[:, :, :], t4[:, :, :], ACT.Exp, scale=1.0 / 16).then_inc(ex_out, 1)
                            s.activation(t2[:, :, :], t2[:, :, :], ACT.Exp, scale=1.0 / 16).then_inc(ex_out, 1)
                            for i, (lo, r) in enumerate(TILES):
                                s.wait_ge(row_full, i + 1)
                                s.activation(rowE[0:r, i, :], ps[6 + i % 2][0:r, :], ACT.Copy).then_inc(row_free, 1)
                            ac(s, s.activation(gS[:, :, :], gS[:, :, :], ACT.Silu))

                        @block.tensor
                        def _(t):
                            t.wait_ge(ga_in, 16)
                            for c in range(GH):
                                mm = t.matmul(ps[c][:, 0:TOK], ga2[:, c * P:(c + 1) * P], xaT[:, :], start=True, stop=True)
                            mm.then_inc(z_full, 1)
                            t.wait_ge(mm_ready, 1)
                            for i, (lo, r) in enumerate(TILES):
                                if i >= 2:
                                    t.wait_ge(at_free, i - 1)
                                for h in range(GH):
                                    mm = t.matmul(ps[4 + i % 2][0:r, h * P:h * P + r], t3[:, h, lo:lo + r], t1[:, h, lo:lo + r], start=True, stop=True)
                                mm.then_inc(at_full, 1)
                            t.wait_ge(mm_ready, 2)
                            for i, (lo, r) in enumerate(TILES):
                                if i >= 2:
                                    t.wait_ge(row_free, i - 1)
                                for h in range(GH):
                                    mm = t.transpose(ps[6 + i % 2][0:r, h * P:(h + 1) * P], t4[:, h, lo:lo + r], C("ident"))
                                mm.then_inc(row_full, 1)
                            t.wait_ge(at_free, 3)
                            for n in range(DC):
                                if n >= 4:
                                    t.wait_ge(o_free, n - 3)
                                for i, (lo, r) in enumerate(TILES):
                                    mm = t.matmul(ps[n % 4][:, lo:lo + r], rowV[0:r, i, n * P:(n + 1) * P], AT[0:r, i, n // 2, 0:r], start=True, stop=True)
                                mm.then_inc(o_full, 1)

                S = sbuf(st, "S", [P, 2, GH, DV])
                vb = sbuf(st, "vb", [64, 2, 2, 512])
                in_full, in_free, up_full, up_ready, so_full, vb_ready, sn_full, sn_ready, s0_ready, so_taken = (sem(x) for x in (
                    "inter_full", "inter_free", "update_full", "update_ready", "sample_inter", "vblk_ready", "snew_full", "snew_ready", "gs0", "sample_taken"))
                NG = SEQ // GC
                with nc.Block() as block:
                    @block.tensor
                    def _(t):
                        t.wait_ge(s0_ready, 1)
                        for c in range(NG):
                            i, js = c // 4, slice(GC * (c % 4), GC * (c % 4) + GC)
                            if c:
                                t.wait_ge(up_ready, c)
                            for h in range(GH):
                                mm = t.matmul(ps[h // 2][:, (h % 2) * DV:(h % 2 + 1) * DV], rowE[js, i, h * DK:(h + 1) * DK],
                                              rowV[js, i, h * DV:(h + 1) * DV], start=True, stop=True, tile_position=(GC * (c % 4), 0))
                            mm.then_inc(up_full, 1)
                            if c >= 2:
                                t.wait_ge(in_free, c - 1)
                            for n in range(DC):
                                mm = t.matmul(ps[2 + c % 2][:, n * GC:(n + 1) * GC], S[:, c % 2, n // 2, (n % 2) * P:(n % 2 + 1) * P],
                                              qb[:, n // 2, c * GC:(c + 1) * GC], start=True, stop=True)
                            mm.then_inc(in_full, 1)
                        t.wait_ge(ss_in.sem, 16 * NB)
                        for n in range(DC):
                            for b in range(NB):
                                mm = t.matmul(ps[4][:, n * 64 + b * DS:n * 64 + (b + 1) * DS], Ss[:, b, n // 2, (n % 2) * P:(n % 2 + 1) * P],
                                              qb[:, n // 2, SEQ + b * DS:SEQ + (b + 1) * DS], start=True, stop=True)
                        mm.then_inc(so_full, 1)
                        t.wait_ge(so_taken, 1)
                        for n in range(16):
                            t.wait_ge(vb_ready, n + 1)
                            if n >= 2:
                                t.wait_ge(sn_ready, n - 1)
                            t.matmul(ps[5 + n % 2][:, :], rowE[0:64, 2, (n // 4) * DK:(n // 4 + 1) * DK], vb[:, n % 2, 0, :], start=True, stop=True).then_inc(sn_full, 1)

                    @block.vector
                    def _(v):
                        dv(v, v.memset(S[:, 0, :, :], 0.0))
                        v.sem_inc(s0_ready, 1)
                        for c in range(NG):
                            v.wait_ge(up_full, c + 1)
                            if c:
                                v.wait_ge(in_full, c)
                            for h in range(GH):
                                last = v.scalar_tensor_tensor(out=S[:, (c + 1) % 2, h, :], in0=S[:, c % 2, h, :], scalar=bend[:, h, c:c + 1],
                                                              in1=ps[h // 2][:, (h % 2) * DV:(h % 2 + 1) * DV], op0=ALU.mult, op1=ALU.add)
                            dv(v, last)
                            v.sem_inc(up_ready, 1)
                            v.wait_ge(in_full, c + 1)
                            v.tensor_tensor(oT[:, :, c * GC:(c + 1) * GC], oT[:, :, c * GC:(c + 1) * GC],
                                            ps[2 + c % 2][:, 0:256].rearrange("p (n t) -> p n t", n=DC), ALU.add).then_inc(in_free, 1)
                        v.wait_ge(so_full, 1)
                        v.tensor_tensor(oT[:, :, SEQ:TOK], oT[:, :, SEQ:TOK], ps[4][:, :].rearrange("p (n t) -> p n t", n=DC), ALU.add).then_inc(so_taken, 1)
                        v.wait_ge(ss_in.sem, 16 * NB)
                        for n in range(16 + 1):
                            if n < 16:
                                h, b = n // 4, 2 * (n % 4)
                                if n >= 2:
                                    v.wait_ge(sn_full, n - 1)
                                for x in range(2):
                                    last = v.tensor_scalar(vb[:, n % 2, 0, x * DV:(x + 1) * DV], rowV[0:64, 2, h * DV:(h + 1) * DV],
                                                           C("bsel", 64, b + x, b + x + 1), None, ALU.mult)
                                last.then_inc(vb_ready, 1)
                            if n:
                                m = n - 1
                                h, b = m // 4, 2 * (m % 4)
                                v.wait_ge(sn_full, m + 1)
                                for x in range(2):
                                    last = v.scalar_tensor_tensor(out=Ss[:, b + x, h, :], in0=Ss[:, b + x, h, :], scalar=bends[:, h, b + x:b + x + 1],
                                                                  in1=ps[5 + m % 2][:, x * DV:(x + 1) * DV], op0=ALU.mult, op1=ALU.add)
                                last.then_inc(sn_ready, 1)

                    @block.sync
                    def _(sp):
                        sp.wait_ge(up_ready, NG)
                        store(sp, O["new_gla_prompt"][0, 0].rearrange("h k v -> k h v"), S[:, NG % 2, :, :])
                        sp.wait_ge(sn_ready, 16)
                        for b in range(NB):
                            store(sp, O["new_gla_sample"][0, b].rearrange("h k v -> k h v"), Ss[:, b, :, :])
                        sp.wait_ge(stored.sem, stored.n)

            with ExitStack() as st:
                sq = sbuf(st, "osq", [P, DC, TOK])
                rs = sbuf(st, "ors", [P, GH, TOK])
                q_ready, f, v_ready, w_ready = (sem(x) for x in ("osq_ready", "osum_full", "ovar_ready", "orstd_ready"))
                with nc.Block() as block:
                    @block.vector
                    def _(v):
                        dv(v, v.tensor_tensor(sq[:, :, :], mixT[:, :, :], mixT[:, :, :], ALU.mult))
                        v.sem_inc(q_ready, 1)
                        for h in range(GH):
                            v.wait_ge(f, h + 1)
                            v.tensor_scalar(rs[:, h, :], ps[h][:, 0:TOK], 1.0 / DV, EPS, ALU.mult, ALU.add).then_inc(v_ready, 1)
                        for n in range(DC):
                            if n % 2 == 0:
                                v.wait_ge(w_ready, n // 2 + 1)
                                dv(v, v.reciprocal(rs[:, n // 2, :], rs[:, n // 2, :]))
                            dv(v, v.scalar_tensor_tensor(out=mixT[:, n, :], in0=mixT[:, n, :], scalar=V("gla_norm", n), in1=rs[:, n // 2, :], op0=ALU.mult, op1=ALU.mult))
                            dv(v, v.tensor_tensor(mixT[:, n, :], mixT[:, n, :], gS[:, n, :], ALU.mult))

                    @block.tensor
                    def _(t):
                        t.wait_ge(q_ready, 1)
                        for h in range(GH):
                            for q in range(2):
                                mm = t.matmul(ps[h][:, 0:TOK], C("ones"), sq[:, 2 * h + q, :], start=(q == 0), stop=(q == 1))
                            mm.then_inc(f, 1)

                    @block.scalar
                    def _(s):
                        for h in range(GH):
                            s.wait_ge(v_ready, h + 1)
                            s.activation(rs[:, h, :], rs[:, h, :], ACT.Sqrt).then_inc(w_ready, 1)

        next_part()
        out_projection("out_odd", A["w_out_odd"][0])

        with ExitStack() as mo:
            rowH = sbuf(mo, "rowH", [P, 3, D])
            slotno = sbuf(mo, "slotno", [P, 3, MAXJOB])
            gate = sbuf(mo, "gate", [P, 3, MAXJOB])
            jobs = sbuf(mo, "jobs", [1, MAXJOB], I32)
            njobs = sbuf(mo, "njobs", [1, 8], I32)
            with ExitStack() as st:
                sq = sbuf(st, "sq", [P, DC, TOK])
                wr = sbuf(st, "router", [P, DC, NE])
                lg = sbuf(st, "logits", [P, 3, NE])
                cmp = sbuf(st, "cmp", [P, NE, NE])
                eq = sbuf(st, "eq", [P, NE, NE])
                rank = sbuf(st, "rank", [P, 3, NE])
                mask = sbuf(st, "mask", [P, 3, NE])
                gt = sbuf(st, "gt", [P, 3, NE])
                top = sbuf(st, "top", [P, 3, 8])
                slot = sbuf(st, "slot", [P, 3, NE])
                cnt = sbuf(st, "cnt", [P, NE])
                over = sbuf(st, "over", [P, 16])
                order = sbuf(st, "order", [P, 16])
                OH = sbuf(st, "OH", [P, 8, 16])
                tmp = sbuf(st, "tmp", [P, 8, 16])
                s16 = sbuf(st, "s16", [P, 16])
                g16 = sbuf(st, "g16", [P, 16])
                red = sbuf(st, "red", [P, 8])
                hit = sbuf(st, "hit", [P, 8])
                wr_in = Signal(sem("router_in"))
                n_dve, n_pe, n_act = rms_steps("moen", xT[:, :, :], DC, V("norm_ffn_odd", 0, 8), hT, D, scratch=sq)
                h_ready, lg_full, ex_in, ex_out, mk_ready, sl_full, rh_full, rh_act, rh_dve = (sem(x) for x in (
                    "moe_h", "logits_full", "gate_exp_in", "gate_exp_out", "mask_ready", "slots_full", "rowh_full", "rowh_act", "rowh_dve"))
                with nc.Block() as block:
                    @block.sync
                    def _(sp):
                        load(sp, wr[:, :, :], A["moe_router"][0].rearrange("(c p) e -> p c e", p=P), wr_in)


                    @block.tensor
                    def _(t):
                        n_pe(t)
                        t.wait_ge(h_ready, 1)
                        t.wait_ge(wr_in.sem, 16)
                        for i, (lo, r) in enumerate(TILES):
                            for k in range(DC):
                                mm = t.matmul(ps[0][0:r, i * NE:(i + 1) * NE], hT[:, k, lo:lo + r], wr[:, k, :], start=(k == 0), stop=(k == DC - 1))
                        mm.then_inc(lg_full, 1)
                        for n in range(6):
                            lo, r = TILES[n // 2]
                            if n >= 4:
                                t.wait_ge(rh_act if n % 2 == 0 else rh_dve, (n - 4) // 2 + 1)
                            for q in range(4):
                                mm = t.transpose(ps[2 + n % 4][0:r, q * P:(q + 1) * P], hT[:, 4 * (n % 2) + q, lo:lo + r], C("ident"))
                            mm.then_inc(rh_full, 1)
                        t.wait_ge(mk_ready, 1)
                        for i, (lo, r) in enumerate(TILES):
                            for k in range(i + 1):
                                rk_ = TILES[k][1]
                                lhs = C("before", r, 0, r) if k == i else C("ones", rk_, 0, r)
                                t.matmul(ps[1][0:r, i * NE:(i + 1) * NE], lhs, mask[0:rk_, k, :], start=(k == 0), stop=(k == i))
                        for k in range(3):
                            rk_ = TILES[k][1]
                            mm = t.matmul(ps[1][:, 3 * NE:4 * NE], C("ones", rk_), mask[0:rk_, k, :], start=(k == 0), stop=(k == 2))
                        mm.then_inc(sl_full, 1)

                    @block.scalar
                    def _(s):
                        n_act(s)
                        for n in range(0, 6, 2):
                            s.wait_ge(rh_full, n + 1)
                            r = TILES[n // 2][1]
                            s.activation(rowH[0:r, n // 2, 0:512], ps[2 + n % 4][0:r, :], ACT.Copy).then_inc(rh_act, 1)
                        s.wait_ge(ex_in, 1)
                        for i, (lo, r) in enumerate(TILES):
                            s.activation(gt[0:r, i, :], gt[0:r, i, :], ACT.Exp)
                            ins = s.activation(top[0:r, i, 1:2], top[0:r, i, 1:2], ACT.Exp)
                        ac(s, ins)
                        s.sem_inc(ex_out, 1)

                    @block.vector
                    def _(v):
                        n_dve(v)
                        v.sem_inc(h_ready, 1)
                        v.wait_ge(lg_full, 1)
                        for i, (lo, r) in enumerate(TILES):
                            last = v.tensor_copy(lg[0:r, i, :], ps[0][0:r, i * NE:(i + 1) * NE])
                        dv(v, last)
                        for i, (lo, r) in enumerate(TILES):
                            L = lg[0:r, i, :]
                            le = L.rearrange("p (e o) -> p e o", o=1).to_broadcast([r, NE, NE])
                            lo_ = L.rearrange("p (o f) -> p o f", o=1).to_broadcast([r, NE, NE])
                            v.max(top[0:r, i, :], L)
                            v.tensor_tensor(cmp[0:r, :, :], lo_, le, ALU.is_gt)
                            dv(v, v.tensor_tensor(eq[0:r, :, :], lo_, le, ALU.is_equal))
                            dv(v, v.tensor_tensor(eq[0:r, :, :], eq[0:r, :, :], C("tie", r).rearrange("p (e f) -> p e f", e=NE), ALU.mult))
                            dv(v, v.tensor_tensor(cmp[0:r, :, :], cmp[0:r, :, :], eq[0:r, :, :], ALU.add))
                            dv(v, v.tensor_reduce(rank[0:r, i, :], cmp[0:r, :, :], AX_X, ALU.add))
                            v.tensor_scalar(mask[0:r, i, :], rank[0:r, i, :], 1.5, None, ALU.is_lt)
                            v.tensor_scalar(gt[0:r, i, :], L, top[0:r, i, 0:1], None, ALU.subtract)
                            dv(v, v.tensor_scalar(top[0:r, i, 1:2], top[0:r, i, 1:2], top[0:r, i, 0:1], None, ALU.subtract))
                        v.sem_inc(mk_ready, 1)
                        v.sem_inc(ex_in, 1)
                        for n in range(1, 6, 2):
                            v.wait_ge(rh_full, n + 1)
                            r = TILES[n // 2][1]
                            v.tensor_copy(rowH[0:r, n // 2, 512:1024], ps[2 + n % 4][0:r, :]).then_inc(rh_dve, 1)
                        v.wait_ge(ex_out, 1)
                        for i, (lo, r) in enumerate(TILES):
                            dv(v, v.tensor_scalar(top[0:r, i, 1:2], top[0:r, i, 1:2], 1.0, None, ALU.add))
                            dv(v, v.reciprocal(top[0:r, i, 2:3], top[0:r, i, 1:2]))
                            dv(v, v.scalar_tensor_tensor(out=gt[0:r, i, :], in0=gt[0:r, i, :], scalar=top[0:r, i, 2:3], in1=mask[0:r, i, :], op0=ALU.mult, op1=ALU.mult))
                        v.wait_ge(sl_full, 1)
                        dv(v, v.tensor_copy(cnt[:, :], ps[1][:, 3 * NE:4 * NE]))
                        for i, (lo, r) in enumerate(TILES):
                            dv(v, v.tensor_scalar(slot[0:r, i, :], ps[1][0:r, i * NE:(i + 1) * NE], FAR, None, ALU.subtract))
                            dv(v, v.tensor_tensor(slot[0:r, i, :], slot[0:r, i, :], mask[0:r, i, :], ALU.mult))
                            dv(v, v.tensor_scalar(slot[0:r, i, :], slot[0:r, i, :], FAR, None, ALU.add))
                        for q in range(2):
                            last = v.tensor_tensor(over[:, q * NE:(q + 1) * NE], cnt[:, :], C("part")[:, q * NE:(q + 1) * NE], ALU.is_gt)
                        dv(v, last)
                        dv(v, v.tensor_tensor_scan(order[:, :], C("ones", P, 0, 16), over[:, :], 0.0, ALU.mult, ALU.add))
                        dv(v, v.tensor_scalar(njobs[0:1, 0:1], order[0:1, 15:16], float(NE), None, ALU.add))
                        dv(v, v.tensor_tensor(order[:, :], order[:, :], over[:, :], ALU.mult))
                        dv(v, v.tensor_scalar(order[:, :], order[:, :], 1.0, None, ALU.subtract))
                        dv(v, v.tensor_tensor(OH[:, :, :], order[:, :].rearrange("p (o c) -> p o c", o=1).to_broadcast([P, 8, 16]),
                                              C("jobno").rearrange("p (j c) -> p j c", j=8), ALU.is_equal))
                        dv(v, v.tensor_tensor(tmp[:, :, :], OH[:, :, :], C("expert").rearrange("p (o c) -> p o c", o=1).to_broadcast([P, 8, 16]), ALU.mult))
                        dv(v, v.tensor_reduce(red[:, :], tmp[:, :, :], AX_X, ALU.add))
                        v.tensor_copy(jobs[0:1, 8:16], red[0:1, :])
                        v.tensor_copy(jobs[0:1, 0:8], C("expert", 1, 0, 8))
                        dv(v, v.tensor_reduce(hit[:, :], OH[:, :, :], AX_X, ALU.add))
                        for i, (lo, r) in enumerate(TILES):
                            v.tensor_copy(slotno[0:r, i, 0:NE], slot[0:r, i, :])
                            v.tensor_copy(gate[0:r, i, 0:NE], gt[0:r, i, :])
                            for q in range(2):
                                v.tensor_tensor(s16[0:r, q * NE:(q + 1) * NE], slot[0:r, i, :], C("part", r)[:, q * NE:(q + 1) * NE], ALU.subtract)
                                last = v.tensor_copy(g16[0:r, q * NE:(q + 1) * NE], gt[0:r, i, :])
                            dv(v, last)
                            dv(v, v.tensor_scalar(s16[0:r, :], s16[0:r, :], FAR, None, ALU.subtract))
                            dv(v, v.tensor_tensor(tmp[0:r, :, :], OH[0:r, :, :], s16[0:r, :].rearrange("p (o c) -> p o c", o=1).to_broadcast([r, 8, 16]), ALU.mult))
                            dv(v, v.tensor_reduce(red[0:r, :], tmp[0:r, :, :], AX_X, ALU.add))
                            dv(v, v.tensor_scalar(slotno[0:r, i, NE:16], red[0:r, :], FAR, None, ALU.add))
                            dv(v, v.tensor_tensor(tmp[0:r, :, :], OH[0:r, :, :], g16[0:r, :].rearrange("p (o c) -> p o c", o=1).to_broadcast([r, 8, 16]), ALU.mult))
                            dv(v, v.tensor_reduce(gate[0:r, i, NE:16], tmp[0:r, :, :], AX_X, ALU.add))

            with ExitStack() as st:
                HALF = 2048
                NSM = 6
                NSP = 3
                KG = DC // 2
                GUP = DFE // 256
                FIRST_DN = 2 * GUP
                PIECES = FIRST_DN + DFE // 256
                assert PIECES % NSM == 0 and PIECES % NSP == 0
                TURN = PIECES // NSM
                FT = DFE // P
                GATHER = {FIRST_DN + 3: 0, FIRST_DN + 6: 1}
                ring = sbuf(st, "ring", [P, NSM, HALF])
                whi = sbuf(st, "w_hi", [P, NSP, HALF], F32R)
                wlo = sbuf(st, "w_lo", [P, NSP, HALF], F32R)
                sel = sbuf(st, "sel", [P, 3, P])
                selg = sbuf(st, "selg", [P, 3, P])
                selT = sbuf(st, "selT", [P, TOK])
                xhi = sbuf(st, "x_hi", [P, DC, P], F32R)
                xlo = sbuf(st, "x_lo", [P, DC, P], F32R)
                sil = sbuf(st, "sil", [P, 2, 256])
                hrow = sbuf(st, "hrow", [P, 2, 256])
                hhi = sbuf(st, "hid_hi", [P, FT, P], F32R)
                hlo = sbuf(st, "hid_lo", [P, FT, P], F32R)
                Y = sbuf(st, "Y", [P, D])
                YB = [2, 3, 6, 7]
                landed = [sem(f"landed{n}") for n in range(NSM)]
                split, used = sem("pieces_split"), sem("pieces_used")
                (hi_ready, sel_ready, selg_ready, xg_full, xhi_ready, xlo_ready, st_full, st_ready, sil_ready, h_ready, ht_full,
                 hhi_ready, hlo_ready, y_ready, yo_full, yo_added) = (sem(x) for x in (
                     "hi_ready", "sel_ready", "selg_ready", "gathered", "xhi_ready", "xlo_ready", "sel_turned", "selT_ready", "silu_ready",
                     "hidden_ready", "hidden_turned", "hid_hi_ready", "hid_lo_ready", "y_ready", "scattered", "y_added"))
                with nc.Block() as block:
                    @block.sync
                    def _(sp):
                        n = sp.value_load(njobs[0:1, 0:1], min_val=NE, max_val=NE + 4)

                        def load_pieces(gu, dn, first, count):
                            for i in range(count):
                                s_ = i % NSM
                                if i < FIRST_DN:
                                    g, half = divmod(i, 2)
                                    for a in range(2):
                                        sp.wait_ge(split, first + i)
                                        sp.dma_start(ring[:, s_, :].rearrange("p (c a n) -> p c a n", c=KG, a=2)[:, :, a, :],
                                                     gu[:, KG * half:KG * (half + 1), a, g * 256:(g + 1) * 256]).then_inc(landed[s_], 16)
                                else:
                                    q = i - FIRST_DN
                                    sp.wait_ge(split, first + i)
                                    sp.dma_start(ring[:, s_, :].rearrange("p (c n) -> p c n", c=2), dn[:, 2 * q:2 * q + 2, :]).then_inc(landed[s_], 32)
                        with sp.Fori(0, n) as j:
                            e = sp.value_load(jobs[0:1, bass.ds(j, 1)], min_val=0, max_val=NE - 1)
                            gu = A["moe_w_gu"][0, bass.ds(e, 1)].rearrange("e (c p) (a n) -> p (e c) a n", p=P, a=2)
                            dn = A["moe_w_down"][0, bass.ds(e, 1)].rearrange("e (c p) n -> p (e c) n", p=P)
                            load_pieces(gu, dn, sp.snap(PIECES * j + 1), PIECES)
                        gu = A["moe_w_gu"][0, 0].rearrange("(c p) (a n) -> p c a n", p=P, a=2)
                        load_pieces(gu, None, sp.snap(PIECES * n + 1), NSP)

                    @block.tensor
                    def _(t):
                        n = t.value_load(njobs[0:1, 0:1], min_val=NE, max_val=NE + 4)
                        for _ in range(NSP):
                            t.sem_inc(used, 1)

                        def gather(half):
                            for c in range(4 * half, 4 * half + 4):
                                for i, (lo, r) in enumerate(TILES):
                                    mm = t.matmul(ps[6 + half][:, (c % 4) * P:(c % 4 + 1) * P], rowH[0:r, i, c * P:(c + 1) * P], sel[0:r, i, :],
                                                  start=(i == 0), stop=(i == 2))
                            mm.then_inc(xg_full, 1)

                        def product(out, a_hi, a_lo, w_hi, w_lo, start, stop):
                            t.matmul(out, a_hi, w_hi, start=start, stop=False)
                            t.matmul(out, a_hi, w_lo, start=False, stop=False)
                            return t.matmul(out, a_lo, w_hi, start=False, stop=stop)
                        t.wait_ge(sel_ready, 1)
                        gather(0)
                        gather(1)
                        with t.Fori(0, n) as j:
                            def turned(p):
                                if p == 0:
                                    t.wait_ge(yo_added, DC * j + 1)
                                t.wait_ge(h_ready, GUP * j + (p + 1))
                                if p >= 2:
                                    t.wait_ge(hlo_ready, GUP * j + (p - 1))
                                for q in range(2):
                                    mm = t.transpose(ps[2 + p % 2][:, q * P:(q + 1) * P], hrow[:, p % 2, q * P:(q + 1) * P], C("ident"))
                                mm.then_inc(ht_full, 1)
                            t.wait_ge(xlo_ready, 2 * j + 2)
                            for i in range(FIRST_DN):
                                g, half = divmod(i, 2)
                                s_ = i % NSP
                                t.wait_ge(split, PIECES * j + (NSM + i + 1))
                                if half == 0 and g >= 2:
                                    t.wait_ge(h_ready, GUP * j + (g - 1))
                                for q in range(KG):
                                    k = KG * half + q
                                    mm = product(ps[g % 2][:, :], xhi[:, k, :], xlo[:, k, :], whi[:, s_, q * 512:(q + 1) * 512],
                                                 wlo[:, s_, q * 512:(q + 1) * 512], k == 0, k == DC - 1)
                                mm.then_inc(used, 1)
                                if i == 9:
                                    t.wait_ge(selg_ready, j + 1)
                                    for tile, (lo, r) in enumerate(TILES):
                                        mm = t.transpose(ps[4][:, lo:lo + r], selg[0:r, tile, :], C("ident", r, 0, r))
                                    mm.then_inc(st_full, 1)
                                if half == 1 and g >= 1:
                                    turned(g - 1)
                            t.wait_ge(st_ready, j + 1)
                            for i in range(FIRST_DN, PIECES):
                                s_ = i % NSP
                                t.wait_ge(split, PIECES * j + (NSM + i + 1))
                                t.wait_ge(hlo_ready, GUP * j + (i - FIRST_DN + 1))
                                for q in range(2):
                                    k = 2 * (i - FIRST_DN) + q
                                    for m in range(2):
                                        cols = slice(q * D + m * 512, q * D + (m + 1) * 512)
                                        mm = product(ps[4 + m][:, :], hhi[:, k, :], hlo[:, k, :], whi[:, s_, cols], wlo[:, s_, cols], k == 0, k == FT - 1)
                                mm.then_inc(used, 1)
                                if i == FIRST_DN:
                                    turned(GUP - 1)
                                if i in GATHER:
                                    t.wait_ge(sel_ready, j + 2)
                                    gather(GATHER[i])
                            t.wait_ge(y_ready, 2 * j + 2)
                            t.wait_ge(xlo_ready, 2 * j + 4)
                            for c in range(DC):
                                if c >= 4:
                                    t.wait_ge(yo_added, DC * j + (c - 2))
                                t.matmul(ps[YB[c % 4]][:, 0:TOK], Y[:, c * P:(c + 1) * P], selT[:, :], start=True, stop=True).then_inc(yo_full, 1)

                    @block.scalar
                    def _(s):
                        n = s.value_load(njobs[0:1, 0:1], min_val=NE, max_val=NE + 4)

                        def split_hi(j, i):
                            s.wait_ge(used, PIECES * j + (i + 1))
                            s.wait_ge(landed[i % NSM], 32 * TURN * j + 32 * (i // NSM + 1))
                            s.activation(whi[:, i % NSP, :], ring[:, i % NSM, :], ACT.Copy).then_inc(hi_ready, 1)
                        for i in range(NSP):
                            split_hi(0, i)
                        with s.Fori(0, n) as j:
                            def turned_hi(g):
                                s.wait_ge(ht_full, GUP * j + (g + 1))
                                s.activation(hhi[:, 2 * g:2 * g + 2, :], ps[2 + g % 2][:, 0:256].rearrange("p (q t) -> p q t", q=2),
                                             ACT.Copy).then_inc(hhi_ready, 1)
                            for i in range(NSP, PIECES):
                                g = i // 2 - 2
                                if i % 2 == 0 and 0 <= g < GUP:
                                    s.wait_ge(used, PIECES * j + (i + 1))
                                    if g >= 2:
                                        s.wait_ge(h_ready, GUP * j + (g - 1))
                                    s.activation(sil[:, g % 2, :], ps[g % 2][:, 0:256], ACT.Silu).then_inc(sil_ready, 1)
                                    if g >= 1:
                                        turned_hi(g - 1)
                                if i == FIRST_DN + 5:
                                    turned_hi(GUP - 1)
                                split_hi(j, i)
                            for i in range(NSP):
                                if i == NSP - 1:
                                    s.wait_ge(used, PIECES * j + (PIECES + NSP))
                                    s.activation(Y[:, 0:512], ps[4][:, :], ACT.Copy).then_inc(y_ready, 1)
                                split_hi(j + 1, i)

                    @block.vector
                    def _(v):
                        n = v.value_load(njobs[0:1, 0:1], min_val=NE, max_val=NE + 4)
                        for _ in range(NSM):
                            v.sem_inc(split, 1)
                        v.sem_inc(yo_added, 1)

                        def select(dst, col, second):
                            for i, (lo, r) in enumerate(TILES):
                                last = v.tensor_scalar(dst[0:r, i, :], C("slots", r), slotno[0:r, i, col], second(i, r), ALU.is_equal, ALU.mult)
                            return last

                        def gather_out(half, value):
                            v.wait_ge(xg_full, value)
                            src = ps[6 + half][:, :].rearrange("p (q t) -> p q t", q=4)
                            part = slice(4 * half, 4 * half + 4)
                            v.tensor_copy(xhi[:, part, :], src).then_inc(xhi_ready, 1)
                            v.wait_ge(xhi_ready, value)
                            v.tensor_tensor(xlo[:, part, :], src, xhi[:, part, :].bitcast(F32), ALU.subtract).then_inc(xlo_ready, 1)
                        select(sel, slice(0, 1), lambda i, r: 1.0).then_inc(sel_ready, 1)
                        gather_out(0, 1)
                        gather_out(1, 2)

                        def split_lo(j, i):
                            v.wait_ge(hi_ready, PIECES * j + (i + 1))
                            v.tensor_tensor(wlo[:, i % NSP, :], ring[:, i % NSM, :], whi[:, i % NSP, :].bitcast(F32), ALU.subtract).then_inc(split, 1)
                        for i in range(NSP):
                            split_lo(0, i)
                        with v.Fori(0, n) as j:
                            def turned_lo(g):
                                v.wait_ge(hhi_ready, GUP * j + (g + 1))
                                v.tensor_tensor(hlo[:, 2 * g:2 * g + 2, :], ps[2 + g % 2][:, 0:256].rearrange("p (q t) -> p q t", q=2),
                                                hhi[:, 2 * g:2 * g + 2, :].bitcast(F32), ALU.subtract).then_inc(hlo_ready, 1)
                            for i in range(NSP, PIECES):
                                g = i // 2 - 2
                                if i % 2 == 0 and 0 <= g < GUP:
                                    v.wait_ge(sil_ready, GUP * j + (g + 1))
                                    if g >= 2:
                                        v.wait_ge(ht_full, GUP * j + (g - 1))
                                    v.tensor_tensor(hrow[:, g % 2, :], sil[:, g % 2, :], ps[g % 2][:, 256:512], ALU.mult).then_inc(h_ready, 1)
                                    if g >= 1:
                                        turned_lo(g - 1)
                                if i == FIRST_DN + 5:
                                    turned_lo(GUP - 1)
                                split_lo(j, i)
                                if i == 5:
                                    select(selg, bass.ds(j, 1), lambda i, r: gate[0:r, i, bass.ds(j, 1)]).then_inc(selg_ready, 1)
                                if i == 7:
                                    select(sel, bass.ds(j + 1, 1), lambda i, r: 1.0).then_inc(sel_ready, 1)
                                if i == 14:
                                    v.wait_ge(st_full, j + 1)
                                    v.tensor_copy(selT[:, :], ps[4][:, 0:TOK]).then_inc(st_ready, 1)
                                if i - 4 in GATHER:
                                    gather_out(GATHER[i - 4], 2 * j + (3 + GATHER[i - 4]))
                            for i in range(NSP):
                                if i == NSP - 1:
                                    v.wait_ge(used, PIECES * j + (PIECES + NSP))
                                    v.tensor_copy(Y[:, 512:1024], ps[5][:, :]).then_inc(y_ready, 1)
                                split_lo(j + 1, i)
                            for c in range(DC):
                                v.wait_ge(yo_full, DC * j + (c + 1))
                                v.tensor_tensor(xT[:, c, :], xT[:, c, :], ps[YB[c % 4]][:, 0:TOK], ALU.add).then_inc(yo_added, 1)

        with ExitStack() as st:
            sq = sbuf(st, "sq", [P, DC, TOK])
            yrow = sbuf(st, "yrow", [P, 3, D])
            n_dve, n_pe, n_act = rms_steps("fin", xT[:, :, :], DC, V("final_norm", 0, 8), hT, D, scratch=sq)
            h_ready, full, f_act, f_dve = (sem(x) for x in ("fin_h", "yrow_full", "yrow_act", "yrow_dve"))
            with nc.Block() as block:

                @block.tensor
                def _(t):
                    n_pe(t)
                    t.wait_ge(h_ready, 1)
                    for n in range(6):
                        lo, r = TILES[n // 2]
                        if n >= 4:
                            t.wait_ge(f_act if n % 2 == 0 else f_dve, 1)
                        for q in range(4):
                            mm = t.transpose(ps[n % 4][0:r, q * P:(q + 1) * P], hT[:, 4 * (n % 2) + q, lo:lo + r], C("ident"))
                        mm.then_inc(full, 1)

                @block.scalar
                def _(s):
                    n_act(s)
                    for n in range(0, 6, 2):
                        s.wait_ge(full, n + 1)
                        r = TILES[n // 2][1]
                        s.activation(yrow[0:r, n // 2, 0:512], ps[n % 4][0:r, :], ACT.Copy).then_inc(f_act, 1)

                @block.vector
                def _(v):
                    n_dve(v)
                    v.sem_inc(h_ready, 1)
                    for n in range(1, 6, 2):
                        v.wait_ge(full, n + 1)
                        r = TILES[n // 2][1]
                        v.tensor_copy(yrow[0:r, n // 2, 512:1024], ps[n % 4][0:r, :]).then_inc(f_dve, 1)

                @block.sync
                def _(sp):
                    for i, (lo, r) in enumerate(TILES):
                        sp.wait_ge(f_act, i + 1)
                        sp.wait_ge(f_dve, i + 1)
                        dst = (O["y_prompt"][0, lo:lo + r, :] if i < 2 else O["y_sample"].rearrange("b t d -> (b t) d"))
                        store(sp, dst, yrow[0:r, i, :])
                    sp.wait_ge(stored.sem, stored.n)


_OUTS = [("y_prompt", (1, SEQ, D)), ("y_sample", (NB, DS, D)), ("new_mla_prompt", (1, 1, SEQ, LAT)), ("new_mla_sample", (1, NB, DS, LAT)),
         ("new_rwkv_prompt", (1, 1, RH, RD, RD)), ("new_rwkv_sample", (1, NB, RH, RD, RD)), ("new_shift_prompt", (1, 1, RPROJ)),
         ("new_shift_sample", (1, NB, RPROJ)), ("new_gla_prompt", (1, 1, GH, DK, DV)), ("new_gla_sample", (1, NB, GH, DK, DV))]


def kernel(**inputs):
    import concourse.bacc as bacc
    from concourse.bass_utils import run_bass_kernel_spmd as run

    nc = bacc.Bacc("TRN2", target_bir_lowering=False, num_devices=1)
    arrays, A, O = {}, {}, {}
    for name, a in list(inputs.items()) + [("consts", constants()[1])]:
        a = np.ascontiguousarray(a)
        arrays[f"in_{name}"] = a
        A[name] = nc.dram_tensor(f"in_{name}", a.shape, mybir.dt.from_np(a.dtype), kind="ExternalInput").ap()
    for name, shape in _OUTS:
        O[name] = nc.dram_tensor(f"out_{name}", shape, F32, kind="ExternalOutput").ap()
    model(nc, A, O)
    r = run(nc, [arrays], core_ids=[0])
    return tuple(r.results[0][f"out_{name}"] for name, _ in _OUTS)
```
